# Optimizing a Trainium2 kernel written in Bass

```python
import jax, jax.numpy as jnp
from jax import lax
import numpy as np

D_MODEL = 1024
BATCH = 1
SEQ = 512
DEPTH = 1
DEC_BATCH = 8
DEC_SEQ = 4
PAST_LEN = 4096
PAGE_SIZE = 128

C_CONV = D_MODEL
CONF_KERNEL = 31
EXPAND = 2
D_INNER = EXPAND * D_MODEL
HEADDIM = 64
N_HEADS_SSM = D_INNER // HEADDIM
N_GROUPS = 8
HEADS_PER_GROUP = N_HEADS_SSM // N_GROUPS
D_STATE = 128
SSM_CONV = 4
CONV_DIM = D_INNER + 2 * N_GROUPS * D_STATE
CHUNK = 128
D_FF = 4 * D_MODEL
EPS = 1e-6
OFF_CONF = 0
OFF_GATE = OFF_CONF + 2 * C_CONV
OFF_Z = OFF_GATE + 2 * D_MODEL
OFF_XBC = OFF_Z + D_INNER
OFF_DT = OFF_XBC + CONV_DIM
IN_COLS = OFF_DT + N_HEADS_SSM

kernel_name = "hybrid_conformer_ssd_decoder_step"

def rmsnorm(x, g):
    xf = x.astype(jnp.float32)
    y = xf * lax.rsqrt(jnp.mean(xf * xf, axis=-1, keepdims=True) + EPS)
    return (y * g.astype(jnp.float32)).astype(x.dtype)

def layernorm(x, g, b):
    xf = x.astype(jnp.float32)
    mu = jnp.mean(xf, axis=-1, keepdims=True)
    xc = xf - mu
    y = xc * lax.rsqrt(jnp.mean(xc * xc, axis=-1, keepdims=True) + EPS)
    return (y * g.astype(jnp.float32) + b.astype(jnp.float32)).astype(x.dtype)

def causal_dwconv(x, prefix, w, b):
    k = w.shape[0]
    xe = jnp.concatenate([prefix.astype(x.dtype), x], axis=1)
    y = lax.conv_general_dilated(
        xe, w[:, None, :].astype(x.dtype), window_strides=(1,), padding="VALID",
        dimension_numbers=("NWC", "WIO", "NWC"), feature_group_count=x.shape[-1])
    new_prefix = xe[:, xe.shape[1] - (k - 1):]
    return y + b.astype(x.dtype), new_prefix

def ssd_scan(x, dt, a_neg, bm, cm, h0):
    b, l = x.shape[0], x.shape[1]
    q = CHUNK if l % CHUNK == 0 else l
    nc = l // q
    f32 = jnp.float32
    G, E, P, N = N_GROUPS, HEADS_PER_GROUP, HEADDIM, D_STATE
    dtg = dt.astype(f32).reshape(b, nc, q, G, E)
    xdt = x.astype(f32).reshape(b, nc, q, G, E, P) * dtg[..., None]
    a = dtg * a_neg.astype(f32).reshape(G, E)
    bc = bm.astype(f32).reshape(b, nc, q, G, N)
    cc = cm.astype(f32).reshape(b, nc, q, G, N)
    xs = (jnp.moveaxis(xdt, 1, 0), jnp.moveaxis(a, 1, 0), jnp.moveaxis(bc, 1, 0), jnp.moveaxis(cc, 1, 0))
    causal = jnp.tril(jnp.ones((q, q), dtype=bool))[None, :, :, None, None]

    def step(h, inp):
        xdt_c, a_c, b_c, c_c = inp
        acum = jnp.cumsum(a_c, axis=1)
        seg = acum[:, :, None] - acum[:, None, :]
        decay = jnp.exp(jnp.where(causal, seg, -jnp.inf))
        scores = jnp.einsum('blgn,bsgn->blsg', c_c, b_c)
        y_diag = jnp.einsum('blsge,bsgep->blgep', scores[..., None] * decay, xdt_c)
        y_off = jnp.einsum('blgn,bgepn->blgep', c_c, h) * jnp.exp(acum)[..., None]
        a_last = acum[:, -1]
        w_s = jnp.exp(a_last[:, None] - acum)
        h_new = h * jnp.exp(a_last)[..., None, None] + jnp.einsum('bsgn,bsge,bsgep->bgepn', b_c, w_s, xdt_c)
        return h_new, y_diag + y_off

    h_init = h0.astype(f32).reshape(b, G, E, P, N)
    h_fin, ys = lax.scan(step, h_init, xs)
    y = jnp.moveaxis(ys, 0, 1).reshape(b, l, N_HEADS_SSM, P)
    return y.astype(x.dtype), h_fin.reshape(b, N_HEADS_SSM, P, N).astype(h0.dtype)

def hybrid_layer(x, conf_buf, ssm_buf, ssm_h, g_mix, w_in, conf_dw_w, conf_dw_b, conf_ln_g, conf_ln_b,
                 conf_w_pw, conf_b_pw, ssm_conv_w, ssm_conv_b, ssm_dt_bias, ssm_a_log, ssm_d,
                 ssm_norm_g, ssm_w_out, w_out, g_ffn, w_up, w_down):
    b, l, _ = x.shape
    u = rmsnorm(x, g_mix)
    proj = u @ w_in
    conf_in = proj[..., OFF_CONF:OFF_GATE]
    gates = proj[..., OFF_GATE:OFF_Z]
    z = proj[..., OFF_Z:OFF_XBC]
    xbc = proj[..., OFF_XBC:OFF_DT]
    dt_raw = proj[..., OFF_DT:IN_COLS]

    glu = conf_in[..., :C_CONV] * jax.nn.sigmoid(conf_in[..., C_CONV:])
    cconv, new_conf_buf = causal_dwconv(glu, conf_buf, conf_dw_w, conf_dw_b)
    cconv = jax.nn.silu(layernorm(cconv, conf_ln_g, conf_ln_b))
    branch_a = cconv @ conf_w_pw + conf_b_pw

    xbc_c, new_ssm_buf = causal_dwconv(xbc, ssm_buf, ssm_conv_w, ssm_conv_b)
    xbc_c = jax.nn.silu(xbc_c)
    xs = xbc_c[..., :D_INNER].reshape(b, l, N_HEADS_SSM, HEADDIM)
    bm = xbc_c[..., D_INNER:D_INNER + N_GROUPS * D_STATE].reshape(b, l, N_GROUPS, D_STATE)
    cm = xbc_c[..., D_INNER + N_GROUPS * D_STATE:].reshape(b, l, N_GROUPS, D_STATE)
    dt = jax.nn.softplus(dt_raw.astype(jnp.float32) + ssm_dt_bias.astype(jnp.float32))
    a_neg = -jnp.exp(ssm_a_log.astype(jnp.float32))
    y, new_h = ssd_scan(xs, dt, a_neg, bm, cm, ssm_h)
    y = y + xs * ssm_d[:, None].astype(xs.dtype)
    y = y.reshape(b, l, D_INNER) * jax.nn.silu(z)
    y = rmsnorm(y.reshape(b, l, N_GROUPS, D_INNER // N_GROUPS),
                ssm_norm_g.reshape(N_GROUPS, D_INNER // N_GROUPS)).reshape(b, l, D_INNER)
    branch_b = y @ ssm_w_out

    merged = jax.nn.sigmoid(gates[..., :D_MODEL]) * branch_a + jax.nn.sigmoid(gates[..., D_MODEL:]) * branch_b
    h = x + merged @ w_out
    hidden = jnp.square(jax.nn.relu(rmsnorm(h, g_ffn) @ w_up))
    h = h + hidden @ w_down
    return h, new_conf_buf, new_ssm_buf, new_h

def setup_inputs(seed: int = 0) -> dict:
    key = jax.random.key(seed)
    ks = jax.random.split(key, 32)
    f32 = jnp.float32

    def nrm(k, shape, scale):
        return jax.random.normal(k, shape, f32) * scale

    def gain(k, shape):
        return 1.0 + 0.05 * jax.random.normal(k, shape, f32)

    dt0 = jnp.exp(jax.random.uniform(ks[15], (DEPTH, N_HEADS_SSM), f32, np.log(1e-3), np.log(1e-1)))
    dt_bias = dt0 + jnp.log(-jnp.expm1(-dt0))
    return {
        "x_prompt": nrm(ks[0], (BATCH, SEQ, D_MODEL), 1.0),
        "x_sample": nrm(ks[1], (DEC_BATCH, DEC_SEQ, D_MODEL), 1.0),
        "state_conf_conv": nrm(ks[2], (DEPTH, DEC_BATCH, CONF_KERNEL - 1, C_CONV), 1.0),
        "state_ssm_conv": nrm(ks[3], (DEPTH, DEC_BATCH, SSM_CONV - 1, CONV_DIM), 1.0),
        "state_ssm": nrm(ks[4], (DEPTH, DEC_BATCH, N_HEADS_SSM, HEADDIM, D_STATE), 0.5),
        "g_mix": gain(ks[5], (DEPTH, D_MODEL)),
        "w_in": nrm(ks[6], (DEPTH, D_MODEL, IN_COLS), D_MODEL ** -0.5),
        "conf_dw_w": nrm(ks[7], (DEPTH, CONF_KERNEL, C_CONV), CONF_KERNEL ** -0.5),
        "conf_dw_b": nrm(ks[8], (DEPTH, C_CONV), 0.02),
        "conf_ln_g": gain(ks[9], (DEPTH, C_CONV)),
        "conf_ln_b": nrm(ks[10], (DEPTH, C_CONV), 0.02),
        "conf_w_pw": nrm(ks[11], (DEPTH, C_CONV, D_MODEL), C_CONV ** -0.5),
        "conf_b_pw": nrm(ks[12], (DEPTH, D_MODEL), 0.02),
        "ssm_conv_w": nrm(ks[13], (DEPTH, SSM_CONV, CONV_DIM), SSM_CONV ** -0.5),
        "ssm_conv_b": nrm(ks[14], (DEPTH, CONV_DIM), 0.02),
        "ssm_dt_bias": dt_bias,
        "ssm_a_log": jnp.log(jax.random.uniform(ks[16], (DEPTH, N_HEADS_SSM), f32, 1.0, 16.0)),
        "ssm_d": gain(ks[17], (DEPTH, N_HEADS_SSM)),
        "ssm_norm_g": gain(ks[18], (DEPTH, D_INNER)),
        "ssm_w_out": nrm(ks[19], (DEPTH, D_INNER, D_MODEL), D_INNER ** -0.5),
        "w_out": nrm(ks[20], (DEPTH, D_MODEL, D_MODEL), D_MODEL ** -0.5),
        "g_ffn": gain(ks[21], (DEPTH, D_MODEL)),
        "w_up": nrm(ks[22], (DEPTH, D_MODEL, D_FF), D_MODEL ** -0.5),
        "w_down": nrm(ks[23], (DEPTH, D_FF, D_MODEL), D_FF ** -0.5),
        "g_final": gain(ks[24], (D_MODEL,)),
    }

def reference(x_prompt, x_sample, state_conf_conv, state_ssm_conv, state_ssm, g_mix, w_in, conf_dw_w,
              conf_dw_b, conf_ln_g, conf_ln_b, conf_w_pw, conf_b_pw, ssm_conv_w, ssm_conv_b, ssm_dt_bias,
              ssm_a_log, ssm_d, ssm_norm_g, ssm_w_out, w_out, g_ffn, w_up, w_down, g_final):
    hp, hs = x_prompt, x_sample
    pc_list, ps_list, ph_list, sc_list, ss_list, sh_list = [], [], [], [], [], []
    for i in range(DEPTH):
        lw = (g_mix[i], w_in[i], conf_dw_w[i], conf_dw_b[i], conf_ln_g[i], conf_ln_b[i], conf_w_pw[i],
              conf_b_pw[i], ssm_conv_w[i], ssm_conv_b[i], ssm_dt_bias[i], ssm_a_log[i], ssm_d[i],
              ssm_norm_g[i], ssm_w_out[i], w_out[i], g_ffn[i], w_up[i], w_down[i])
        pc0 = jnp.zeros((BATCH, CONF_KERNEL - 1, C_CONV), x_prompt.dtype)
        ps0 = jnp.zeros((BATCH, SSM_CONV - 1, CONV_DIM), x_prompt.dtype)
        ph0 = jnp.zeros((BATCH, N_HEADS_SSM, HEADDIM, D_STATE), x_prompt.dtype)
        hp, pc, ps, ph = hybrid_layer(hp, pc0, ps0, ph0, *lw)
        hs, sc, ss, sh = hybrid_layer(hs, state_conf_conv[i], state_ssm_conv[i], state_ssm[i], *lw)
        pc_list.append(pc); ps_list.append(ps); ph_list.append(ph)
        sc_list.append(sc); ss_list.append(ss); sh_list.append(sh)
    y_prompt = rmsnorm(hp, g_final)
    y_sample = rmsnorm(hs, g_final)
    new_conf_conv_prompt = jnp.stack(pc_list)
    new_ssm_conv_prompt = jnp.stack(ps_list)
    new_ssm_prompt = jnp.stack(ph_list)
    new_conf_conv_sample = jnp.stack(sc_list)
    new_ssm_conv_sample = jnp.stack(ss_list)
    new_ssm_sample = jnp.stack(sh_list)
    return (y_prompt, y_sample, new_conf_conv_prompt, new_ssm_conv_prompt, new_ssm_prompt,
            new_conf_conv_sample, new_ssm_conv_sample, new_ssm_sample)


_drawn_inputs = setup_inputs


def setup_inputs(seed=0):
    import zlib

    import numpy as np

    out = dict(_drawn_inputs(seed))
    spreads = {}
    factors = {'conf_dw_b': 4.934,
     'conf_ln_g': 3.182,
     'conf_ln_b': 8.0,
     'conf_b_pw': 5.777,
     'ssm_d': 26.115,
     'ssm_norm_g': 3.207}
    for name, (base, spread) in spreads.items():
        noise = np.random.default_rng([zlib.crc32(name.encode()), seed]).standard_normal(out[name].shape)
        drawn = base * np.exp(spread * noise) if base else spread * noise
        out[name] = __import__('jax').numpy.asarray(drawn.astype(out[name].dtype))
    for name, factor in factors.items():
        out[name] = (out[name] * factor).astype(out[name].dtype)
    return out
```

```python
from contextlib import ExitStack

import numpy as np

import concourse.bass as bass
from concourse import mybir

F32 = mybir.dt.float32
F32R = mybir.dt.float32r
BF16 = mybir.dt.bfloat16
ALU = mybir.AluOpType
ACT = mybir.ActivationFunctionType
AX = mybir.AxisListType

P = 128
D_MODEL = 1024
KT = D_MODEL // P
SEQ, NSEQ, TDEC = 512, 8, 4
NDEC = NSEQ * TDEC
T = SEQ + NDEC
H2 = T // 2
GROUPS, HPG, HD, NST = 8, 4, 64, 128
HEADS = GROUPS * HPG
CK, SK = 31, 4
CPRE, SPRE = CK - 1, SK - 1
CHUNK = 128
NCH = SEQ // CHUNK
EPS = 1e-6
BW = 256
NBLOCKS = 88
BIG = -1.0e30
B_GROUP, B_HALF, B_PW, B_WOUT, B_FFN = 0, 32, 48, 52, 56
PARAMS = {}
_at = 0
for _name, _n in [("g_mix", 8), ("conf_w", 8 * CK), ("conf_b", 8), ("ln_g", 8), ("ln_b", 8), ("b_pw", 8),
                  ("ssm_w", 32 * SK), ("ssm_b", 32), ("d_skip", 16), ("norm_g", 16), ("g_ffn", 8),
                  ("g_final", 8)]:
    PARAMS[_name] = (_at, _n)
    _at += _n
NPAR = _at


class Steps:

    def __init__(self, eng, sem):
        self.eng, self.sem, self.base, self.n = eng, sem, 0, 0

    def did(self, ins):
        ins.then_inc(self.sem, 1)
        self.n += 1
        return self.n

    def need(self, step):
        self.eng.wait_ge(self.sem, self.base + step)

    def enter(self, i, per):
        self.outer, self.per = self.base + self.n, per
        self.base, self.n = self.outer + i * per, 0

    def leave(self, rounds):
        assert self.n == self.per, f"{self.sem}: the body makes {self.n} steps, {self.per} given"
        self.base, self.n = self.outer + rounds * self.per, 0


def hybrid_layer(nc, x_all, w_all, w_dt, par, dt_par, conf_state, conv_state, ssm_state,
                 y_out, conf_out, conv_out, hp_out, hs_out):
    ctx = ExitStack()
    with ctx:
        def sb(name, shape, dt=F32):
            return ctx.enter_context(nc.sbuf_tensor(name, shape, dt))

        def sem(name):
            return ctx.enter_context(nc.semaphore(name))

        y_dram = nc.dram_tensor("y_scratch", (GROUPS, P, 2, SEQ), F32, kind="Internal").ap()
        cc_dram = nc.dram_tensor("cc_scratch", (GROUPS, P, T), F32, kind="Internal").ap()
        gate_dram = nc.dram_tensor("gate_scratch", (GROUPS, P, 2, T), F32, kind="Internal").ap()

        w_raw = sb("w_raw", [P, 2, KT * BW])
        w_hi = sb("w_hi", [P, 2, KT * BW], F32R)
        w_lo = sb("w_lo", [P, 2, KT * BW], F32R)
        ra_hi = sb("ra_hi", [P, KT, T], F32R)
        ra_lo = sb("ra_lo", [P, KT, T], F32R)
        rb_hi = sb("rb_hi", [P, KT, T], F32R)
        rb_lo = sb("rb_lo", [P, KT, T], F32R)
        ident = sb("ident", [P, P])
        ones = sb("ones", [P, P])
        ident_bf = sb("ident_bf", [P, P], BF16)
        mask_bf = sb("mask_bf", [P, P], BF16)
        mask_dec = sb("mask_dec", [NDEC, NDEC], BF16)
        seq_mask = sb("seq_mask", [NDEC, NSEQ])
        sel = sb("sel", [96, HEADS, HD], BF16)
        last_sel = sb("last_sel", [NDEC, NDEC])
        acum_bf = sb("acum_bf", [96, T], BF16)
        dt_nat = sb("dt_nat", [P, NCH + 1, HEADS])
        acum_nat = sb("acum_nat", [P, NCH + 1, HEADS])
        nacum_nat = sb("nacum_nat", [P, NCH + 1, HEADS])
        w_nat = sb("w_nat", [P, NCH + 1, HEADS])
        exp_last = sb("exp_last", [P, NCH + NSEQ, HEADS])
        pars = sb("pars", [P, NPAR])
        dt_pars = sb("dt_pars", [P, 2])
        a_neg = sb("a_neg", [P, 1])
        eps = sb("eps", [P, 1])
        cc_sum = sb("cc_sum", [P, T])
        dec_xbc = sb("dec_xbc", [P, GROUPS, 4, NDEC])
        dec_z = sb("dec_z", [P, GROUPS, 2, NDEC])
        ARENA = 17120
        arena = sb("arena", [P, ARENA])

        def views(*fields, at=0):
            out = []
            for shape in fields:
                n = int(np.prod(shape))
                v = arena[:, at:at + n]
                if len(shape) == 2:
                    v = v.rearrange("p (a b) -> p a b", b=shape[1])
                elif len(shape) == 3:
                    v = v.rearrange("p (a b c) -> p a b c", b=shape[1], c=shape[2])
                out.append(v)
                at += n
            assert at <= ARENA, at
            return out, at

        (raw, raw_d, acc, sil, zs, zh, gx, gd, conv_a, conv_b, ccs, cstate, cout, sstate, sout), ssd_at = views(
            (4, SPRE + SEQ), (4, NSEQ, SPRE + TDEC), (4, T), (4, T), (2, T), (2, T), (CPRE + SEQ,),
            (NSEQ, CPRE + TDEC), (SEQ,), (SEQ,), (T,), (NSEQ, CPRE), (CPRE * (NSEQ + 1),),
            (4, NSEQ, SPRE), (4, SPRE * (NSEQ + 1)))
        (h_t, xdt, wxdt, b_nat, scores, decay, m_t, y_tmp, e_acc, y_sb), _ = views(
            (HPG * HD,), (HPG * HD,), (HPG * HD,), (P,), (P,), (HPG, P), (HPG, P), (2, P), (2, SEQ), (2, SEQ),
            at=ssd_at)
        (x_t, sq0, rstd0, xn0), norm_end = views((KT, T), (2, T), (T,), (2, T))
        assert norm_end + 1024 <= ssd_at
        wdt_raw = arena[:, norm_end:norm_end + 1024]
        (dt_v, dt_e, dt_z, dt_z2, dt_p, dt_r, dt_t, scan_keep), _ = views(*[(T,)] * 8, at=ssd_at)
        (b_sum, st0, st1, y0, y1, gates_sb, d_sq, d_ssum, d_rstd, d_cur, d_xdt, d_wxdt, d_bn, d_bm, d_sc,
         d_decay, d_m, d_e, d_tmp), _ = views(
            (KT, T), (NSEQ, 256), (NSEQ, 256), (2, T), (2, T), (2, T), (2, T), (T,), (T,), (4, NDEC),
            (256,), (256,), (P,), (NSEQ, P), (NDEC,), (HPG, NDEC), (HPG, NDEC), (2, NDEC), (2, NDEC))
        st, y_cur = [st0, st1], [y0, y1]
        d_yn = d_sq
        (_, xc, l_sq, l_mean, l_ssum, l_rstd, l_a, l_th), _ = views(
            (KT, T), (KT, T), (2, T), (T,), (T,), (T,), (2, T), (2, T))
        (g_in, pw_a), _ = views((2, 2 * T), (2, T), at=2 * KT * T + 9 * T)
        pw_m = l_sq
        g_in = g_in.rearrange("p a (b t) -> p a b t", b=2)
        (h_sb, x_in, o_sq, o_ssum, o_rstd, f_r, f_v, f_s, o_y), _ = views(
            (KT, T), (2, T), (2, T), (T,), (T,), (2, T), (2, T), (2, T), (2, T))

        psum = [ctx.enter_context(nc.psum_tensor(f"main{s}", [P, 2, 512], F32)) for s in range(2)]
        pt = ctx.enter_context(nc.psum_tensor("pt", [P, 512], F32))
        ps = ctx.enter_context(nc.psum_tensor("ps", [P, 512], F32))
        py = ctx.enter_context(nc.psum_tensor("py", [P, 512], F32))
        ph = ctx.enter_context(nc.psum_tensor("ph", [P, 512], F32))

        def main(t):
            return psum[t % 2][:, :, 0:H2]

        def halves(ap):
            return ap.rearrange("p (a b) -> p a b", a=2)

        def par1(name, i, n=1):
            at, _ = PARAMS[name]
            return pars[:, bass.ds(at + i, n)]

        def fr(ap):
            return ap.bitcast(F32)

        w_in = [sem(f"w_in{s}") for s in range(2)]
        w_hi_s, w_lo_s, w_used = sem("w_hi_done"), sem("w_lo_done"), sem("w_used")
        tile_done = sem("tile_done")
        tile_free = [sem(f"tile_free{s}") for s in range(2)]
        const_s, pool_c = sem("const_s"), sem("pool_c")
        x_in_s = [sem(f"x_in_s{i}") for i in range(2)]
        par_s, wdt_in = sem("par_s"), sem("wdt_in")
        act_c, dve_c = sem("act_c"), sem("dve_c")
        n_sq, n_sum, n_rstd, n_xn, u_hi_s, u_ready = (sem(n) for n in (
            "n_sq", "n_sum", "n_rstd", "n_xn", "u_hi_s", "u_ready"))
        wdt_hi_s, wdt_ready, dt_psum, dt_act, dt_dve, acum_ready, nat_t, nat_copied, nat_b, nat_diff, nat_ready = (
            sem(n) for n in ("wdt_hi_s", "wdt_ready", "dt_psum", "dt_act", "dt_dve", "acum_ready", "nat_t",
                             "nat_copied", "nat_b", "nat_diff", "nat_ready"))
        raw_ready, conv4_s, sil_th, sil_ready, dec_saved = (sem(n) for n in (
            "raw_ready", "conv4_s", "sil_th", "sil_ready", "dec_saved"))
        z_act, z_ready, glu_act, glu_ready, cc_ready = (sem(n) for n in (
            "z_act", "z_ready", "glu_act", "glu_ready", "cc_ready"))
        e_psum, e_ready, pt_done, ps_done, decay_ready, m_ready, ys_done, h_ready, y_done = (sem(n) for n in (
            "e_psum", "e_ready", "pt_done", "ps_done", "decay_ready", "m_ready", "ys_done", "h_ready", "y_done"))
        cstate_in, sstate_in, sstate_used, cpre_ready, cc_added = (sem(n) for n in (
            "cstate_in", "sstate_in", "sstate_used", "cpre_ready", "cc_added"))
        cout_copied, sout_copied, cout_st, sout_st, ssd_st, cc_st = (sem(n) for n in (
            "cout_copied", "sout_copied", "cout_st", "sout_st", "ssd_st", "cc_st"))
        cc_free, ssd_free, gates_free, o_sum_s, par_ready = (sem(n) for n in (
            "cc_free", "ssd_free", "gates_free", "o_sum_s", "par_ready"))
        bs_ready = sem("bs_ready")
        f_sq_s, pool_passed = sem("f_sq_s"), sem("pool_passed")
        st_in = [sem(f"st_in{s}") for s in range(2)]
        y_in = [sem(f"y_in{s}") for s in range(2)]
        d_cur_s, d_off, d_pt, d_ps, d_bn_s, d_dec_s, d_m_s, d_y, d_add, d_r3, d_ycur, d_sq_s, d_ssum_s, d_stat, \
            d_rstd_s, d_yn_s, yn_hi_s, yn_ready, st_ready, st_st, gates_ev, gates_st = (sem(n) for n in (
                "d_cur_s", "d_off", "d_pt", "d_ps", "d_bn_s", "d_dec_s", "d_m_s", "d_y", "d_add", "d_r3",
                "d_ycur", "d_sq_s", "d_ssum_s", "d_stat", "d_rstd_s", "d_yn_s", "yn_hi_s", "yn_ready",
                "st_ready", "st_st", "gates_ev", "gates_st"))
        cc_in, l_stat, l_mean_s, l_xc, l_sq_s, l_ssum_s, l_stat2, l_rstd_s, l_t, l_th_s, l_sil, cc_hi_s, cc_ready2 = (
            sem(n) for n in ("cc_in", "l_stat", "l_mean_s", "l_xc", "l_sq_s", "l_ssum_s", "l_stat2", "l_rstd_s",
                             "l_t", "l_th_s", "l_sil", "cc_hi_s", "cc_split"))
        b_ready = sem("b_ready")
        g_in_s = [sem(f"g_in_s{s}") for s in range(2)]
        p_act, p_m, mg_hi, mg_ready = sem("p_act"), sem("p_m"), sem("mg_hi"), sem("mg_ready")
        x_in2 = [sem(f"x_in2_{s}") for s in range(2)]
        o_h, o_act, hn_ready, o_stat, o_rstd_s = sem("o_h"), sem("o_act"), sem("hn_ready"), sem("o_stat"), sem("o_rstd_s")
        f_act, f_v_s, f_hi, f_ready = sem("f_act"), sem("f_v_s"), sem("f_hi"), sem("f_ready")
        z_sq, z_stat, z_rstd, z_y = sem("z_sq"), sem("z_stat"), sem("z_rstd"), sem("z_y")
        out_st = [sem(f"out_st{s}") for s in range(2)]

        block = ctx.enter_context(nc.Block())

        @block.sync
        def _(sp):
            half = KT // 2
            for i in range(2):
                sp.dma_start(x_t[:, i * half:(i + 1) * half, :],
                             x_all[:, i * half * T:(i + 1) * half * T]
                             .rearrange("p (k t) -> p k t", t=T)).then_inc(x_in_s[i], 16)
                if i == 0:
                    sp.dma_start(pars[:, :], par).then_inc(par_s, 16)
                    sp.dma_start(dt_pars[:, :], dt_par).then_inc(par_s, 16)
            sp.dma_start(w_raw[:, 0, :], w_all[0]).then_inc(w_in[0], 16)
            sp.dma_start(wdt_raw, w_dt).then_inc(wdt_in, 16)
            sp.dma_start(w_raw[:, 1, :], w_all[1]).then_inc(w_in[1], 16)
            with sp.Fori(1, NBLOCKS // 2) as i:
                for s in range(2):
                    sp.wait_ge(w_lo_s, 2 * i + (s - 1))
                    sp.dma_start(w_raw[:, s, :], w_all[bass.ds(2 * i + s, 1), :, :]
                                 .rearrange("a p n -> p (a n)")).then_inc(w_in[s], 16)

        @block.gpsimd
        def _(pool):
            st_c = Steps(pool, pool_c)
            st_c.did(pool.memset(ident[:, :], 0.0))
            st_c.did(pool.memset(mask_bf[:, :], 0.0))
            st_c.did(pool.memset(mask_dec[:, :], 0.0))
            st_c.did(pool.memset(seq_mask[:, :], 1.0))
            pool.memset(ones[:, :], 1.0).then_inc(const_s, 1)
            pool.memset(eps[:, :], EPS).then_inc(const_s, 1)
            st_c.did(pool.memset(scan_keep, 1.0))
            st_c.need(5)
            n = st_c.did(pool.memset(scan_keep[:, 0:SEQ:CHUNK], 0.0))
            pool.memset(scan_keep[:, SEQ:T:TDEC], 0.0).then_inc(const_s, 1)
            n = st_c.did(pool.affine_select(out=ident[:, :], in_=ident[:, :], compare_op=ALU.not_equal, fill=1.0,
                                            base=0, pattern=[[-1, P]], channel_multiplier=1))
            st_c.did(pool.affine_select(out=mask_bf[:, :], in_=mask_bf[:, :], compare_op=ALU.is_ge, fill=BIG,
                                        base=0, pattern=[[1, P]], channel_multiplier=-1))
            st_c.need(n)
            m = st_c.did(pool.tensor_copy(ident_bf[:, :], ident[:, :]))
            dec3 = mask_dec[:, :].rearrange("s (b t) -> s b t", t=TDEC)
            m = st_c.did(pool.affine_select(out=mask_dec[:, :], in_=mask_dec[:, :], compare_op=ALU.is_ge, fill=BIG,
                                            base=0, pattern=[[1, NDEC]], channel_multiplier=-1))
            st_c.need(m)
            m = st_c.did(pool.affine_select(out=dec3, in_=dec3, compare_op=ALU.is_ge, fill=BIG, base=TDEC - 1,
                                            pattern=[[TDEC, NSEQ], [0, TDEC]], channel_multiplier=-1))
            st_c.need(m)
            st_c.did(pool.affine_select(out=dec3, in_=dec3, compare_op=ALU.is_ge, fill=BIG, base=0,
                                        pattern=[[-TDEC, NSEQ], [0, TDEC]], channel_multiplier=1))
            m = st_c.did(pool.affine_select(out=seq_mask[:, :], in_=seq_mask[:, :], compare_op=ALU.is_ge, fill=0.0,
                                            base=TDEC - 1, pattern=[[TDEC, NSEQ]], channel_multiplier=-1))
            st_c.need(m)
            st_c.did(pool.affine_select(out=seq_mask[:, :], in_=seq_mask[:, :], compare_op=ALU.is_ge, fill=0.0,
                                        base=0, pattern=[[-TDEC, NSEQ]], channel_multiplier=1))
            st_c.did(pool.tensor_copy(last_sel[:, :].rearrange("s (b t) -> s b t", t=TDEC),
                                      ident[0:NDEC, TDEC - 1:NDEC:TDEC].unsqueeze(2)
                                      .broadcast_to([NDEC, NSEQ, TDEC])))
            m = st_c.did(pool.memset(sel[:, :, :], 0.0))
            for part in range(3):
                st_c.need(m)
                m = st_c.did(pool.affine_select(out=sel[:, :, :], in_=sel[:, :, :], compare_op=ALU.not_equal,
                                                fill=1.0, base=-HEADS * part, pattern=[[-1, HEADS], [0, HD]],
                                                channel_multiplier=1))
            pool.memset(cc_sum[:, :], 0.0).then_inc(const_s, 1)
            pool.wait_ge(u_ready, KT)
            pool.memset(raw[:, :, 0:SPRE], 0.0).then_inc(const_s, 1)
            pool.memset(gx[:, 0:CPRE], 0.0).then_inc(const_s, 1)

            def held(s, value):
                pool.wait_ge(s, value)
                pool.sem_inc(pool_passed, 1)

            def load_conv_state(g):
                pool.dma_start(sstate.rearrange("p a b c -> p (a b c)"),
                               conv_state[bass.ds(g, 1), :, :].rearrange("a p n -> p (a n)"))\
                    .then_inc(sstate_in, 16)

            def load_conf_state(g):
                pool.dma_start(cstate.rearrange("p a b -> p (a b)"),
                               conf_state[bass.ds(g, 1), :, :].rearrange("a p n -> p (a n)"))\
                    .then_inc(cstate_in, 16)

            def conf_prefix(g):
                held(cstate_in, 16 * g + 16)
                pool.tensor_copy(gd[:, :, 0:CPRE], cstate).then_inc(cpre_ready, 1)

            def save_conv_state(g):
                held(raw_ready, 4 * g + 4)
                pool.tensor_copy(sout[:, :, 0:SPRE], raw[:, :, SEQ:SEQ + SPRE])
                pool.tensor_copy(sout[:, :, SPRE:].rearrange("p a (b c) -> p a b c", c=SPRE),
                                 raw_d[:, :, :, TDEC:TDEC + SPRE]).then_inc(sout_copied, 1)
                pool.wait_ge(sout_copied, g + 1)
                pool.dma_start(conv_out[bass.ds(g, 1), :, :].rearrange("a p n -> p (a n)"),
                               sout.rearrange("p a b -> p (a b)")).then_inc(sout_st, 16)

            def save_conf_state(g):
                held(glu_ready, g + 1)
                pool.tensor_copy(cout[:, 0:CPRE], gx[:, SEQ:SEQ + CPRE])
                pool.tensor_copy(cout[:, CPRE:].rearrange("p (b c) -> p b c", c=CPRE),
                                 gd[:, :, TDEC:TDEC + CPRE]).then_inc(cout_copied, 1)
                pool.wait_ge(cout_copied, g + 1)
                pool.dma_start(conf_out[bass.ds(g, 1), :, :].rearrange("a p n -> p (a n)"), cout)\
                    .then_inc(cout_st, 16)

            def add_cc(p):
                pool.wait_ge(cc_ready, p + 1)
                pool.dma_start(cc_dram[bass.ds(p, 1), :, :].rearrange("a p n -> p (a n)"), ccs).then_inc(cc_st, 16)
                pool.tensor_tensor(cc_sum[:, :], cc_sum[:, :], ccs, ALU.add).then_inc(cc_added, 1)
                pool.wait_ge(cc_added, p + 1)
                pool.wait_ge(cc_st, 16 * p + 16)
                pool.sem_inc(cc_free, 1)

            def store_ssd(p):
                pool.wait_ge(y_done, p + 1)
                pool.dma_start(y_dram[bass.ds(p, 1), :, :, :].rearrange("a p j n -> p (a j) n"), y_sb)\
                    .then_inc(ssd_st, 16)
                pool.dma_start(hp_out[bass.ds(p, 1), :, :].rearrange("a p n -> p (a n)"), h_t).then_inc(ssd_st, 16)
                pool.wait_ge(ssd_st, 32 * p + 32)
                pool.sem_inc(ssd_free, 1)

            pool.sem_inc(cc_free, 1)
            pool.sem_inc(ssd_free, 1)
            load_conv_state(0)
            load_conf_state(0)
            conf_prefix(0)
            save_conv_state(0)
            save_conf_state(0)
            with pool.Fori(1, GROUPS) as g:
                pool.wait_ge(sstate_used, g)
                load_conv_state(g)
                load_conf_state(g)
                add_cc(g - 1)
                conf_prefix(g)
                pool.wait_ge(sout_st, 16 * g)
                save_conv_state(g)
                store_ssd(g - 1)
                pool.wait_ge(cout_st, 16 * g)
                save_conf_state(g)
            add_cc(GROUPS - 1)
            store_ssd(GROUPS - 1)

            def load_group(g):
                s = g % 2
                pool.dma_start(st[s], ssm_state[g].rearrange("p (b n) -> p b n", n=256)).then_inc(st_in[s], 16)
                pool.dma_start(y_cur[s][:, :, 0:SEQ], y_dram[g]).then_inc(y_in[s], 16)

            pool.wait_ge(ssd_st, 32 * GROUPS)
            pool.wait_ge(cc_st, 16 * GROUPS)
            pool.wait_ge(cout_st, 16 * GROUPS)
            pool.wait_ge(sout_st, 16 * GROUPS)
            pool.wait_ge(dec_saved, 2 * GROUPS)
            pool.sem_inc(gates_free, 1)
            for g in range(2):
                load_group(g)
            for g in range(GROUPS):
                for j in range(2):
                    pool.wait_ge(tile_free[j], B_HALF + 8 * (g // 4) + g % 4 + 1)
                    pool.dma_start(gate_dram[g][:, j, :], gates_sb[:, j, :]).then_inc(gates_st, 16)
                pool.wait_ge(st_ready, g + 1)
                pool.dma_start(hs_out[g].rearrange("p (b n) -> p b n", n=256), st[g % 2]).then_inc(st_st, 16)
                pool.wait_ge(gates_st, 32 * (g + 1))
                pool.sem_inc(gates_free, 1)
                if g + 2 < GROUPS:
                    pool.wait_ge(st_st, 16 * (g + 1))
                    pool.wait_ge(yn_ready, 2 * (g + 1))
                    load_group(g + 2)

            pool.wait_ge(yn_ready, 2 * GROUPS)
            pool.wait_ge(st_st, 16 * GROUPS)
            pool.wait_ge(gates_st, 32 * GROUPS)
            for i in range(2):
                pool.dma_start(xc[:, 4 * i:4 * i + 4, :], cc_dram[4 * i:4 * i + 4].rearrange("a p n -> p a n"))\
                    .then_inc(cc_in, 16)
            pool.wait_ge(cc_in, 32)
            for m in range(KT):
                if m >= 2:
                    pool.wait_ge(p_m, 3 * (m - 1))
                pool.dma_start(g_in[:, m % 2, :, :], gate_dram[m]).then_inc(g_in_s[m % 2], 16)
            pool.wait_ge(p_m, 3 * KT)
            for m in range(KT):
                if m >= 2:
                    pool.wait_ge(tile_free[m % 2], B_WOUT + (m - 2) // 2 + 1)
                pool.dma_start(x_in[:, m % 2, :], x_all[:, m * T:(m + 1) * T]).then_inc(x_in2[m % 2], 16)
            for m in range(KT):
                pool.wait_ge(z_y, m + 1)
                pool.dma_start(y_out[:, m * T:(m + 1) * T], o_y[:, m % 2, :]).then_inc(out_st[m % 2], 16)
            for s in range(2):
                pool.wait_ge(out_st[s], 16 * KT // 2)

        @block.tensor
        def _(pe):
            def fill(b, rhs_hi, rhs_lo, t0, m0=0, m1=2):
                bs, be, count = b
                for m in range(m0, m1):
                    t = t0 + m
                    if m == 0:
                        pe.wait_ge(w_lo_s, be + 1)
                    if count(t) is not None:
                        pe.wait_ge(tile_free[t % 2], count(t))
                    for hf in range(2):
                        for k in range(KT):
                            at = k * BW + m * P
                            for j, (w, x) in enumerate(((w_hi, rhs_hi), (w_hi, rhs_lo), (w_lo, rhs_hi))):
                                last = pe.matmul(psum[t % 2][:, hf, 0:H2], w[:, bs, at:at + P],
                                                 x[:, k, hf * H2:(hf + 1) * H2],
                                                 start=(k == 0 and j == 0), stop=(k == KT - 1 and j == 2))
                    last.then_inc(tile_done, 1)

            def blk(slot, b):
                return slot, b, (lambda t: b) if not (isinstance(b, int) and b == 0) else (lambda t: None)

            pe.wait_ge(const_s, 1)
            for k in range(KT):
                pe.wait_ge(n_sq, k + 1)
                for hf in range(2):
                    last = pe.matmul(psum[0][:, hf, 0:H2], ones[:, :], sq0[:, k % 2, hf * H2:(hf + 1) * H2],
                                     start=(k == 0), stop=(k == KT - 1))
                last.then_inc(n_sum, 1)
            pe.wait_ge(wdt_ready, 1)
            pe.wait_ge(n_rstd, 1)
            wdt_hi = rb_hi[:, :, :].rearrange("p k t -> p (k t)")
            wdt_lo = rb_lo[:, :, :].rearrange("p k t -> p (k t)")
            for k in range(KT):
                pe.wait_ge(u_ready, k + 1)
                for hf in range(2):
                    for j, (w, x) in enumerate(((wdt_hi, ra_hi), (wdt_hi, ra_lo), (wdt_lo, ra_hi))):
                        last = pe.matmul(psum[0][:, hf, 0:H2], w[:, k * P:(k + 1) * P],
                                         x[:, k, hf * H2:(hf + 1) * H2],
                                         start=(k == 0 and j == 0), stop=(k == KT - 1 and j == 2))
            last.then_inc(dt_psum, 1)

            def pick_head(p, h):
                return sel[:, bass.ds(4 * p + h, 1), 0:1].rearrange("r a b -> r (a b)").broadcast_to([96, P])

            def pick_pair(p, j):
                return sel[:, bass.ds(4 * p + 2 * j, 2), :].rearrange("r a b -> r (a b)")

            def ssd_e(p):
                pe.wait_ge(sil_ready, 4 * p + 4)
                pe.wait_ge(nat_ready, 1)
                for j, bank in enumerate((ps, ph)):
                    pe.matmul(bank[:, :], pick_pair(p, j), acum_bf[:, 0:SEQ],
                              start=True, stop=True).then_inc(e_psum, 1)

            def ssd_1(c, p):
                cs = slice(c * CHUNK, (c + 1) * CHUNK)
                for j in range(3):
                    pe.transpose(pt[:, j * P:(j + 1) * P], sil[:, j, cs], ident[:, :])
                pe.matmul(pt[:, 3 * P:4 * P], sil[:, 2, cs], sil[:, 3, cs], start=True, stop=True)\
                    .then_inc(pt_done, 1)
                if c == 0:
                    pe.wait_ge(e_ready, p + 1)
                for h in range(HPG):
                    pe.matmul(ps[:, h * P:(h + 1) * P], pick_head(p, h), acum_bf[:, cs],
                              start=(h == 0), stop=False, skip_group_check=True)
                pe.matmul(ps[:, :], ident_bf[:, :], mask_bf[:, :].unsqueeze(1).broadcast_to([P, HPG, P]),
                          start=False, stop=True, skip_group_check=True).then_inc(ps_done, 1)

            def ssd_2(c, p):
                cs = slice(c * CHUNK, (c + 1) * CHUNK)
                pe.wait_ge(m_ready, NCH * p + c + 1)
                if c:
                    pe.wait_ge(h_ready, NCH * p + c)
                for h in range(HPG):
                    pe.matmul(py[(h % 2) * HD:(h % 2 + 1) * HD, (h // 2) * P:(h // 2 + 1) * P],
                              xdt[:, h * HD:(h + 1) * HD], m_t[:, h, :], start=True, stop=True,
                              skip_group_check=True)
                if c:
                    for j in range(2):
                        pe.matmul(py[:, 256 + j * P:256 + (j + 1) * P], h_t[:, j * P:(j + 1) * P], sil[:, 3, cs],
                                  start=True, stop=True, skip_group_check=True)
                pe.matmul(ph[:, 0:256], b_nat, wxdt, start=True, stop=True).then_inc(ys_done, 1)

            def group(g, ssd):
                p = g - 1
                if ssd:
                    ssd_e(p)
                    ssd_1(0, p)
                for j in range(4):
                    for m in range(2):
                        if not ssd and j == 0 and m == 0:
                            pe.wait_ge(dt_act, 1)
                        fill(blk(j % 2, 4 * g + j), ra_hi, ra_lo, 0, m, m + 1)
                        if ssd and j < 2:
                            c = 2 * j + m
                            ssd_2(c, p)
                            if c < NCH - 1:
                                ssd_1(c + 1, p)

            group(0, False)
            pe.wait_ge(acum_ready, 1)
            pe.wait_ge(const_s, 4)
            for q, src in enumerate((dt_r, dt_t)):
                for c in range(NCH + 1):
                    n = CHUNK if c < NCH else NDEC
                    last = pe.transpose(ps[0:n, (q * (NCH + 1) + c) * HEADS:(q * (NCH + 1) + c + 1) * HEADS],
                                        src[0:HEADS, c * CHUNK:c * CHUNK + n], ident[0:HEADS, 0:HEADS])
            last.then_inc(nat_t, 1)
            pe.wait_ge(nat_copied, 2)
            pe.matmul(py[:, 0:NCH * HEADS], ident[:, P - 1:P].broadcast_to([P, P]),
                      acum_nat[:, 0:NCH, :], start=True, stop=True)
            for b in range(NSEQ):
                last_tok = TDEC * b + TDEC - 1
                pe.matmul(py[:, (NCH + b) * HEADS:(NCH + b + 1) * HEADS],
                          ident[0:NDEC, last_tok:last_tok + 1].broadcast_to([NDEC, P]),
                          acum_nat[0:NDEC, NCH, :], start=True, stop=True)
            pe.matmul(ph[0:NDEC, 0:HEADS],
                      last_sel[:, :],
                      acum_nat[0:NDEC, NCH, :], start=True, stop=True).then_inc(nat_b, 1)
            with pe.Fori(1, GROUPS) as g:
                group(g, True)
            ssd_e(GROUPS - 1)
            ssd_1(0, GROUPS - 1)
            for c in range(NCH):
                ssd_2(c, GROUPS - 1)
                if c < NCH - 1:
                    ssd_1(c + 1, GROUPS - 1)

            def decode_in(g, s, turn):
                pe.wait_ge(d_cur_s, g + 1)
                pe.wait_ge(st_in[s], 16 * turn + 16)
                for j in range(2):
                    for b in range(NSEQ):
                        tok = slice(TDEC * b, TDEC * (b + 1))
                        last = pe.matmul(py[:, 64 + j * NDEC + TDEC * b:64 + j * NDEC + TDEC * (b + 1)],
                                         st[s][:, b, j * P:(j + 1) * P], d_cur[:, 3, tok], start=True, stop=True,
                                         skip_group_check=True)
                last.then_inc(d_off, 1)
                for j in range(3):
                    pe.transpose(pt[0:NDEC, j * P:(j + 1) * P], d_cur[:, j, :], ident[:, :])
                pe.matmul(pt[0:NDEC, 384:384 + NDEC], d_cur[:, 2, :], d_cur[:, 3, :], start=True, stop=True)\
                    .then_inc(d_pt, 1)
                for h in range(HPG):
                    pe.matmul(ps[:, h * NDEC:(h + 1) * NDEC], pick_head(g, h),
                              acum_bf[:, SEQ:T], start=(h == 0), stop=False, skip_group_check=True)
                pe.matmul(ps[:, 0:HPG * NDEC], ident_bf[0:NDEC, :],
                          mask_dec[:, :].unsqueeze(1).broadcast_to([NDEC, HPG, NDEC]), start=False, stop=True,
                          skip_group_check=True)
                for j in range(2):
                    last = pe.matmul(ps[:, 128 + j * NDEC:128 + (j + 1) * NDEC],
                                     pick_pair(g, j), acum_bf[:, SEQ:T],
                                     start=True, stop=True, skip_group_check=True)
                last.then_inc(d_ps, 1)

            def decode_add(bank, r):
                for b in range(2):
                    last = pe.matmul(bank[:, b * 256:(b + 1) * 256], d_bm[0:NDEC, 2 * r + b, :], d_wxdt[0:NDEC, :],
                                     start=True, stop=True, skip_group_check=True)
                return last

            def decode_mid(g):
                pe.wait_ge(d_m_s, g + 1)
                for h in range(HPG):
                    pe.matmul(py[(h % 2) * HD:(h % 2 + 1) * HD, (h // 2) * NDEC:(h // 2 + 1) * NDEC],
                              d_xdt[0:NDEC, h * HD:(h + 1) * HD], d_m[0:NDEC, h, :], start=True, stop=True,
                              skip_group_check=True)
                for r, bank in enumerate((ph, ps, pt)):
                    last = decode_add(bank, r)
                last.then_inc(d_y, 1)

            def decode_end(g):
                pe.wait_ge(d_add, 3 * g + 1)
                decode_add(ph, 3).then_inc(d_r3, 1)
                pe.wait_ge(d_ssum_s, g + 1)
                pe.matmul(ps[:, :], ones[:, :], d_ssum[:, 0:SEQ], start=True, stop=True)
                pe.matmul(pt[:, 0:NDEC], ones[:, :], d_ssum[:, SEQ:T], start=True, stop=True).then_inc(d_stat, 1)

            pe.wait_ge(h_ready, NCH * GROUPS)
            for q in range(2):
                with pe.Fori(0, 2) as i:
                    for s in range(2):
                        g = 4 * q + 2 * i + s
                        b = B_HALF + 8 * q + 2 * i + s
                        decode_in(g, s, 2 * q + i)
                        fill(blk(s, b), ra_hi, ra_lo, 0, 0, 1)
                        decode_mid(g)
                        fill(blk(s, b), ra_hi, ra_lo, 0, 1, 2)
                        decode_end(g)
                if q == 1:
                    pe.wait_ge(cc_added, GROUPS)
                    pe.wait_ge(d_rstd_s, GROUPS)
                    for hf, bank in enumerate((pt, ps)):
                        last = pe.matmul(bank[:, 0:H2], ones[:, :], cc_sum[:, hf * H2:(hf + 1) * H2],
                                         start=True, stop=True)
                    last.then_inc(l_stat, 1)
                pe.wait_ge(yn_ready, 8 * (q + 1))
                for i in range(4):
                    fill(blk(i % 2, B_HALF + 8 * q + 4 + i), rb_hi, rb_lo, 0)
                    if q == 1 and i == 1:
                        pe.wait_ge(l_ssum_s, KT)
                        for hf, bank in enumerate((py, ph)):
                            last = pe.matmul(bank[:, 0:H2], ones[:, :], l_ssum[:, hf * H2:(hf + 1) * H2],
                                             start=True, stop=True)
                        last.then_inc(l_stat2, 1)
            pe.wait_ge(cc_ready2, KT)
            with pe.Fori(0, 2) as i:
                for s in range(2):
                    fill(blk(s, B_PW + 2 * i + s), ra_hi, ra_lo, 0)
            pe.wait_ge(mg_ready, KT)
            with pe.Fori(0, 2) as i:
                for s in range(2):
                    fill(blk(s, B_WOUT + 2 * i + s), rb_hi, rb_lo, 0)
            pe.wait_ge(hn_ready, KT)
            pe.wait_ge(o_sum_s, KT)
            for hf, bank in enumerate((pt, ps)):
                last = pe.matmul(bank[:, 0:H2], ones[:, :], o_ssum[:, hf * H2:(hf + 1) * H2],
                                 start=True, stop=True)
            last.then_inc(o_stat, 1)
            with pe.Fori(0, 4) as i:
                for j in range(4):
                    fill(blk(j % 2, B_FFN + 8 * i + j), ra_hi, ra_lo, 0)
                pe.wait_ge(f_ready, KT * i + KT)
                for j in range(4):
                    fill(blk(j % 2, B_FFN + 8 * i + 4 + j), rb_hi, rb_lo, 0)
            for k in range(KT):
                pe.wait_ge(z_sq, k + 1)
                for hf, bank in enumerate((py, ph)):
                    last = pe.matmul(bank[:, 0:H2], ones[:, :], o_sq[:, k % 2, hf * H2:(hf + 1) * H2],
                                     start=(k == 0), stop=(k == KT - 1))
                last.then_inc(z_stat, 1)

        @block.scalar
        def _(act):
            steps = Steps(act, act_c)

            def hi(b, s, turn):
                act.wait_ge(w_in[s], 16 * turn + 16)
                if not isinstance(b, int) or b >= 2:
                    act.wait_ge(tile_done, 2 * b - 2)
                act.activation(w_hi[:, s, :], w_raw[:, s, :], ACT.Copy).then_inc(w_hi_s, 1)

            def hi_next(pair, s):
                if s == 0:
                    hi(2 * pair + 1, 1, pair)
                else:
                    hi(2 * pair + 2, 0, pair + 1)

            for k in range(KT):
                act.wait_ge(x_in_s[2 * k // KT], 16)
                if k >= 2:
                    act.wait_ge(n_sum, k - 1)
                act.activation(sq0[:, k % 2, :], x_t[:, k, :], ACT.Square).then_inc(n_sq, 1)
            act.wait_ge(const_s, 2)
            act.wait_ge(n_sum, KT)
            n = steps.did(act.activation(halves(rstd0), main(0), ACT.Ln, bias=eps[:, :], scale=1.0 / D_MODEL))
            steps.need(n)
            act.activation(rstd0, rstd0, ACT.Exp, scale=-0.5).then_inc(n_rstd, 1)
            act.wait_ge(wdt_in, 16)
            act.activation(rb_hi[:, :, :].rearrange("p k t -> p (k t)")[:, 0:KT * P], wdt_raw, ACT.Copy)\
                .then_inc(wdt_hi_s, 1)
            for k in range(KT):
                act.wait_ge(n_xn, k + 1)
                act.activation(ra_hi[:, k, :], xn0[:, k % 2, :], ACT.Copy).then_inc(u_hi_s, 1)
            hi(0, 0, 0)
            act.wait_ge(par_s, 32)
            act.wait_ge(dt_psum, 1)
            act.activation(halves(dt_v), main(0), ACT.Identity, bias=dt_pars[:, 0:1]).then_inc(dt_act, 1)
            act.activation(a_neg[:, :], dt_pars[:, 1:2], ACT.Exp).then_inc(dt_act, 1)
            hi(1, 1, 0)
            act.wait_ge(dt_dve, 1)
            act.activation(dt_e, dt_e, ACT.Exp).then_inc(dt_act, 1)

            def evac_raw(g, j, m, first):
                i = 2 * j + m
                if i == 0:
                    act.wait_ge(par_ready, 1)
                    act.wait_ge(sstate_in, 16 * g + 16)
                    if not first:
                        act.wait_ge(sil_ready, 4 * g)
                        act.wait_ge(sout_copied, g)
                    act.activation(raw_d[:, :, :, 0:SPRE], sstate, ACT.Copy).then_inc(sstate_used, 1)
                act.wait_ge(tile_done, 8 * g + i + 1)
                q = H2 - NDEC
                act.activation(raw[:, i, SPRE:SPRE + H2], psum[m][:, 0, 0:H2], ACT.Copy)
                act.activation(raw[:, i, SPRE + H2:], psum[m][:, 1, 0:q], ACT.Copy)
                act.activation(raw_d[:, i, :, SPRE:], psum[m][:, 1, q:H2].rearrange("p (b t) -> p b t", t=TDEC),
                               ACT.Copy).then_inc(raw_ready, 1)
                act.activation(halves(acc[:, i, :]), main(m), ACT.Identity,
                               bias=par1("ssm_b", 4 * g + i), scale=par1("ssm_w", (4 * g + i) * SK + SK - 1))\
                    .then_inc(tile_free[m], 1)

            def ssd_exps(c, p):
                act.wait_ge(pt_done, NCH * p + c + 1)
                act.activation(b_nat, pt[:, 2 * P:3 * P], ACT.Copy)
                act.activation(scores, pt[:, 3 * P:4 * P], ACT.Copy).then_inc(bs_ready, 1)
                act.wait_ge(ps_done, NCH * p + c + 1)
                for h in range(HPG):
                    last = act.activation(decay[:, h, :], ps[:, h * P:(h + 1) * P], ACT.Exp,
                                          bias=nacum_nat[:, c, bass.ds(4 * p + h, 1)])
                last.then_inc(decay_ready, 1)

            def ssd_e_exp(p):
                for j, bank in enumerate((ps, ph)):
                    act.wait_ge(e_psum, 2 * p + j + 1)
                    last = act.activation(e_acc[:, j, :], bank[:, :], ACT.Exp)
                last.then_inc(e_ready, 1)

            def group(g, ssd):
                p = g - 1
                hi(4 * g + 1, 1, 2 * g) if ssd else None
                if ssd:
                    ssd_e_exp(p)
                for j in range(2):
                    for m in range(2):
                        if ssd:
                            ssd_exps(2 * j + m, p)
                        evac_raw(g, j, m, not ssd)
                    hi(4 * g + 2 + j, j % 2, 2 * g + 1)
                for m in range(2):
                    if m == 0 and ssd:
                        act.wait_ge(y_done, g)
                        act.wait_ge(glu_ready, g)
                    act.wait_ge(tile_done, 8 * g + 5 + m)
                    act.activation(zs[:, m, :].rearrange("p (a b) -> p a b", a=2), main(m), ACT.Tanh, scale=0.5)
                    act.activation(halves(zh[:, m, :]), main(m), ACT.Copy, scale=0.5).then_inc(tile_free[m], 1)
                hi(4 * g + 4, 0, 2 * g + 2)
                for i in range(4):
                    act.wait_ge(conv4_s, 4 * g + i + 1)
                    act.activation(sil[:, i, :], acc[:, i, :], ACT.Tanh).then_inc(sil_th, 1)
                act.wait_ge(z_ready, g + 1)
                for m, func in ((0, ACT.Copy), (1, ACT.Tanh)):
                    act.wait_ge(tile_done, 8 * g + 7 + m)
                    act.activation(halves(zh[:, m, :]), main(m), func, scale=0.5).then_inc(tile_free[m], 1)
                act.wait_ge(sil_ready, 4 * g + 4)
                act.activation(dec_xbc[:, bass.ds(g, 1), :, :].rearrange("p a i n -> p (a i) n"), sil[:, :, SEQ:T],
                               ACT.Copy).then_inc(dec_saved, 1)
                act.activation(dec_z[:, bass.ds(g, 1), :, :].rearrange("p a i n -> p (a i) n"), zs[:, :, SEQ:T],
                               ACT.Copy).then_inc(dec_saved, 1)

            group(0, False)
            act.wait_ge(nat_t, 1)
            for q, dst in enumerate((dt_nat, acum_nat)):
                at = q * (NCH + 1) * HEADS
                steps.did(act.activation(dst[:, 0:NCH, :].rearrange("p c h -> p (c h)"),
                                         ps[:, at:at + NCH * HEADS], ACT.Copy))
                act.activation(dst[0:NDEC, NCH, :], ps[0:NDEC, at + NCH * HEADS:at + (NCH + 1) * HEADS],
                               ACT.Copy).then_inc(nat_copied, 1)
            act.wait_ge(nat_diff, 1)
            act.activation(exp_last[:, :, :].rearrange("p c h -> p (c h)"), py[:, 0:(NCH + NSEQ) * HEADS], ACT.Exp)
            steps.did(act.activation(w_nat[:, 0:NCH, :], w_nat[:, 0:NCH, :], ACT.Exp))
            act.activation(w_nat[0:NDEC, NCH, :], w_nat[0:NDEC, NCH, :], ACT.Exp).then_inc(nat_ready, 1)
            with act.Fori(1, GROUPS) as g:
                group(g, True)
            ssd_e_exp(GROUPS - 1)
            for c in range(NCH):
                ssd_exps(c, GROUPS - 1)

            act.wait_ge(y_done, GROUPS)
            for q in range(2):
                with act.Fori(0, 2) as i:
                    steps.enter(i, 4)
                    for s in range(2):
                        g = 4 * q + 2 * i + s
                        b = B_HALF + 8 * q + 2 * i + s
                        act.activation(d_cur, dec_xbc[:, bass.ds(g, 1), :, :].rearrange("p a i n -> p (a i) n"),
                                       ACT.Copy).then_inc(d_cur_s, 1)
                        hi_next(B_HALF // 2 + 4 * q + i, s)
                        act.wait_ge(d_pt, g + 1)
                        act.activation(d_bn[0:NDEC, :], pt[0:NDEC, 2 * P:3 * P], ACT.Copy)
                        act.activation(d_sc[0:NDEC, :], pt[0:NDEC, 384:384 + NDEC], ACT.Copy).then_inc(d_bn_s, 1)
                        act.wait_ge(d_ps, g + 1)
                        for h in range(HPG):
                            act.activation(d_decay[0:NDEC, h, :], ps[0:NDEC, h * NDEC:(h + 1) * NDEC], ACT.Exp,
                                           bias=nacum_nat[0:NDEC, NCH, bass.ds(4 * g + h, 1)])
                        act.activation(d_e.rearrange("p a b -> p (a b)"), ps[:, 128:128 + 2 * NDEC], ACT.Exp)\
                            .then_inc(d_dec_s, 1)
                        act.wait_ge(gates_free, g + 1)
                        act.wait_ge(tile_done, 2 * b + 1)
                        act.activation(halves(gates_sb[:, 0, :]), main(0), ACT.Copy).then_inc(tile_free[0], 1)
                        act.wait_ge(d_ycur, g + 1)
                        act.activation(d_sq, y_cur[s], ACT.Square).then_inc(d_sq_s, 1)
                        act.wait_ge(tile_done, 2 * b + 2)
                        act.activation(halves(gates_sb[:, 1, :]), main(1), ACT.Copy).then_inc(tile_free[1], 1)
                        act.wait_ge(d_stat, g + 1)
                        steps.did(act.activation(d_rstd[:, 0:SEQ], ps[:, :], ACT.Ln, bias=eps[:, :],
                                                 scale=1.0 / 256))
                        n = steps.did(act.activation(d_rstd[:, SEQ:T], pt[:, 0:NDEC], ACT.Ln, bias=eps[:, :],
                                                     scale=1.0 / 256))
                        steps.need(n)
                        act.activation(d_rstd, d_rstd, ACT.Exp, scale=-0.5).then_inc(d_rstd_s, 1)
                        for j in range(2):
                            act.wait_ge(d_yn_s, 2 * g + j + 1)
                            act.activation(rb_hi[:, bass.ds(4 * i + 2 * s + j, 1), :].rearrange("p a n -> p (a n)"),
                                           d_yn[:, j, :], ACT.Copy).then_inc(yn_hi_s, 1)
                steps.leave(2)
                if q == 0:
                    with act.Fori(0, 2) as i:
                        for s in range(2):
                            hi_next(B_HALF // 2 + 2 + i, s)
                            for m in range(2):
                                act.wait_ge(tile_done, 2 * (B_HALF + 4 + 2 * i + s) + m + 1)
                                act.activation(b_sum[:, bass.ds(4 * i + 2 * s + m, 1), :]
                                               .rearrange("p a (h n) -> p (a h) n", h=2), main(m), ACT.Copy,
                                               scale=0.5).then_inc(tile_free[m], 1)
            act.wait_ge(l_stat, 1)
            for hf, bank in enumerate((pt, ps)):
                last = act.activation(l_mean[:, hf * H2:(hf + 1) * H2], bank[:, 0:H2], ACT.Copy,
                                      scale=1.0 / D_MODEL)
            last.then_inc(l_mean_s, 1)
            hi_next(B_HALF // 2 + 6, 0)
            for m in range(KT):
                act.wait_ge(l_xc, m + 1)
                if m >= 2:
                    act.wait_ge(l_ssum_s, m - 1)
                act.activation(l_sq[:, m % 2, :], xc[:, m, :], ACT.Square).then_inc(l_sq_s, 1)
                if m == 5:
                    hi_next(B_HALF // 2 + 6, 1)
            act.wait_ge(l_stat2, 1)
            for hf, bank in enumerate((py, ph)):
                n = steps.did(act.activation(l_rstd[:, hf * H2:(hf + 1) * H2], bank[:, 0:H2], ACT.Ln,
                                             bias=eps[:, :], scale=1.0 / D_MODEL))
            steps.need(n)
            act.activation(l_rstd, l_rstd, ACT.Exp, scale=-0.5).then_inc(l_rstd_s, 1)
            hi_next(B_HALF // 2 + 7, 0)

            def cc_high(m):
                act.wait_ge(l_sil, m + 1)
                act.activation(ra_hi[:, m, :], xc[:, m, :], ACT.Copy).then_inc(cc_hi_s, 1)

            for m in range(KT):
                act.wait_ge(l_t, m + 1)
                if m >= 2:
                    act.wait_ge(l_sil, m - 1)
                n = steps.did(act.activation(l_a[:, m % 2, :], xc[:, m, :], ACT.Identity,
                                             bias=par1("ln_b", m), scale=par1("ln_g", m)))
                steps.need(n)
                act.activation(l_th[:, m % 2, :], l_a[:, m % 2, :], ACT.Tanh).then_inc(l_th_s, 1)
                if m >= 1:
                    cc_high(m - 1)
                if m == 5:
                    hi_next(B_HALF // 2 + 7, 1)
            cc_high(KT - 1)
            for m in range(KT):
                act.wait_ge(g_in_s[m % 2], 16 * (m // 2) + 16)
                act.activation(g_in[:, m % 2, :, :], g_in[:, m % 2, :, :], ACT.Tanh, scale=0.5)
                act.wait_ge(tile_done, 2 * B_PW + m + 1)
                act.activation(halves(pw_a[:, m % 2, :]), main(m), ACT.Identity, bias=par1("b_pw", m), scale=0.5)\
                    .then_inc(tile_free[m % 2], 1)
                if m >= 1:
                    act.wait_ge(p_m, 3 * m)
                    act.activation(rb_hi[:, m - 1, :], pw_m[:, (m - 1) % 2, :], ACT.Copy).then_inc(mg_hi, 1)
                if m % 2 == 0:
                    hi_next((B_PW + m // 2) // 2, (m // 2) % 2)
            act.wait_ge(p_m, 3 * KT)
            act.activation(rb_hi[:, KT - 1, :], pw_m[:, (KT - 1) % 2, :], ACT.Copy).then_inc(mg_hi, 1)
            for m in range(KT):
                if m % 2 == 0:
                    hi_next((B_WOUT + m // 2) // 2, (m // 2) % 2)
                act.wait_ge(tile_free[m % 2], B_WOUT + m // 2 + 1)
                if m >= 2:
                    act.wait_ge(o_sum_s, m - 1)
                act.activation(o_sq[:, m % 2, :], h_sb[:, m, :], ACT.Square).then_inc(o_act, 1)
                act.activation(ra_hi[:, m, :], h_sb[:, m, :], ACT.Copy, scale=par1("g_ffn", m)).then_inc(o_act, 1)
            act.wait_ge(o_stat, 1)
            for hf, bank in enumerate((pt, ps)):
                n = steps.did(act.activation(o_rstd[:, hf * H2:(hf + 1) * H2], bank[:, 0:H2], ACT.Ln,
                                             bias=eps[:, :], scale=1.0 / D_MODEL))
            steps.need(n)
            act.activation(o_rstd, o_rstd, ACT.Exp, scale=-0.5).then_inc(o_rstd_s, 1)

            def hidden(i, n):
                k = KT * i + n
                act.wait_ge(f_v_s, k + 1)
                act.activation(f_s[:, n % 2, :], f_v[:, n % 2, :], ACT.Square).then_inc(f_sq_s, 1)
                act.wait_ge(f_sq_s, k + 1)
                act.activation(rb_hi[:, n, :], f_s[:, n % 2, :], ACT.Copy).then_inc(f_hi, 1)

            def quarter(i, last):
                for j in range(4):
                    hi_next(B_FFN // 2 + 4 * i + j // 2, j % 2)
                    for m in range(2):
                        n = 2 * j + m
                        act.wait_ge(tile_done, 2 * B_FFN + 16 * i + n + 1)
                        act.activation(halves(f_r[:, n % 2, :]), main(m), ACT.Relu).then_inc(tile_free[m], 1)
                        if n >= 1:
                            hidden(i, n - 1)
                hidden(i, KT - 1)
                for j in range(3 if last else 4):
                    hi_next(B_FFN // 2 + 4 * i + 2 + j // 2, j % 2)

            with act.Fori(0, 3) as i:
                quarter(i, False)
            quarter(3, True)
            for m in range(KT):
                act.wait_ge(tile_free[m % 2], NBLOCKS - 3 + m // 2)
                if m >= 2:
                    act.wait_ge(z_stat, m - 1)
                act.activation(o_sq[:, m % 2, :], h_sb[:, m, :], ACT.Square).then_inc(z_sq, 1)
            act.wait_ge(z_stat, KT)
            for hf, bank in enumerate((py, ph)):
                n = steps.did(act.activation(o_rstd[:, hf * H2:(hf + 1) * H2], bank[:, 0:H2], ACT.Ln,
                                             bias=eps[:, :], scale=1.0 / D_MODEL))
            steps.need(n)
            act.activation(o_rstd, o_rstd, ACT.Exp, scale=-0.5).then_inc(z_rstd, 1)

        @block.vector
        def _(dve):
            steps = Steps(dve, dve_c)

            def lo(b, s):
                dve.wait_ge(w_hi_s, b + 1)
                dve.tensor_tensor(w_lo[:, s, :], w_raw[:, s, :], fr(w_hi[:, s, :]), ALU.subtract)\
                    .then_inc(w_lo_s, 1)

            def lo_next(pair, s):
                lo(2 * pair + 1, 1) if s == 0 else lo(2 * pair + 2, 0)

            dve.wait_ge(par_s, 32)
            for name in ("ssm_w", "ssm_b", "ln_g", "ln_b"):
                at, n = PARAMS[name]
                steps.did(dve.tensor_scalar(pars[:, at:at + n], pars[:, at:at + n], 0.5, None, ALU.mult))
            at, n = PARAMS["b_pw"]
            dve.tensor_scalar(pars[:, at:at + n], pars[:, at:at + n], 0.5, None, ALU.mult).then_inc(par_ready, 1)
            dve.wait_ge(n_rstd, 1)
            for k in range(KT):
                if k >= 2:
                    dve.wait_ge(u_hi_s, k - 1)
                dve.scalar_tensor_tensor(xn0[:, k % 2, :], x_t[:, k, :], par1("g_mix", k), rstd0, ALU.mult,
                                         ALU.mult).then_inc(n_xn, 1)
                if k == 0:
                    dve.wait_ge(wdt_hi_s, 1)
                    dve.tensor_tensor(rb_lo[:, :, :].rearrange("p k t -> p (k t)")[:, 0:KT * P], wdt_raw,
                                      fr(rb_hi[:, :, :].rearrange("p k t -> p (k t)")[:, 0:KT * P]),
                                      ALU.subtract).then_inc(wdt_ready, 1)
                dve.wait_ge(u_hi_s, k + 1)
                dve.wait_ge(n_xn, k + 1)
                dve.tensor_tensor(ra_lo[:, k, :], xn0[:, k % 2, :], fr(ra_hi[:, k, :]), ALU.subtract)\
                    .then_inc(u_ready, 1)
            lo(0, 0)
            dve.wait_ge(dt_act, 2)
            dve.scalar_tensor_tensor(dt_e, dt_v, -1.0, dt_v, ALU.mult, ALU.min).then_inc(dt_dve, 1)
            steps.did(dve.tensor_scalar(a_neg[:, :], a_neg[:, :], -1.0, None, ALU.mult))
            n_r = steps.did(dve.tensor_scalar(dt_r, dt_v, 0.0, None, ALU.max))
            lo(1, 1)
            dve.wait_ge(dt_act, 3)
            n = steps.did(dve.tensor_scalar(dt_z, dt_e, 2.0, None, ALU.add))
            steps.need(n)
            n = steps.did(dve.reciprocal(dt_z, dt_z))
            steps.need(n)
            n_z = steps.did(dve.tensor_tensor(dt_z, dt_z, dt_e, ALU.mult))
            steps.need(n_z)
            n = steps.did(dve.tensor_tensor(dt_z2, dt_z, dt_z, ALU.mult))
            steps.need(n)
            n = steps.did(dve.tensor_scalar(dt_p, dt_z2, 1.0 / 17, None, ALU.mult))
            for odd in range(15, 1, -2):
                steps.need(n)
                n = steps.did(dve.scalar_tensor_tensor(dt_p, dt_p, 1.0 / odd, dt_z2, ALU.add, ALU.mult))
            steps.need(n)
            n = steps.did(dve.scalar_tensor_tensor(dt_t, dt_p, 1.0, dt_z, ALU.add, ALU.mult))
            steps.need(n)
            n = steps.did(dve.scalar_tensor_tensor(dt_r, dt_t, 2.0, dt_r, ALU.mult, ALU.add))
            steps.need(n)
            n = steps.did(dve.tensor_scalar(dt_p, dt_r, a_neg[:, :], None, ALU.mult))
            steps.need(n)
            dve.wait_ge(const_s, 3)
            n = steps.did(dve.tensor_tensor_scan(dt_t, scan_keep, dt_p, 0.0, ALU.mult, ALU.add))
            steps.need(n)
            n = steps.did(dve.tensor_copy(acum_bf[:, :], dt_t[0:96, :]))
            steps.need(n)
            n = steps.did(dve.tensor_tensor(dt_z[0:96, :], dt_t[0:96, :], acum_bf[:, :], ALU.subtract))
            steps.need(n)
            steps.did(dve.tensor_copy(acum_bf[32:64, :], dt_z[32:64, :]))
            n = steps.did(dve.tensor_copy(acum_bf[64:96, :], dt_z[64:96, :]))
            steps.need(n)
            n = steps.did(dve.tensor_tensor(dt_z[64:96, :], dt_z[64:96, :], acum_bf[64:96, :], ALU.subtract))
            steps.need(n)
            dve.tensor_copy(acum_bf[64:96, :], dt_z[64:96, :]).then_inc(acum_ready, 1)

            class Conv31:

                def __init__(self, p):
                    self.p, self.k, self.last = p, 0, [None, None]
                    dve.wait_ge(glu_ready, p + 1)

                def taps(self, n):
                    for k in range(self.k, min(self.k + n, CK)):
                        to = (conv_a, conv_b)[k % 2]
                        w = par1("conf_w", self.p * CK + k)
                        src = gx[:, k:k + SEQ]
                        if k == 0:
                            ins = dve.tensor_scalar(to, src, w, par1("conf_b", self.p), ALU.mult, ALU.add)
                        elif k == 1:
                            ins = dve.tensor_scalar(to, src, w, None, ALU.mult)
                        else:
                            steps.need(self.last[k % 2])
                            ins = dve.scalar_tensor_tensor(to, src, w, to, ALU.mult, ALU.add)
                        self.last[k % 2] = steps.did(ins)
                    self.k = min(self.k + n, CK)

                def finish(self):
                    self.taps(CK)
                    dve.wait_ge(cc_free, self.p + 1)
                    steps.need(max(self.last))
                    n = steps.did(dve.tensor_tensor(ccs[:, 0:SEQ], conv_a, conv_b, ALU.add))
                    dve.wait_ge(cpre_ready, self.p + 1)
                    hs = NSEQ // 2
                    prod = conv_b[:, 0:hs * TDEC * CK]
                    base = gd[:, 0:1, 0:1]
                    w = par1("conf_w", self.p * CK, CK)
                    for b in range(2):
                        wins = bass.AP(base.tensor, base.offset + b * hs * (CPRE + TDEC),
                                       [[base.ap[0][0], P], [CPRE + TDEC, hs], [1, TDEC], [1, CK]])
                        steps.need(n)
                        n = steps.did(dve.tensor_tensor(
                            prod.rearrange("p (b t k) -> p b t k", b=hs, t=TDEC), wins,
                            w.unsqueeze(1).unsqueeze(1).broadcast_to([P, hs, TDEC, CK]), ALU.mult))
                        steps.need(n)
                        n = steps.did(dve.tensor_reduce(
                            ccs[:, SEQ + b * hs * TDEC:SEQ + (b + 1) * hs * TDEC],
                            prod.rearrange("p (n k) -> p n k", k=CK), AX.X, ALU.add))
                    steps.need(n)
                    dve.tensor_scalar(ccs[:, SEQ:T], ccs[:, SEQ:T], par1("conf_b", self.p), None, ALU.add)\
                        .then_inc(cc_ready, 1)

            def by_head(ap, c, p):
                return ap[:, c, bass.ds(4 * p, HPG)].unsqueeze(2).broadcast_to([P, HPG, HD])

            def heads(ap):
                return ap.rearrange("p (h d) -> p h d", d=HD)

            def ssd_steps(c, p):
                dve.wait_ge(bs_ready, NCH * p + c + 1)
                n = steps.did(dve.tensor_tensor(heads(xdt), heads(pt[:, 0:256]), by_head(dt_nat, c, p), ALU.mult))
                steps.need(n)
                steps.did(dve.tensor_tensor(heads(wxdt), heads(xdt), by_head(w_nat, c, p), ALU.mult))

            def ssd_scores(c, p):
                dve.wait_ge(decay_ready, NCH * p + c + 1)
                dve.tensor_tensor(m_t, decay, scores.unsqueeze(1).broadcast_to([P, HPG, P]), ALU.mult)\
                    .then_inc(m_ready, 1)

            def ssd_state(c, p):
                cs = slice(c * CHUNK, (c + 1) * CHUNK)
                y_in_chunk = py[:, 0:256].rearrange("p (j n) -> p j n", j=2)
                dve.wait_ge(ys_done, NCH * p + c + 1)
                if c == 0:
                    dve.wait_ge(ssd_free, p + 1)
                    steps.did(dve.tensor_copy(y_sb[:, :, cs], y_in_chunk))
                    dve.tensor_copy(h_t, ph[:, 0:256]).then_inc(h_ready, 1)
                else:
                    if c == 1:
                        dve.wait_ge(e_ready, p + 1)
                    n = steps.did(dve.tensor_tensor(y_tmp, py[:, 256:512].rearrange("p (j n) -> p j n", j=2),
                                                    e_acc[:, :, cs], ALU.mult))
                    dve.wait_ge(h_ready, NCH * p + c)
                    n2 = steps.did(dve.tensor_tensor(heads(h_t), heads(h_t), by_head(exp_last, c, p), ALU.mult))
                    steps.need(n)
                    steps.did(dve.tensor_tensor(y_sb[:, :, cs], y_tmp, y_in_chunk, ALU.add))
                    steps.need(n2)
                    dve.tensor_tensor(h_t, h_t, ph[:, 0:256], ALU.add).then_inc(h_ready, 1)

            def ssd_y(p):
                steps.need(steps.n)
                for j in range(2):
                    n = steps.did(dve.scalar_tensor_tensor(y_sb[:, j, :], sil[:, j, 0:SEQ],
                                                           par1("d_skip", 2 * p + j), y_sb[:, j, :], ALU.mult,
                                                           ALU.add))
                steps.need(n)
                dve.tensor_tensor(y_sb, y_sb, zs[:, :, 0:SEQ], ALU.mult).then_inc(y_done, 1)

            def conv4(g, pair):
                tiles = (2 * pair, 2 * pair + 1)
                for i in tiles:
                    dve.wait_ge(tile_free[i % 2], 4 * g + i // 2 + 1)
                last = {}
                for k in range(SK - 1):
                    for i in tiles:
                        w = par1("ssm_w", (4 * g + i) * SK + k)
                        if k:
                            steps.need(last[i])
                        to = acc[:, i, 0:SEQ]
                        to_d = acc[:, i, SEQ:T].rearrange("p (b t) -> p b t", t=TDEC)
                        steps.did(dve.scalar_tensor_tensor(to, raw[:, i, k:k + SEQ], w, to, ALU.mult, ALU.add))
                        ins = dve.scalar_tensor_tensor(to_d, raw_d[:, i, :, k:k + TDEC], w, to_d, ALU.mult, ALU.add)
                        if k == SK - 2:
                            ins.then_inc(conv4_s, 1)
                        else:
                            last[i] = steps.did(ins)

            def silu4(g, i):
                dve.wait_ge(sil_th, 4 * g + i + 1)
                dve.scalar_tensor_tensor(sil[:, i, :], sil[:, i, :], 1.0, acc[:, i, :], ALU.add, ALU.mult)\
                    .then_inc(sil_ready, 1)

            def group(g, ssd):
                p = g - 1
                if ssd:
                    lo(4 * g + 1, 1)
                    conv = Conv31(p)
                    for c in range(NCH):
                        ssd_steps(c, p)
                        conv.taps(5)
                        ssd_scores(c, p)
                        conv.taps(3)
                        ssd_state(c, p)
                        if c == 1:
                            lo(4 * g + 2, 0)
                    ssd_y(p)
                    conv.finish()
                else:
                    dve.wait_ge(const_s, 6)
                    lo(4 * g + 2, 0)
                lo(4 * g + 3, 1)
                conv4(g, 0)
                conv4(g, 1)
                for i in range(4):
                    silu4(g, i)
                dve.wait_ge(tile_free[1], 4 * g + 3)
                dve.scalar_tensor_tensor(zs, zs, 1.0, zh, ALU.add, ALU.mult).then_inc(z_ready, 1)
                lo(4 * g + 4, 0)
                dve.wait_ge(tile_free[1], 4 * g + 4)
                if ssd:
                    dve.wait_ge(cout_copied, g)
                steps.did(dve.scalar_tensor_tensor(gx[:, CPRE:], zh[:, 1, 0:SEQ], 1.0, zh[:, 0, 0:SEQ], ALU.add,
                                                   ALU.mult))
                dve.scalar_tensor_tensor(gd[:, :, CPRE:], zh[:, 1, SEQ:T].rearrange("p (b t) -> p b t", t=TDEC), 1.0,
                                         zh[:, 0, SEQ:T].rearrange("p (b t) -> p b t", t=TDEC), ALU.add, ALU.mult)\
                    .then_inc(glu_ready, 1)

            group(0, False)
            dve.wait_ge(nat_copied, 2)
            steps.did(dve.tensor_scalar(nacum_nat[:, 0:NCH, :], acum_nat[:, 0:NCH, :], -1.0, None, ALU.mult))
            steps.did(dve.tensor_scalar(nacum_nat[0:NDEC, NCH, :], acum_nat[0:NDEC, NCH, :], -1.0, None, ALU.mult))
            dve.wait_ge(nat_b, 1)
            steps.did(dve.tensor_tensor(w_nat[:, 0:NCH, :], py[:, 0:NCH * HEADS]
                                        .rearrange("p (c h) -> p c h", h=HEADS), acum_nat[:, 0:NCH, :],
                                        ALU.subtract))
            dve.tensor_tensor(w_nat[0:NDEC, NCH, :], ph[0:NDEC, 0:HEADS], acum_nat[0:NDEC, NCH, :], ALU.subtract)\
                .then_inc(nat_diff, 1)
            dve.wait_ge(nat_ready, 1)
            with dve.Fori(1, GROUPS) as g:
                steps.enter(g - 1, K_GROUP)
                group(g, True)
            steps.leave(GROUPS - 1)
            conv = Conv31(GROUPS - 1)
            for c in range(NCH):
                ssd_steps(c, GROUPS - 1)
                conv.taps(3)
                ssd_scores(c, GROUPS - 1)
                conv.taps(3)
                ssd_state(c, GROUPS - 1)
            ssd_y(GROUPS - 1)
            conv.finish()

            dve.wait_ge(dec_saved, 2 * GROUPS)
            for q in range(2):
                with dve.Fori(0, 2) as i:
                    steps.enter(i, K_DECODE)
                    for s in range(2):
                        g = 4 * q + 2 * i + s
                        turn = 2 * q + i
                        lo_next(B_HALF // 2 + 4 * q + i, s)
                        dve.wait_ge(d_bn_s, g + 1)
                        n = steps.did(dve.tensor_tensor(
                            heads(d_xdt[0:NDEC, :]), heads(pt[0:NDEC, 0:256]),
                            dt_nat[0:NDEC, NCH, bass.ds(4 * g, HPG)].unsqueeze(2).broadcast_to([NDEC, HPG, HD]),
                            ALU.mult))
                        steps.need(n)
                        steps.did(dve.tensor_tensor(
                            heads(d_wxdt[0:NDEC, :]), heads(d_xdt[0:NDEC, :]),
                            w_nat[0:NDEC, NCH, bass.ds(4 * g, HPG)].unsqueeze(2).broadcast_to([NDEC, HPG, HD]),
                            ALU.mult))
                        steps.did(dve.tensor_tensor(
                            d_bm[0:NDEC], d_bn[0:NDEC, :].unsqueeze(1).broadcast_to([NDEC, NSEQ, P]),
                            seq_mask[:, :].unsqueeze(2).broadcast_to([NDEC, NSEQ, P]), ALU.mult))
                        dve.wait_ge(d_dec_s, g + 1)
                        dve.tensor_tensor(d_m[0:NDEC], d_decay[0:NDEC],
                                          d_sc[0:NDEC, :].unsqueeze(1).broadcast_to([NDEC, HPG, NDEC]), ALU.mult)\
                            .then_inc(d_m_s, 1)
                        dve.wait_ge(d_off, g + 1)
                        n_st = steps.did(dve.tensor_tensor(
                            st[s].rearrange("p b (h d) -> p b h d", d=HD), st[s].rearrange("p b (h d) -> p b h d", d=HD),
                            exp_last[:, NCH:, bass.ds(4 * g, HPG)].unsqueeze(3)
                            .broadcast_to([P, NSEQ, HPG, HD]), ALU.mult))
                        dve.wait_ge(d_y, g + 1)
                        n = steps.did(dve.tensor_tensor(
                            d_tmp, py[:, 64:128].rearrange("p (j n) -> p j n", j=2), d_e, ALU.mult))
                        steps.need(n)
                        n = steps.did(dve.tensor_tensor(
                            d_tmp, d_tmp, py[:, 0:64].rearrange("p (j n) -> p j n", j=2), ALU.add))
                        steps.need(n)
                        for j in range(2):
                            n = steps.did(dve.scalar_tensor_tensor(
                                d_tmp[:, j, :], dec_xbc[:, bass.ds(g, 1), j, :].rearrange("p a n -> p (a n)"),
                                par1("d_skip", 2 * g + j), d_tmp[:, j, :], ALU.mult, ALU.add))
                        steps.need(n)
                        dve.wait_ge(y_in[s], 16 * turn + 16)
                        dve.tensor_tensor(y_cur[s][:, :, SEQ:T], d_tmp,
                                          dec_z[:, bass.ds(g, 1), :, :].rearrange("p a j n -> p (a j) n"), ALU.mult)\
                            .then_inc(d_ycur, 1)
                        steps.need(n_st)
                        for r, bank in enumerate((ph, ps, pt, ph)):
                            if r == 3:
                                dve.wait_ge(d_sq_s, g + 1)
                                dve.tensor_tensor(d_ssum, d_sq[:, 0, :], d_sq[:, 1, :], ALU.add)\
                                    .then_inc(d_ssum_s, 1)
                                dve.wait_ge(d_r3, g + 1)
                            v = st[s][:, 2 * r:2 * r + 2, :].rearrange("p b n -> p (b n)")
                            dve.tensor_tensor(v, v, bank[:, :], ALU.add).then_inc(d_add if r < 3 else st_ready, 1)
                        dve.wait_ge(d_rstd_s, g + 1)
                        for j in range(2):
                            dve.scalar_tensor_tensor(d_yn[:, j, :], y_cur[s][:, j, :], par1("norm_g", 2 * g + j),
                                                     d_rstd, ALU.mult, ALU.mult).then_inc(d_yn_s, 1)
                        for j in range(2):
                            dve.wait_ge(yn_hi_s, 2 * g + j + 1)
                            k = 4 * i + 2 * s + j
                            dve.tensor_tensor(rb_lo[:, bass.ds(k, 1), :].rearrange("p a n -> p (a n)"), d_yn[:, j, :],
                                              fr(rb_hi[:, bass.ds(k, 1), :].rearrange("p a n -> p (a n)")),
                                              ALU.subtract).then_inc(yn_ready, 1)
                steps.leave(2)
                if q == 0:
                    with dve.Fori(0, 2) as i:
                        for s in range(2):
                            lo_next(B_HALF // 2 + 2 + i, s)

            def b_add(i):
                for m in range(2):
                    dve.wait_ge(tile_done, 2 * (B_HALF + 12 + i) + m + 1)
                    v = halves(b_sum[:, 2 * i + m, :])
                    dve.scalar_tensor_tensor(v, main(m), 0.5, v, ALU.mult, ALU.add).then_inc(tile_free[m], 1)

            lo_next(B_HALF // 2 + 6, 0)
            dve.wait_ge(l_mean_s, 1)
            dve.wait_ge(cc_in, 32)

            def square_sum(m):
                dve.wait_ge(l_sq_s, m + 1)
                if m == 0:
                    ins = dve.tensor_copy(l_ssum, l_sq[:, 0, :])
                else:
                    dve.wait_ge(l_ssum_s, m)
                    ins = dve.tensor_tensor(l_ssum, l_ssum, l_sq[:, m % 2, :], ALU.add)
                ins.then_inc(l_ssum_s, 1)

            for m in range(KT):
                dve.tensor_tensor(xc[:, m, :], xc[:, m, :], l_mean, ALU.subtract).then_inc(l_xc, 1)
                if m >= 1:
                    square_sum(m - 1)
                if m == 3:
                    b_add(0)
                if m == 5:
                    lo_next(B_HALF // 2 + 6, 1)
            square_sum(KT - 1)
            b_add(1)
            lo_next(B_HALF // 2 + 7, 0)
            dve.wait_ge(l_rstd_s, 1)

            def silu_ln(m):
                dve.wait_ge(l_th_s, m + 1)
                dve.scalar_tensor_tensor(xc[:, m, :], l_th[:, m % 2, :], 1.0, l_a[:, m % 2, :], ALU.add, ALU.mult)\
                    .then_inc(l_sil, 1)

            def cc_low(m):
                dve.wait_ge(cc_hi_s, m + 1)
                dve.tensor_tensor(ra_lo[:, m, :], xc[:, m, :], fr(ra_hi[:, m, :]), ALU.subtract)\
                    .then_inc(cc_ready2, 1)

            for m in range(KT):
                dve.wait_ge(l_xc, KT)
                dve.tensor_tensor(xc[:, m, :], xc[:, m, :], l_rstd, ALU.mult).then_inc(l_t, 1)
                if m >= 1:
                    silu_ln(m - 1)
                if m >= 2:
                    cc_low(m - 2)
                if m == 3:
                    b_add(2)
                if m == 5:
                    lo_next(B_HALF // 2 + 7, 1)
            silu_ln(KT - 1)
            cc_low(KT - 2)
            cc_low(KT - 1)
            b_add(3)
            dve.wait_ge(tile_free[1], B_PW)

            def mg_low(m):
                dve.wait_ge(mg_hi, m + 1)
                dve.tensor_tensor(rb_lo[:, m, :], pw_m[:, m % 2, :], fr(rb_hi[:, m, :]), ALU.subtract)\
                    .then_inc(mg_ready, 1)

            for m in range(KT):
                if m % 2 == 0:
                    lo_next((B_PW + m // 2) // 2, (m // 2) % 2)
                dve.wait_ge(tile_free[m % 2], B_PW + m // 2 + 1)
                if m >= 2:
                    dve.wait_ge(mg_ready, m - 1)
                a, o = pw_a[:, m % 2, :], pw_m[:, m % 2, :]
                dve.scalar_tensor_tensor(a, g_in[:, m % 2, 0, :], 1.0, a, ALU.add, ALU.mult).then_inc(p_m, 1)
                dve.scalar_tensor_tensor(o, g_in[:, m % 2, 1, :], 1.0, b_sum[:, m, :], ALU.add, ALU.mult)\
                    .then_inc(p_m, 1)
                dve.wait_ge(p_m, 3 * m + 2)
                dve.tensor_tensor(o, o, a, ALU.add).then_inc(p_m, 1)
                if m >= 1:
                    mg_low(m - 1)
            mg_low(KT - 1)

            def h_low(m):
                dve.wait_ge(o_act, 2 * m + 2)
                if m == 0:
                    ins = dve.tensor_copy(o_ssum, o_sq[:, 0, :])
                else:
                    dve.wait_ge(o_sum_s, m)
                    ins = dve.tensor_tensor(o_ssum, o_ssum, o_sq[:, m % 2, :], ALU.add)
                ins.then_inc(o_sum_s, 1)
                dve.scalar_tensor_tensor(ra_lo[:, m, :], h_sb[:, m, :], par1("g_ffn", m), fr(ra_hi[:, m, :]),
                                         ALU.mult, ALU.subtract).then_inc(hn_ready, 1)

            for m in range(KT):
                if m % 2 == 0:
                    lo_next((B_WOUT + m // 2) // 2, (m // 2) % 2)
                dve.wait_ge(x_in2[m % 2], 16 * (m // 2) + 16)
                dve.wait_ge(tile_done, 2 * B_WOUT + m + 1)
                dve.tensor_tensor(halves(h_sb[:, m, :]), main(m), halves(x_in[:, m % 2, :]), ALU.add)\
                    .then_inc(tile_free[m % 2], 1)
                if m >= 1:
                    h_low(m - 1)
            h_low(KT - 1)
            dve.wait_ge(o_rstd_s, 1)

            def quarter(i, last):
                def hidden_low(n):
                    dve.wait_ge(f_hi, KT * i + n + 1)
                    dve.tensor_tensor(rb_lo[:, n, :], f_s[:, n % 2, :], fr(rb_hi[:, n, :]), ALU.subtract)\
                        .then_inc(f_ready, 1)

                for j in range(4):
                    lo_next(B_FFN // 2 + 4 * i + j // 2, j % 2)
                    for m in range(2):
                        n = 2 * j + m
                        dve.wait_ge(tile_free[m], B_FFN + 8 * i + j + 1)
                        dve.tensor_tensor(f_v[:, n % 2, :], f_r[:, n % 2, :], o_rstd, ALU.mult).then_inc(f_v_s, 1)
                        if n >= 1:
                            hidden_low(n - 1)
                hidden_low(KT - 1)
                for j in range(4):
                    if not last or j < 3:
                        lo_next(B_FFN // 2 + 4 * i + 2 + j // 2, j % 2)
                    for m in range(2):
                        n = 2 * j + m
                        dve.wait_ge(tile_done, 2 * B_FFN + 16 * i + 8 + n + 1)
                        v = halves(h_sb[:, n, :])
                        dve.tensor_tensor(v, v, main(m), ALU.add).then_inc(tile_free[m], 1)

            with dve.Fori(0, 3) as i:
                quarter(i, False)
            quarter(3, True)
            dve.wait_ge(z_rstd, 1)
            dve.wait_ge(tile_free[1], NBLOCKS)
            for m in range(KT):
                if m >= 2:
                    dve.wait_ge(out_st[m % 2], 16 * (m // 2))
                dve.scalar_tensor_tensor(o_y[:, m % 2, :], h_sb[:, m, :], par1("g_final", m), o_rstd, ALU.mult,
                                         ALU.mult).then_inc(z_y, 1)


K_GROUP = 77
K_DECODE = 16


def _cols(w, *ranges):
    b = np.concatenate([w[:, a:a + n] for a, n in ranges], axis=1)
    return b.reshape(KT, P, BW).transpose(1, 0, 2).reshape(P, KT * BW)


def _tiles(x, k):
    return x.T.reshape(k, P, -1).transpose(1, 0, 2).reshape(P, -1)


def kernel(**inputs):
    import concourse.bacc as bacc
    from concourse.bass_utils import run_bass_kernel_spmd

    a = {k: np.asarray(v) for k, v in inputs.items()}
    w_in, w_pw, w_so, w_o, w_up, w_dn = (a[n][0] for n in (
        "w_in", "conf_w_pw", "ssm_w_out", "w_out", "w_up", "w_down"))
    gate0, z0 = 2 * D_MODEL, 4 * D_MODEL
    xbc0 = z0 + 2 * D_MODEL
    dt0 = xbc0 + 4 * D_MODEL
    blocks = []
    for g in range(GROUPS):
        blocks += [_cols(w_in, (xbc0 + 256 * g, 256)),
                   _cols(w_in, (xbc0 + 2048 + P * g, P), (xbc0 + 3072 + P * g, P)),
                   _cols(w_in, (z0 + 256 * g, 256)),
                   _cols(w_in, (P * g, P), (D_MODEL + P * g, P))]
    for q in range(2):
        blocks += [_cols(w_in, (gate0 + P * g, P), (gate0 + D_MODEL + P * g, P)) for g in range(4 * q, 4 * q + 4)]
        blocks += [_cols(w_so[1024 * q:1024 * (q + 1)], (256 * i, 256)) for i in range(4)]
    blocks += [_cols(w_pw, (256 * i, 256)) for i in range(4)]
    blocks += [_cols(w_o, (256 * i, 256)) for i in range(4)]
    for q in range(4):
        blocks += [_cols(w_up, (1024 * q + 256 * i, 256)) for i in range(4)]
        blocks += [_cols(w_dn[1024 * q:1024 * (q + 1)], (256 * i, 256)) for i in range(4)]
    w_all = np.stack(blocks)
    w_dt = np.tile(w_in[:, dt0:dt0 + HEADS], (1, 4)).reshape(KT, P, P).transpose(1, 0, 2).reshape(P, KT * P)
    x_all = _tiles(np.concatenate([a["x_prompt"].reshape(SEQ, -1), a["x_sample"].reshape(NDEC, -1)]), KT)

    def xbc_order(v, n):
        xs = v[:2048].reshape(GROUPS, 2, P, n)
        bc = [v[s:s + 1024].reshape(GROUPS, 1, P, n) for s in (2048, 3072)]
        return np.concatenate([xs] + bc, axis=1).transpose(2, 0, 1, 3)

    def vec(v):
        return v.reshape(-1, P).T

    par = np.concatenate([
        vec(a["g_mix"][0]), a["conf_dw_w"][0].T.reshape(8, P, CK).transpose(1, 0, 2).reshape(P, -1),
        vec(a["conf_dw_b"][0]), vec(a["conf_ln_g"][0]), vec(a["conf_ln_b"][0]), vec(a["conf_b_pw"][0]),
        xbc_order(a["ssm_conv_w"][0].T, SK).reshape(P, -1),
        xbc_order(a["ssm_conv_b"][0].reshape(-1, 1), 1).reshape(P, -1),
        vec(np.repeat(a["ssm_d"][0], HD)), vec(a["ssm_norm_g"][0]), vec(a["g_ffn"][0]), vec(a["g_final"])], axis=1)
    dt_par = np.stack([np.tile(a["ssm_dt_bias"][0], 4), np.tile(a["ssm_a_log"][0], 4)], axis=1)
    conf_state = a["state_conf_conv"][0].transpose(2, 0, 1).reshape(GROUPS, P, NSEQ * CPRE)
    conv_state = xbc_order(a["state_ssm_conv"][0].transpose(2, 0, 1).reshape(4096, -1), NSEQ * SPRE)        .transpose(1, 0, 2, 3).reshape(GROUPS, P, -1)
    ssm_state = a["state_ssm"][0].reshape(NSEQ, GROUPS, 256, NST).transpose(1, 3, 0, 2).reshape(GROUPS, P, -1)

    nc = bacc.Bacc("TRN2", target_bir_lowering=False, num_devices=1)
    arrays, args = {}, []
    for name, v in [("x_all", x_all), ("w_all", w_all), ("w_dt", w_dt), ("par", par), ("dt_par", dt_par),
                    ("conf_state", conf_state), ("conv_state", conv_state), ("ssm_state", ssm_state)]:
        v = np.ascontiguousarray(v, dtype=np.float32)
        arrays[f"in_{name}"] = v
        args.append(nc.dram_tensor(f"in_{name}", v.shape, F32, kind="ExternalInput").ap())
    for name, shape in [("y", (P, KT * T)), ("conf", (GROUPS, P, CPRE * (NSEQ + 1))),
                        ("conv", (GROUPS, P, 4 * SPRE * (NSEQ + 1))), ("hp", (GROUPS, P, 256)),
                        ("hs", (GROUPS, P, NSEQ * 256))]:
        args.append(nc.dram_tensor(f"out_{name}", shape, F32, kind="ExternalOutput").ap())
    hybrid_layer(nc, *args)
    r = run_bass_kernel_spmd(nc, [arrays], core_ids=[0]).results[0]

    y = r["out_y"].reshape(P, KT, T).transpose(2, 1, 0).reshape(T, D_MODEL)
    conf = r["out_conf"].reshape(D_MODEL, NSEQ + 1, CPRE).transpose(1, 2, 0)
    conv = r["out_conv"].reshape(GROUPS, P, 4, NSEQ + 1, SPRE)
    conv = np.concatenate([conv[:, :, 0:2].transpose(0, 2, 1, 3, 4).reshape(2048, NSEQ + 1, SPRE),
                           conv[:, :, 2].reshape(1024, NSEQ + 1, SPRE),
                           conv[:, :, 3].reshape(1024, NSEQ + 1, SPRE)]).transpose(1, 2, 0)
    hp = r["out_hp"].reshape(GROUPS, NST, HPG, HD).transpose(0, 2, 3, 1).reshape(1, 1, HEADS, HD, NST)
    hs = r["out_hs"].reshape(GROUPS, NST, NSEQ, HPG, HD).transpose(2, 0, 3, 4, 1).reshape(1, NSEQ, HEADS, HD, NST)
    return (y[:SEQ].reshape(1, SEQ, D_MODEL), y[SEQ:].reshape(NSEQ, TDEC, D_MODEL),
            conf[None, 0:1], conv[None, 0:1], hp, conf[None, 1:], conv[None, 1:], hs)
```

```python
from contextlib import ExitStack

import numpy as np

import concourse.bass as bass
from concourse import mybir

F32 = mybir.dt.float32
F32R = mybir.dt.float32r
BF16 = mybir.dt.bfloat16
ALU = mybir.AluOpType
ACT = mybir.ActivationFunctionType
AX = mybir.AxisListType

P = 128
D_MODEL = 1024
KT = D_MODEL // P
SEQ, NSEQ, TDEC = 512, 8, 4
NDEC = NSEQ * TDEC
T = SEQ + NDEC
H2 = T // 2
GROUPS, HPG, HD, NST = 8, 4, 64, 128
HEADS = GROUPS * HPG
CK, SK = 31, 4
CPRE, SPRE = CK - 1, SK - 1
CHUNK = 128
NCH = SEQ // CHUNK
EPS = 1e-6
BW = 256
NBLOCKS = 88
XW = SPRE + SEQ + NSEQ * (SPRE + TDEC)
CW = XW - SPRE
BIG = -1.0e30
B_GROUP, B_GATES, B_SSM, B_PW, B_WOUT, B_FFN = 0, 32, 40, 48, 52, 56
PARAMS = {}
_at = 0
for _name, _n in [("g_mix", 8), ("conf_w", 8 * CK), ("conf_b", 8), ("ln_g", 8), ("ln_b", 8), ("b_pw", 8),
                  ("ssm_w", 32 * SK), ("ssm_b", 32), ("d_skip", 16), ("norm_g", 16), ("g_ffn", 8),
                  ("g_final", 8)]:
    PARAMS[_name] = (_at, _n)
    _at += _n
NPAR = _at


class Steps:

    def __init__(self, eng, sem):
        self.eng, self.sem, self.base, self.n = eng, sem, 0, 0

    def did(self, ins):
        ins.then_inc(self.sem, 1)
        self.n += 1
        return self.n

    def need(self, step):
        self.eng.wait_ge(self.sem, self.base + step)

    def enter(self, i, per):
        self.outer, self.per = self.base + self.n, per
        self.base, self.n = self.outer + i * per, 0

    def leave(self, rounds):
        assert self.n == self.per, f"{self.sem}: the body makes {self.n} steps, {self.per} given"
        self.base, self.n = self.outer + rounds * self.per, 0


def hybrid_layer(nc, x_all, w_all, w_dt, par, dt_par, conf_state, conv_state, ssm_state,
                 y_out, conf_out, conv_out, hp_out, hs_out):
    ctx = ExitStack()
    with ctx:
        def sb(name, shape, dt=F32):
            return ctx.enter_context(nc.sbuf_tensor(name, shape, dt))

        def sem(name):
            return ctx.enter_context(nc.semaphore(name))

        y_dram = nc.dram_tensor("y_scratch", (GROUPS, P, 2, T), F32, kind="Internal").ap()
        cc_dram = nc.dram_tensor("cc_scratch", (GROUPS, P, T), F32, kind="Internal").ap()
        gate_dram = nc.dram_tensor("gate_scratch", (GROUPS, P, 2, T), F32, kind="Internal").ap()

        w_raw = sb("w_raw", [P, 2, KT * BW])
        w_hi = sb("w_hi", [P, 2, KT * BW], F32R)
        w_lo = sb("w_lo", [P, 2, KT * BW], F32R)
        ra_hi = sb("ra_hi", [P, KT, T], F32R)
        ra_lo = sb("ra_lo", [P, KT, T], F32R)
        with nc.sbuf_tensor("dec", [P, 2 * KT * T], F32) as dec:
            pass
        rb_hi = sb("rb_hi", [P, KT, T], F32R)
        rb_lo = sb("rb_lo", [P, KT, T], F32R)
        ident = sb("ident", [P, P])
        ones = sb("ones", [P, P])
        ident_bf = sb("ident_bf", [P, P], BF16)
        mask_bf = sb("mask_bf", [P, P], BF16)
        mask_dec = sb("mask_dec", [NDEC, NDEC], BF16)
        seq_mask = sb("seq_mask", [NDEC, NSEQ])
        sel = sb("sel", [96, HEADS, HD], BF16)
        last_sel = sb("last_sel", [NDEC, NDEC])
        acum_bf = sb("acum_bf", [96, T], BF16)
        dt_nat = sb("dt_nat", [P, NCH + 1, HEADS])
        acum_nat = sb("acum_nat", [P, NCH + 1, HEADS])
        nacum_nat = sb("nacum_nat", [P, NCH + 1, HEADS])
        w_nat = sb("w_nat", [P, NCH + 1, HEADS])
        dtw_nat = sb("dtw_nat", [P, NCH + 1, HEADS])
        exp_last = sb("exp_last", [P, NCH + NSEQ, HEADS])
        pars = sb("pars", [P, NPAR])
        dt_pars = sb("dt_pars", [P, 2])
        a_neg = sb("a_neg", [P, 1])
        eps = sb("eps", [P, 1])
        cc_sum = sb("cc_sum", [P, T])
        d_cur = sb("d_cur", [P, 4, NDEC])[:, :, :]
        d_z = sb("d_z", [P, 2, NDEC])[:, :, :]
        ARENA = 17920
        arena = sb("arena", [P, ARENA])

        def views(*fields, at=0, space=arena, size=ARENA):
            out = []
            for shape in fields:
                n = int(np.prod(shape))
                v = space[:, at:at + n]
                if len(shape) == 2:
                    v = v.rearrange("p (a b) -> p a b", b=shape[1])
                elif len(shape) == 3:
                    v = v.rearrange("p (a b c) -> p a b c", b=shape[1], c=shape[2])
                out.append(v)
                at += n
            assert at <= size, at
            return out, at

        (raw, acc, sil, zs, zh, gx, gd, conv_a, conv_b, ccs, cstate, cout, sstate, sout), ssd_at = views(
            (4, XW), (4, XW), (4, XW), (2, T), (2, T), (CPRE + SEQ,),
            (NSEQ, CPRE + TDEC), (SEQ,), (SEQ,), (T,), (NSEQ, CPRE), (CPRE * (NSEQ + 1),),
            (4, NSEQ, SPRE), (4, SPRE * (NSEQ + 1)))
        raw_d, sil_d = (x[:, :, SPRE + SEQ:XW].rearrange("p a (b t) -> p a b t", b=NSEQ)
                        for x in (raw, sil))
        sil_d = sil_d[:, :, :, 0:TDEC]
        (h_t, xdt, wxdt, b_nat, scores, decay, m_t, y_tmp, e_acc, y_sb), ssd_end = views(
            (HPG * HD,), (HPG * HD,), (HPG * HD,), (P,), (P,), (HPG, P), (HPG, P), (2, P), (2, SEQ), (2, T),
            at=ssd_at)
        d_ssum = e_acc.rearrange("p j n -> p (j n)")[:, 0:T]
        (st, d_sq, d_xdt, d_wxdt, d_bn, d_sc, d_decay, d_m, d_e, d_tmp), _ = views(
            (NSEQ, 256), (2, T), (256,), (256,), (P,), (NDEC,), (HPG, NDEC), (HPG, NDEC), (2, NDEC), (2, NDEC),
            space=dec, size=2 * KT * T, at=KT * T)
        (d_bm, d_rstd), _ = views((NSEQ, P), (T,), space=dec, size=KT * T)
        d_yn = d_sq
        (x_t, sq0, rstd0, xn0), norm_end = views((KT, T), (2, T), (T,), (2, T))
        assert norm_end + 1024 <= ssd_at
        wdt_raw = arena[:, norm_end:norm_end + 1024]
        (dt_v, dt_e, dt_z, dt_z2, dt_p, dt_r, dt_t, scan_keep), _ = views(*[(T,)] * 8, at=ssd_at)
        (gates_sb,), _ = views((2, T))
        (y_ld,), b_at = views((2, 2 * T), at=4 * XW)
        y_ld = y_ld.rearrange("p a (j t) -> p a j t", j=2)
        (b_sum, xc, l_sq, l_mean, l_ssum, l_rstd, pw_m), _ = views(
            (KT, T), (KT, T), (2, T), (T,), (T,), (T,), (2, T), at=b_at)
        g_in, pw_a = y_ld, l_sq
        (h_sb, x_in, o_sq, o_ssum, o_rstd, f_r, f_v, f_s, o_y), _ = views(
            (KT, T), (2, T), (2, T), (T,), (T,), (2, T), (2, T), (2, T), (2, T))

        psum = [ctx.enter_context(nc.psum_tensor(f"main{s}", [P, 2, 512], F32)) for s in range(2)]
        pt = ctx.enter_context(nc.psum_tensor("pt", [P, 512], F32))
        ps = ctx.enter_context(nc.psum_tensor("ps", [P, 512], F32))
        py = ctx.enter_context(nc.psum_tensor("py", [P, 512], F32))
        ph = ctx.enter_context(nc.psum_tensor("ph", [P, 512], F32))

        def main(t):
            return psum[t % 2][:, :, 0:H2]

        def halves(ap):
            return ap.rearrange("p (a b) -> p a b", a=2)

        def par1(name, i, n=1):
            at, _ = PARAMS[name]
            return pars[:, bass.ds(at + i, n)]

        def fr(ap):
            return ap.bitcast(F32)

        w_in = [sem(f"w_in{s}") for s in range(2)]
        w_hi_s, w_lo_s, w_used = sem("w_hi_done"), sem("w_lo_done"), sem("w_used")
        tile_done = sem("tile_done")
        tile_free = [sem(f"tile_free{s}") for s in range(2)]
        const_s, pool_c = sem("const_s"), sem("pool_c")
        x_in_s = [sem(f"x_in_s{i}") for i in range(2)]
        par_s, wdt_in = sem("par_s"), sem("wdt_in")
        act_c, dve_c = sem("act_c"), sem("dve_c")
        n_sq, n_sum, n_rstd, n_xn, u_hi_s, u_ready = (sem(n) for n in (
            "n_sq", "n_sum", "n_rstd", "n_xn", "u_hi_s", "u_ready"))
        wdt_hi_s, wdt_ready, dt_psum, dt_act, dt_dve, acum_ready, nat_t, nat_copied, nat_b, nat_diff, nat_ready = (
            sem(n) for n in ("wdt_hi_s", "wdt_ready", "dt_psum", "dt_act", "dt_dve", "acum_ready", "nat_t",
                             "nat_copied", "nat_b", "nat_diff", "nat_ready"))
        raw_ready, conv4_s, sil_th, sil_ready, dec_saved = (sem(n) for n in (
            "raw_ready", "conv4_s", "sil_th", "sil_ready", "dec_saved"))
        z_act, z_ready, glu_act, glu_ready, cc_ready = (sem(n) for n in (
            "z_act", "z_ready", "glu_act", "glu_ready", "cc_ready"))
        e_psum, e_ready, pt_done, ps_done, decay_ready, m_ready, ys_done, h_ready, y_done = (sem(n) for n in (
            "e_psum", "e_ready", "pt_done", "ps_done", "decay_ready", "m_ready", "ys_done", "h_ready", "y_done"))
        cstate_in, y_ln_s, sstate_in, sstate_used, cpre_ready, cc_added = (sem(n) for n in (
            "cstate_in", "y_ln_s", "sstate_in", "sstate_used", "cpre_ready", "cc_added"))
        cout_copied, sout_copied, cout_st, sout_st, ssd_st, cc_st = (sem(n) for n in (
            "cout_copied", "sout_copied", "cout_st", "sout_st", "ssd_st", "cc_st"))
        cc_free, ssd_free, o_sum_s, par_ready, conv01_s, xb_ready = (sem(n) for n in (
            "cc_free", "ssd_free", "o_sum_s", "par_ready", "conv01_s", "xb_ready"))
        f_sq_s, pool_passed = sem("f_sq_s"), sem("pool_passed")
        nat_exp = sem("nat_exp")
        gates_st = [sem(f"gates_st{m}") for m in range(2)]
        y_in = [sem(f"y_in{s}") for s in range(2)]
        d_off, d_pt, d_ps, d_bn_s, d_dec_s, d_m_s, d_y, d_add, d_r3, d_ycur, d_sq_s, d_ssum_s, d_stat, \
            d_rstd_s, d_yn_s, yn_st, ys_hi, ys_ready, st_in, st_ready, st_st = (sem(n) for n in (
                "d_off", "d_pt", "d_ps", "d_bn_s", "d_dec_s", "d_m_s", "d_y", "d_add", "d_r3", "d_ycur",
                "d_sq_s", "d_ssum_s", "d_stat", "d_rstd_s", "d_yn_s", "yn_st", "ys_hi", "ys_ready", "st_in",
                "st_ready", "st_st"))
        cc_in, l_stat, l_mean_s, l_xc, l_sq_s, l_ssum_s, l_stat2, l_rstd_s, l_t, l_th_s, l_sil, cc_hi_s, cc_ready2 = (
            sem(n) for n in ("cc_in", "l_stat", "l_mean_s", "l_xc", "l_sq_s", "l_ssum_s", "l_stat2", "l_rstd_s",
                             "l_t", "l_th_s", "l_sil", "cc_hi_s", "cc_split"))
        b_ready = sem("b_ready")
        g_in_s = [sem(f"g_in_s{s}") for s in range(2)]
        p_act, p_m, mg_hi, mg_ready = sem("p_act"), sem("p_m"), sem("mg_hi"), sem("mg_ready")
        x_in2 = [sem(f"x_in2_{s}") for s in range(2)]
        o_h, o_act, hn_ready, o_stat, o_rstd_s = sem("o_h"), sem("o_act"), sem("hn_ready"), sem("o_stat"), sem("o_rstd_s")
        f_act, f_v_s, f_hi, f_ready = sem("f_act"), sem("f_v_s"), sem("f_hi"), sem("f_ready")
        z_sq, z_stat, z_rstd, z_y = sem("z_sq"), sem("z_stat"), sem("z_rstd"), sem("z_y")
        out_st = [sem(f"out_st{s}") for s in range(2)]

        block = ctx.enter_context(nc.Block())

        @block.sync
        def _(sp):
            half = KT // 2
            for i in range(2):
                sp.dma_start(x_t[:, i * half:(i + 1) * half, :],
                             x_all[:, i * half * T:(i + 1) * half * T]
                             .rearrange("p (k t) -> p k t", t=T)).then_inc(x_in_s[i], 16)
                if i == 0:
                    sp.dma_start(pars[:, :], par).then_inc(par_s, 16)
                    sp.dma_start(dt_pars[:, :], dt_par).then_inc(par_s, 16)
            sp.dma_start(w_raw[:, 0, :], w_all[0]).then_inc(w_in[0], 16)
            sp.dma_start(wdt_raw, w_dt).then_inc(wdt_in, 16)
            sp.dma_start(w_raw[:, 1, :], w_all[1]).then_inc(w_in[1], 16)
            with sp.Fori(1, NBLOCKS // 2) as i:
                for s in range(2):
                    sp.wait_ge(w_lo_s, 2 * i + (s - 1))
                    sp.dma_start(w_raw[:, s, :], w_all[bass.ds(2 * i + s, 1), :, :]
                                 .rearrange("a p n -> p (a n)")).then_inc(w_in[s], 16)

        @block.gpsimd
        def _(pool):
            st_c = Steps(pool, pool_c)
            st_c.did(pool.memset(ident[:, :], 0.0))
            st_c.did(pool.memset(mask_bf[:, :], 0.0))
            st_c.did(pool.memset(mask_dec[:, :], 0.0))
            st_c.did(pool.memset(seq_mask[:, :], 1.0))
            pool.memset(ones[:, :], 1.0).then_inc(const_s, 1)
            pool.memset(eps[:, :], EPS).then_inc(const_s, 1)
            st_c.did(pool.memset(scan_keep, 1.0))
            st_c.need(5)
            n = st_c.did(pool.memset(scan_keep[:, 0:SEQ:CHUNK], 0.0))
            pool.memset(scan_keep[:, SEQ:T:TDEC], 0.0).then_inc(const_s, 1)
            n = st_c.did(pool.affine_select(out=ident[:, :], in_=ident[:, :], compare_op=ALU.not_equal, fill=1.0,
                                            base=0, pattern=[[-1, P]], channel_multiplier=1))
            st_c.did(pool.affine_select(out=mask_bf[:, :], in_=mask_bf[:, :], compare_op=ALU.is_ge, fill=BIG,
                                        base=0, pattern=[[1, P]], channel_multiplier=-1))
            st_c.need(n)
            m = st_c.did(pool.tensor_copy(ident_bf[:, :], ident[:, :]))
            dec3 = mask_dec[:, :].rearrange("s (b t) -> s b t", t=TDEC)
            m = st_c.did(pool.affine_select(out=mask_dec[:, :], in_=mask_dec[:, :], compare_op=ALU.is_ge, fill=BIG,
                                            base=0, pattern=[[1, NDEC]], channel_multiplier=-1))
            st_c.need(m)
            m = st_c.did(pool.affine_select(out=dec3, in_=dec3, compare_op=ALU.is_ge, fill=BIG, base=TDEC - 1,
                                            pattern=[[TDEC, NSEQ], [0, TDEC]], channel_multiplier=-1))
            st_c.need(m)
            st_c.did(pool.affine_select(out=dec3, in_=dec3, compare_op=ALU.is_ge, fill=BIG, base=0,
                                        pattern=[[-TDEC, NSEQ], [0, TDEC]], channel_multiplier=1))
            m = st_c.did(pool.affine_select(out=seq_mask[:, :], in_=seq_mask[:, :], compare_op=ALU.is_ge, fill=0.0,
                                            base=TDEC - 1, pattern=[[TDEC, NSEQ]], channel_multiplier=-1))
            st_c.need(m)
            st_c.did(pool.affine_select(out=seq_mask[:, :], in_=seq_mask[:, :], compare_op=ALU.is_ge, fill=0.0,
                                        base=0, pattern=[[-TDEC, NSEQ]], channel_multiplier=1))
            st_c.did(pool.tensor_copy(last_sel[:, :].rearrange("s (b t) -> s b t", t=TDEC),
                                      ident[0:NDEC, TDEC - 1:NDEC:TDEC].unsqueeze(2)
                                      .broadcast_to([NDEC, NSEQ, TDEC])))
            m = st_c.did(pool.memset(sel[:, :, :], 0.0))
            for part in range(3):
                st_c.need(m)
                m = st_c.did(pool.affine_select(out=sel[:, :, :], in_=sel[:, :, :], compare_op=ALU.not_equal,
                                                fill=1.0, base=-HEADS * part, pattern=[[-1, HEADS], [0, HD]],
                                                channel_multiplier=1))
            pool.memset(cc_sum[:, :], 0.0).then_inc(const_s, 1)
            pool.wait_ge(u_ready, KT)
            pool.memset(raw[:, :, 0:SPRE], 0.0).then_inc(const_s, 1)
            pool.memset(gx[:, 0:CPRE], 0.0).then_inc(const_s, 1)

            def held(s, value):
                pool.wait_ge(s, value)
                pool.sem_inc(pool_passed, 1)

            def load_conv_state(g):
                pool.dma_start(sstate.rearrange("p a b c -> p (a b c)"),
                               conv_state[bass.ds(g, 1), :, :].rearrange("a p n -> p (a n)"))\
                    .then_inc(sstate_in, 16)

            def load_conf_state(g):
                pool.dma_start(cstate.rearrange("p a b -> p (a b)"),
                               conf_state[bass.ds(g, 1), :, :].rearrange("a p n -> p (a n)"))\
                    .then_inc(cstate_in, 16)

            def conf_prefix(g):
                held(cstate_in, 16 * g + 16)
                pool.tensor_copy(gd[:, :, 0:CPRE], cstate).then_inc(cpre_ready, 1)
                held(cpre_ready, g + 1)

            def save_conv_state(g):
                held(raw_ready, 4 * g + 4)
                pool.tensor_copy(sout[:, :, 0:SPRE], raw[:, :, SEQ:SEQ + SPRE])
                pool.tensor_copy(sout[:, :, SPRE:].rearrange("p a (b c) -> p a b c", c=SPRE),
                                 raw_d[:, :, :, TDEC:TDEC + SPRE]).then_inc(sout_copied, 1)
                pool.wait_ge(sout_copied, g + 1)
                pool.dma_start(conv_out[bass.ds(g, 1), :, :].rearrange("a p n -> p (a n)"),
                               sout.rearrange("p a b -> p (a b)")).then_inc(sout_st, 16)

            def save_conf_state(g):
                held(glu_ready, g + 1)
                pool.tensor_copy(cout[:, 0:CPRE], gx[:, SEQ:SEQ + CPRE])
                pool.tensor_copy(cout[:, CPRE:].rearrange("p (b c) -> p b c", c=CPRE),
                                 gd[:, :, TDEC:TDEC + CPRE]).then_inc(cout_copied, 1)
                pool.wait_ge(cout_copied, g + 1)
                pool.dma_start(conf_out[bass.ds(g, 1), :, :].rearrange("a p n -> p (a n)"), cout)\
                    .then_inc(cout_st, 16)

            def add_cc(p):
                pool.wait_ge(cc_ready, p + 1)
                pool.dma_start(cc_dram[bass.ds(p, 1), :, :].rearrange("a p n -> p (a n)"), ccs).then_inc(cc_st, 16)
                pool.tensor_tensor(cc_sum[:, :], cc_sum[:, :], ccs, ALU.add).then_inc(cc_added, 1)
                pool.wait_ge(cc_added, p + 1)
                pool.wait_ge(cc_st, 16 * p + 16)
                pool.sem_inc(cc_free, 1)

            def load_states(p):
                pool.dma_start(st.rearrange("p b n -> p (b n)"),
                               ssm_state[bass.ds(p, 1), :, :].rearrange("a p n -> p (a n)")).then_inc(st_in, 16)

            def store_hp(p):
                pool.wait_ge(y_done, p + 1)
                pool.dma_start(hp_out[bass.ds(p, 1), :, :].rearrange("a p n -> p (a n)"), h_t).then_inc(ssd_st, 16)

            def store_states(p):
                pool.wait_ge(st_ready, p + 1)
                pool.dma_start(hs_out[bass.ds(p, 1), :, :].rearrange("a p n -> p (a n)"),
                               st.rearrange("p b n -> p (b n)")).then_inc(st_st, 16)

            def store_yn(p):
                pool.wait_ge(d_yn_s, p + 1)
                pool.dma_start(y_dram[bass.ds(p, 1), :, :, :].rearrange("a p j n -> p (a j) n"), d_yn)\
                    .then_inc(yn_st, 16)

            pool.sem_inc(cc_free, 1)
            pool.sem_inc(ssd_free, 1)
            load_conv_state(0)
            load_conf_state(0)
            pool.wait_ge(dt_psum, 1)
            load_states(0)
            conf_prefix(0)
            save_conv_state(0)

            def conv_out_of(p):
                add_cc(p)
                conf_prefix(p + 1)

            def states_out_of(p):
                store_states(p)
                store_yn(p)
                pool.wait_ge(st_st, 16 * (p + 1))
                pool.wait_ge(yn_st, 16 * (p + 1))
                load_states(p + 1)

            def saves(g):
                save_conf_state(g - 1)
                pool.wait_ge(sout_st, 16 * g)
                store_hp(g - 1)
                save_conv_state(g)
                pool.wait_ge(ssd_st, 16 * g)
                pool.sem_inc(ssd_free, 1)

            load_conv_state(1)
            load_conf_state(1)
            saves(1)
            with pool.Fori(2, GROUPS) as g:
                load_conv_state(g)
                conv_out_of(g - 2)
                load_conf_state(g)
                states_out_of(g - 2)
                pool.wait_ge(cout_st, 16 * (g - 1))
                saves(g)
            conv_out_of(GROUPS - 2)
            states_out_of(GROUPS - 2)
            pool.wait_ge(cout_st, 16 * (GROUPS - 1))
            save_conf_state(GROUPS - 1)

            def store_gates(i):
                for m in range(2):
                    pool.wait_ge(tile_free[m], B_GATES + i + 1)
                    pool.dma_start(gate_dram[i][:, m, :], gates_sb[:, m, :]).then_inc(gates_st[m], 16)

            def load_yn(i):
                pool.dma_start(y_ld[:, i % 2, :, :], y_dram[i]).then_inc(y_in[i % 2], 16)

            for i in range(3):
                store_gates(i)
            store_hp(GROUPS - 1)
            store_gates(3)
            store_states(GROUPS - 1)
            pool.wait_ge(sil_ready, 4 * GROUPS)
            load_yn(0)
            load_yn(1)
            store_yn(GROUPS - 1)
            add_cc(GROUPS - 1)
            pool.wait_ge(yn_st, 16 * GROUPS)
            for i in range(2, GROUPS):
                if i + 2 < GROUPS:
                    store_gates(i + 2)
                pool.wait_ge(ys_ready, 2 * (i - 1))
                load_yn(i)
            for m in range(2):
                pool.wait_ge(gates_st[m], 16 * GROUPS)
            for s_out, n in ((ssd_st, 16), (st_st, 16), (cc_st, 16), (cout_st, 16), (sout_st, 16)):
                pool.wait_ge(s_out, n * GROUPS)

            for i in range(2):
                pool.dma_start(xc[:, 4 * i:4 * i + 4, :], cc_dram[4 * i:4 * i + 4].rearrange("a p n -> p a n"))\
                    .then_inc(cc_in, 16)
            pool.wait_ge(cc_in, 32)
            pool.wait_ge(ys_ready, 2 * GROUPS)
            for m in range(KT):
                if m >= 2:
                    pool.wait_ge(p_m, 3 * (m - 1))
                pool.dma_start(g_in[:, m % 2, :, :], gate_dram[m]).then_inc(g_in_s[m % 2], 16)
            pool.wait_ge(p_m, 3 * KT)
            for m in range(KT):
                if m >= 2:
                    pool.wait_ge(tile_free[m % 2], B_WOUT + (m - 2) // 2 + 1)
                pool.dma_start(x_in[:, m % 2, :], x_all[:, m * T:(m + 1) * T]).then_inc(x_in2[m % 2], 16)
            for m in range(KT):
                pool.wait_ge(z_y, m + 1)
                pool.dma_start(y_out[:, m * T:(m + 1) * T], o_y[:, m % 2, :]).then_inc(out_st[m % 2], 16)
            for s in range(2):
                pool.wait_ge(out_st[s], 16 * KT // 2)

        @block.tensor
        def _(pe):
            def fill(b, rhs_hi, rhs_lo, t0, m0=0, m1=2):
                bs, be, count = b
                for m in range(m0, m1):
                    t = t0 + m
                    if m == 0:
                        pe.wait_ge(w_lo_s, be + 1)
                    if count(t) is not None:
                        pe.wait_ge(tile_free[t % 2], count(t))
                    for hf in range(2):
                        for k in range(KT):
                            at = k * BW + m * P
                            for j, (w, x) in enumerate(((w_hi, rhs_hi), (w_hi, rhs_lo), (w_lo, rhs_hi))):
                                last = pe.matmul(psum[t % 2][:, hf, 0:H2], w[:, bs, at:at + P],
                                                 x[:, k, hf * H2:(hf + 1) * H2],
                                                 start=(k == 0 and j == 0), stop=(k == KT - 1 and j == 2))
                    last.then_inc(tile_done, 1)

            def blk(slot, b):
                return slot, b, (lambda t: b) if not (isinstance(b, int) and b == 0) else (lambda t: None)

            pe.wait_ge(const_s, 1)
            for k in range(KT):
                pe.wait_ge(n_sq, k + 1)
                for hf in range(2):
                    last = pe.matmul(psum[0][:, hf, 0:H2], ones[:, :], sq0[:, k % 2, hf * H2:(hf + 1) * H2],
                                     start=(k == 0), stop=(k == KT - 1))
                last.then_inc(n_sum, 1)
            pe.wait_ge(wdt_ready, 1)
            pe.wait_ge(n_rstd, 1)
            wdt_hi, wdt_lo = (x[:, :, :].rearrange("p k t -> p (k t)") for x in (rb_hi, rb_lo))
            for k in range(KT):
                pe.wait_ge(u_ready, k + 1)
                for hf in range(2):
                    for j, (w, x) in enumerate(((wdt_hi, ra_hi), (wdt_hi, ra_lo), (wdt_lo, ra_hi))):
                        last = pe.matmul(psum[0][:, hf, 0:H2], w[:, k * P:(k + 1) * P],
                                         x[:, k, hf * H2:(hf + 1) * H2],
                                         start=(k == 0 and j == 0), stop=(k == KT - 1 and j == 2))
            last.then_inc(dt_psum, 1)

            def pick_head(p, h):
                return sel[:, bass.ds(4 * p + h, 1), 0:1].rearrange("r a b -> r (a b)").broadcast_to([96, P])

            def pick_pair(p, j):
                return sel[:, bass.ds(4 * p + 2 * j, 2), :].rearrange("r a b -> r (a b)")

            def ssd_e(p):
                pe.wait_ge(glu_ready, p + 1)
                for j, bank in enumerate((ph, py)):
                    pe.matmul(bank[:, :], pick_pair(p, j), acum_bf[:, 0:SEQ],
                              start=True, stop=True).then_inc(e_psum, 1)

            def ssd_1(c, p):
                cs = slice(c * CHUNK, (c + 1) * CHUNK)
                if c == 0:
                    pe.wait_ge(sil_ready, 4 * p + 4)
                    pe.wait_ge(dec_saved, p + 1)
                    pe.wait_ge(nat_ready, 1)
                for j in range(3):
                    pe.transpose(pt[:, j * P:(j + 1) * P], sil[:, j, cs], ident[:, :])
                pe.matmul(pt[:, 3 * P:4 * P], sil[:, 2, cs], sil[:, 3, cs], start=True, stop=True)\
                    .then_inc(pt_done, 1)
                for h in range(HPG):
                    pe.matmul(ps[:, h * P:(h + 1) * P], pick_head(p, h), acum_bf[:, cs],
                              start=(h == 0), stop=False, skip_group_check=True)
                pe.matmul(ps[:, :], ident_bf[:, :], mask_bf[:, :].unsqueeze(1).broadcast_to([P, HPG, P]),
                          start=False, stop=True, skip_group_check=True).then_inc(ps_done, 1)

            def ssd_2(c, p):
                cs = slice(c * CHUNK, (c + 1) * CHUNK)
                if c == 0:
                    pe.wait_ge(e_ready, p + 1)
                pe.wait_ge(m_ready, NCH * p + c + 1)
                pe.wait_ge(xb_ready, NCH * p + c + 1)
                if c:
                    pe.wait_ge(h_ready, NCH * p + c)
                for h in range(HPG):
                    pe.matmul(py[(h % 2) * HD:(h % 2 + 1) * HD, (h // 2) * P:(h // 2 + 1) * P],
                              xdt[:, h * HD:(h + 1) * HD], m_t[:, h, :], start=True, stop=True,
                              skip_group_check=True)
                if c:
                    for j in range(2):
                        pe.matmul(py[:, 256 + j * P:256 + (j + 1) * P], h_t[:, j * P:(j + 1) * P], sil[:, 3, cs],
                                  start=True, stop=True, skip_group_check=True)
                pe.matmul(ph[:, 0:256], b_nat, wxdt, start=True, stop=True).then_inc(ys_done, 1)

            def decode_in(g):
                pe.wait_ge(dec_saved, g + 1)
                pe.wait_ge(st_in, 16 * g + 16)
                pe.wait_ge(h_ready, NCH * g + NCH)
                for j in range(2):
                    for b in range(NSEQ):
                        tok = slice(TDEC * b, TDEC * (b + 1))
                        last = pe.matmul(py[:, 64 + j * NDEC + TDEC * b:64 + j * NDEC + TDEC * (b + 1)],
                                         st[:, b, j * P:(j + 1) * P], d_cur[:, 3, tok], start=True, stop=True,
                                         skip_group_check=True)
                last.then_inc(d_off, 1)
                for j in range(3):
                    pe.transpose(pt[0:NDEC, j * P:(j + 1) * P], d_cur[:, j, :], ident[:, :])
                pe.matmul(pt[0:NDEC, 384:384 + NDEC], d_cur[:, 2, :], d_cur[:, 3, :], start=True, stop=True)\
                    .then_inc(d_pt, 1)
                for h in range(HPG):
                    pe.matmul(ps[:, h * NDEC:(h + 1) * NDEC], pick_head(g, h),
                              acum_bf[:, SEQ:T], start=(h == 0), stop=False, skip_group_check=True)
                pe.matmul(ps[:, 0:HPG * NDEC], ident_bf[0:NDEC, :],
                          mask_dec[:, :].unsqueeze(1).broadcast_to([NDEC, HPG, NDEC]), start=False, stop=True,
                          skip_group_check=True)
                for j in range(2):
                    last = pe.matmul(ps[:, 128 + j * NDEC:128 + (j + 1) * NDEC],
                                     pick_pair(g, j), acum_bf[:, SEQ:T],
                                     start=True, stop=True, skip_group_check=True)
                last.then_inc(d_ps, 1)

            def decode_add(bank, r):
                for b in range(2):
                    last = pe.matmul(bank[:, b * 256:(b + 1) * 256], d_bm[0:NDEC, 2 * r + b, :], d_wxdt[0:NDEC, :],
                                     start=True, stop=True, skip_group_check=True)
                return last

            def decode_mid(g):
                pe.wait_ge(d_m_s, g + 1)
                pe.wait_ge(d_bn_s, g + 1)
                for h in range(HPG):
                    pe.matmul(py[(h % 2) * HD:(h % 2 + 1) * HD, (h // 2) * NDEC:(h // 2 + 1) * NDEC],
                              d_xdt[0:NDEC, h * HD:(h + 1) * HD], d_m[0:NDEC, h, :], start=True, stop=True,
                              skip_group_check=True)
                for r, bank in enumerate((ph, ps, pt)):
                    last = decode_add(bank, r)
                last.then_inc(d_y, 1)

            def decode_end(g):
                pe.wait_ge(d_add, 3 * g + 1)
                decode_add(ph, 3).then_inc(d_r3, 1)
                pe.wait_ge(d_ssum_s, g + 1)
                pe.matmul(ps[:, :], ones[:, :], d_ssum[:, 0:SEQ], start=True, stop=True)
                pe.matmul(pt[:, 0:NDEC], ones[:, :], d_ssum[:, SEQ:T], start=True, stop=True).then_inc(d_stat, 1)

            def group(g, ssd):
                p = g - 1
                if ssd:
                    ssd_1(0, p)
                    ssd_e(p)
                for j in range(4):
                    for m in range(2):
                        if not ssd and j == 0 and m == 0:
                            pe.wait_ge(dt_act, 1)
                        fill(blk(j % 2, 4 * g + j), ra_hi, ra_lo, 0, m, m + 1)
                        if ssd and j < 2:
                            c = 2 * j + m
                            ssd_2(c, p)
                            if c < NCH - 1:
                                ssd_1(c + 1, p)
                        elif ssd and (j, m) == (2, 0):
                            decode_in(p)
                        elif ssd and (j, m) == (2, 1):
                            decode_mid(p)
                        elif ssd and (j, m) == (3, 0):
                            decode_end(p)

            group(0, False)
            pe.wait_ge(acum_ready, 1)
            pe.wait_ge(const_s, 4)
            for q, src in enumerate((dt_r, dt_t)):
                for c in range(NCH + 1):
                    n = CHUNK if c < NCH else NDEC
                    last = pe.transpose(ps[0:n, (q * (NCH + 1) + c) * HEADS:(q * (NCH + 1) + c + 1) * HEADS],
                                        src[0:HEADS, c * CHUNK:c * CHUNK + n], ident[0:HEADS, 0:HEADS])
            last.then_inc(nat_t, 1)
            pe.wait_ge(nat_copied, 2)
            pe.matmul(py[:, 0:NCH * HEADS], ident[:, P - 1:P].broadcast_to([P, P]),
                      acum_nat[:, 0:NCH, :], start=True, stop=True)
            for b in range(NSEQ):
                last_tok = TDEC * b + TDEC - 1
                pe.matmul(py[:, (NCH + b) * HEADS:(NCH + b + 1) * HEADS],
                          ident[0:NDEC, last_tok:last_tok + 1].broadcast_to([NDEC, P]),
                          acum_nat[0:NDEC, NCH, :], start=True, stop=True)
            pe.matmul(ph[0:NDEC, 0:HEADS],
                      last_sel[:, :],
                      acum_nat[0:NDEC, NCH, :], start=True, stop=True).then_inc(nat_b, 1)
            with pe.Fori(1, GROUPS) as g:
                group(g, True)
            group(GROUPS, True)
            with pe.Fori(2, 4) as i:
                for s in range(2):
                    fill(blk(s, B_GATES + 2 * i + s), ra_hi, ra_lo, 0)
            pe.wait_ge(ys_ready, KT)
            for i in range(4):
                if i == 2:
                    pe.wait_ge(cc_added, GROUPS)
                    pe.wait_ge(d_rstd_s, GROUPS)
                    for hf, bank in enumerate((pt, ps)):
                        last = pe.matmul(bank[:, 0:H2], ones[:, :], cc_sum[:, hf * H2:(hf + 1) * H2],
                                         start=True, stop=True)
                    last.then_inc(l_stat, 1)
                fill(blk(i % 2, B_SSM + i), rb_hi, rb_lo, 0)
            pe.wait_ge(ys_ready, 2 * KT)
            for i in range(4):
                fill(blk(i % 2, B_SSM + 4 + i), ra_hi, ra_lo, 0)
                if i == 0:
                    pe.wait_ge(l_ssum_s, KT)
                    for hf, bank in enumerate((py, ph)):
                        last = pe.matmul(bank[:, 0:H2], ones[:, :], l_ssum[:, hf * H2:(hf + 1) * H2],
                                         start=True, stop=True)
                    last.then_inc(l_stat2, 1)
            pe.wait_ge(cc_ready2, KT)
            with pe.Fori(0, 2) as i:
                for s in range(2):
                    fill(blk(s, B_PW + 2 * i + s), rb_hi, rb_lo, 0)
            pe.wait_ge(mg_ready, KT)
            with pe.Fori(0, 2) as i:
                for s in range(2):
                    fill(blk(s, B_WOUT + 2 * i + s), ra_hi, ra_lo, 0)
            pe.wait_ge(hn_ready, KT)
            pe.wait_ge(o_sum_s, KT)
            for hf, bank in enumerate((pt, ps)):
                last = pe.matmul(bank[:, 0:H2], ones[:, :], o_ssum[:, hf * H2:(hf + 1) * H2],
                                 start=True, stop=True)
            last.then_inc(o_stat, 1)
            with pe.Fori(0, 4) as i:
                for j in range(4):
                    fill(blk(j % 2, B_FFN + 8 * i + j), rb_hi, rb_lo, 0)
                pe.wait_ge(f_ready, KT * i + KT)
                for j in range(4):
                    fill(blk(j % 2, B_FFN + 8 * i + 4 + j), ra_hi, ra_lo, 0)
            for k in range(KT):
                pe.wait_ge(z_sq, k + 1)
                for hf, bank in enumerate((py, ph)):
                    last = pe.matmul(bank[:, 0:H2], ones[:, :], o_sq[:, k % 2, hf * H2:(hf + 1) * H2],
                                     start=(k == 0), stop=(k == KT - 1))
                last.then_inc(z_stat, 1)

        @block.scalar
        def _(act):
            steps = Steps(act, act_c)

            def hi(b, s, turn):
                act.wait_ge(w_in[s], 16 * turn + 16)
                if not isinstance(b, int) or b >= 2:
                    act.wait_ge(tile_done, 2 * b - 2)
                act.activation(w_hi[:, s, :], w_raw[:, s, :], ACT.Copy).then_inc(w_hi_s, 1)

            def hi_next(pair, s):
                if s == 0:
                    hi(2 * pair + 1, 1, pair)
                else:
                    hi(2 * pair + 2, 0, pair + 1)

            for k in range(KT):
                act.wait_ge(x_in_s[2 * k // KT], 16)
                if k >= 2:
                    act.wait_ge(n_sum, k - 1)
                act.activation(sq0[:, k % 2, :], x_t[:, k, :], ACT.Square).then_inc(n_sq, 1)
            act.wait_ge(const_s, 2)
            act.wait_ge(n_sum, KT)
            n = steps.did(act.activation(halves(rstd0), main(0), ACT.Ln, bias=eps[:, :], scale=1.0 / D_MODEL))
            steps.need(n)
            act.activation(rstd0, rstd0, ACT.Exp, scale=-0.5).then_inc(n_rstd, 1)
            act.wait_ge(wdt_in, 16)
            act.activation(rb_hi[:, :, :].rearrange("p k t -> p (k t)")[:, 0:KT * P], wdt_raw, ACT.Copy)\
                .then_inc(wdt_hi_s, 1)
            for k in range(KT):
                act.wait_ge(n_xn, k + 1)
                act.activation(ra_hi[:, k, :], xn0[:, k % 2, :], ACT.Copy).then_inc(u_hi_s, 1)
            hi(0, 0, 0)
            act.wait_ge(par_s, 32)
            act.wait_ge(dt_psum, 1)
            act.activation(halves(dt_v), main(0), ACT.Identity, bias=dt_pars[:, 0:1]).then_inc(dt_act, 1)
            act.activation(a_neg[:, :], dt_pars[:, 1:2], ACT.Exp).then_inc(dt_act, 1)
            hi(1, 1, 0)
            act.wait_ge(dt_dve, 1)
            act.activation(dt_e, dt_e, ACT.Exp).then_inc(dt_act, 1)

            def evac_raw(g, j, m, first):
                i = 2 * j + m
                if i == 0:
                    act.wait_ge(par_ready, 1)
                    act.wait_ge(sstate_in, 16 * g + 16)
                    if not first:
                        act.wait_ge(sout_copied, g)
                    act.activation(raw_d[:, :, :, 0:SPRE], sstate, ACT.Copy).then_inc(sstate_used, 1)
                act.wait_ge(tile_done, 8 * g + i + 1)
                q = H2 - NDEC
                act.activation(raw[:, i, SPRE:SPRE + H2], psum[m][:, 0, 0:H2], ACT.Copy)
                act.activation(raw[:, i, SPRE + H2:SPRE + SEQ], psum[m][:, 1, 0:q], ACT.Copy)
                act.activation(raw_d[:, i, :, SPRE:], psum[m][:, 1, q:H2].rearrange("p (b t) -> p b t", t=TDEC),
                               ACT.Copy).then_inc(tile_free[m], 1)
                act.wait_ge(tile_free[m], 4 * g + j + 1)
                act.activation(acc[:, i, 0:CW], raw[:, i, SPRE:], ACT.Identity,
                               bias=par1("ssm_b", 4 * g + i), scale=par1("ssm_w", (4 * g + i) * SK + SK - 1))\
                    .then_inc(raw_ready, 1)

            def ssd_exps(c, p):
                act.wait_ge(pt_done, NCH * p + c + 1)
                act.activation(scores, pt[:, 3 * P:4 * P], ACT.Copy)
                act.wait_ge(ps_done, NCH * p + c + 1)
                for h in range(HPG):
                    last = act.activation(decay[:, h, :], ps[:, h * P:(h + 1) * P], ACT.Exp,
                                          bias=nacum_nat[:, c, bass.ds(4 * p + h, 1)])
                last.then_inc(decay_ready, 1)
                act.activation(b_nat, pt[:, 2 * P:3 * P], ACT.Copy)
                for to, factor in ((xdt, dt_nat), (wxdt, dtw_nat)):
                    for h in range(HPG):
                        last = act.activation(to[:, h * HD:(h + 1) * HD], pt[:, h * HD:(h + 1) * HD], ACT.Copy,
                                              scale=factor[:, c, bass.ds(4 * p + h, 1)])
                last.then_inc(xb_ready, 1)

            def ssd_e_exp(p):
                for j, bank in enumerate((ph, py)):
                    act.wait_ge(e_psum, 2 * p + j + 1)
                    last = act.activation(e_acc[:, j, :], bank[:, :], ACT.Exp)
                last.then_inc(e_ready, 1)

            def conv01(g):
                act.wait_ge(glu_ready, g + 1)
                act.activation(conv_a, gx[:, 0:SEQ], ACT.Identity, bias=par1("conf_b", g),
                               scale=par1("conf_w", g * CK))
                act.activation(conv_b, gx[:, 1:1 + SEQ], ACT.Copy, scale=par1("conf_w", g * CK + 1))\
                    .then_inc(conv01_s, 1)

            def decode_in(p):
                act.wait_ge(d_pt, p + 1)
                act.wait_ge(d_ps, p + 1)
                act.activation(d_sc[0:NDEC, :], pt[0:NDEC, 384:384 + NDEC], ACT.Copy)
                for h in range(HPG):
                    act.activation(d_decay[0:NDEC, h, :], ps[0:NDEC, h * NDEC:(h + 1) * NDEC], ACT.Exp,
                                   bias=nacum_nat[0:NDEC, NCH, bass.ds(4 * p + h, 1)])
                act.activation(d_e.rearrange("p a b -> p (a b)"), ps[:, 128:128 + 2 * NDEC], ACT.Exp)\
                    .then_inc(d_dec_s, 1)
                for to, factor in ((d_xdt, dt_nat), (d_wxdt, dtw_nat)):
                    for h in range(HPG):
                        act.activation(to[0:NDEC, h * HD:(h + 1) * HD], pt[0:NDEC, h * HD:(h + 1) * HD], ACT.Copy,
                                       scale=factor[0:NDEC, NCH, bass.ds(4 * p + h, 1)])
                for b in range(NSEQ):
                    last = act.activation(d_bm[0:NDEC, b, :], pt[0:NDEC, 2 * P:3 * P], ACT.Copy,
                                          scale=seq_mask[:, b:b + 1])
                last.then_inc(d_bn_s, 1)

            def y_square(p):
                act.wait_ge(d_ycur, p + 1)
                act.activation(d_sq, y_sb, ACT.Square).then_inc(d_sq_s, 1)

            def y_rstd(p):
                act.wait_ge(d_stat, p + 1)
                act.activation(d_rstd[:, 0:SEQ], ps[:, :], ACT.Ln, bias=eps[:, :], scale=1.0 / 256)\
                    .then_inc(y_ln_s, 1)
                act.activation(d_rstd[:, SEQ:T], pt[:, 0:NDEC], ACT.Ln, bias=eps[:, :], scale=1.0 / 256)\
                    .then_inc(y_ln_s, 1)
                act.wait_ge(y_ln_s, 2 * p + 2)
                act.activation(d_rstd, d_rstd, ACT.Exp, scale=-0.5).then_inc(d_rstd_s, 1)

            def group(g, ssd):
                p = g - 1
                for j in range(2):
                    for m in range(2):
                        if ssd:
                            ssd_exps(2 * j + m, p)
                        if ssd and (j, m) == (0, 0):
                            ssd_e_exp(p)
                            conv01(p)
                            hi(4 * g + 1, 1, 2 * g)
                        evac_raw(g, j, m, not ssd)
                    hi(4 * g + 2 + j, j % 2, 2 * g + 1)
                if ssd:
                    act.wait_ge(y_done, g)
                act.wait_ge(tile_done, 8 * g + 5)
                act.activation(halves(zs[:, 0, :]), main(0), ACT.Copy).then_inc(tile_free[0], 1)
                if ssd:
                    decode_in(p)
                act.wait_ge(tile_free[0], 4 * g + 3)
                act.activation(zs[:, 0, :], zs[:, 0, :], ACT.Silu)
                for i in range(4):
                    act.wait_ge(conv4_s, 4 * g + i + 1)
                    act.activation(sil[:, i, 0:CW], acc[:, i, 0:CW], ACT.Silu).then_inc(sil_ready, 1)
                    if i == 1:
                        act.wait_ge(tile_done, 8 * g + 6)
                        act.activation(halves(zs[:, 1, :]), main(1), ACT.Silu).then_inc(tile_free[1], 1)
                if ssd:
                    y_square(p)
                hi(4 * g + 4, 0, 2 * g + 2)
                if ssd:
                    act.wait_ge(glu_ready, g)
                act.wait_ge(tile_done, 8 * g + 7)
                act.activation(halves(zh[:, 0, :]), main(0), ACT.Copy, scale=0.5).then_inc(tile_free[0], 1)
                if ssd:
                    y_rstd(p)
                act.wait_ge(sil_ready, 4 * g + 4)
                act.activation(d_cur.rearrange("p a (b t) -> p a b t", b=NSEQ), sil_d, ACT.Copy)\
                    .then_inc(dec_saved, 1)
                act.activation(d_z, zs[:, :, SEQ:T], ACT.Copy).then_inc(z_ready, 1)
                act.wait_ge(tile_done, 8 * g + 8)
                act.activation(halves(zh[:, 1, :]), main(1), ACT.Tanh, scale=0.5).then_inc(tile_free[1], 1)

            group(0, False)
            act.wait_ge(nat_t, 1)
            for q, dst in enumerate((dt_nat, acum_nat)):
                at = q * (NCH + 1) * HEADS
                steps.did(act.activation(dst[:, 0:NCH, :].rearrange("p c h -> p (c h)"),
                                         ps[:, at:at + NCH * HEADS], ACT.Copy))
                act.activation(dst[0:NDEC, NCH, :], ps[0:NDEC, at + NCH * HEADS:at + (NCH + 1) * HEADS],
                               ACT.Copy).then_inc(nat_copied, 1)
            act.wait_ge(nat_diff, 1)
            act.activation(exp_last[:, :, :].rearrange("p c h -> p (c h)"), py[:, 0:(NCH + NSEQ) * HEADS], ACT.Exp)
            steps.did(act.activation(w_nat[:, 0:NCH, :], w_nat[:, 0:NCH, :], ACT.Exp))
            act.activation(w_nat[0:NDEC, NCH, :], w_nat[0:NDEC, NCH, :], ACT.Exp).then_inc(nat_exp, 1)
            act.wait_ge(nat_ready, 1)
            with act.Fori(1, GROUPS) as g:
                group(g, True)

            def gate(i, m):
                act.wait_ge(tile_done, 2 * (B_GATES + i) + m + 1)
                if not isinstance(i, int) or i:
                    act.wait_ge(gates_st[m], 16 * i)
                act.activation(halves(gates_sb[:, m, :]), main(m), ACT.Copy).then_inc(tile_free[m], 1)

            p = GROUPS - 1
            for c in range(NCH):
                ssd_exps(c, p)
                if c == 0:
                    ssd_e_exp(p)
                    conv01(p)
                    hi(B_GATES + 1, 1, B_GATES // 2)
                    act.wait_ge(sout_copied, GROUPS)
                gate(c // 2, c % 2)
                if c % 2:
                    hi(B_GATES + 2 + c // 2, c // 2, B_GATES // 2 + 1)
            gate(2, 0)
            decode_in(p)
            gate(2, 1)
            y_square(p)
            hi(B_GATES + 4, 0, B_GATES // 2 + 2)
            gate(3, 0)
            y_rstd(p)
            gate(3, 1)

            def y_high(i, to):
                act.wait_ge(y_in[i % 2], 16 * (i // 2) + 16)
                for j in range(2):
                    act.activation(to[:, (2 * i + j) % KT, :], y_ld[:, i % 2, j, :], ACT.Copy).then_inc(ys_hi, 1)

            act.wait_ge(d_yn_s, GROUPS)
            for i in range(4):
                hi_next((B_GATES + 4 + i) // 2, i % 2)
                for m in range(2):
                    gate(4 + i, m)
                    if m == 0:
                        y_high(i, rb_hi)
            for i in range(4):
                hi_next((B_SSM + i) // 2, i % 2)
                if i == 0:
                    act.wait_ge(tile_done, 2 * B_SSM)
                y_high(4 + i, ra_hi)
                for m in range(2):
                    act.wait_ge(tile_done, 2 * (B_SSM + i) + m + 1)
                    act.activation(halves(b_sum[:, 2 * i + m, :]), main(m), ACT.Copy, scale=0.5)\
                        .then_inc(tile_free[m], 1)
            act.wait_ge(l_stat, 1)
            for hf, bank in enumerate((pt, ps)):
                last = act.activation(l_mean[:, hf * H2:(hf + 1) * H2], bank[:, 0:H2], ACT.Copy,
                                      scale=1.0 / D_MODEL)
            last.then_inc(l_mean_s, 1)
            hi_next(B_SSM // 2 + 2, 0)
            for m in range(KT):
                act.wait_ge(l_xc, m + 1)
                if m >= 2:
                    act.wait_ge(l_ssum_s, m - 1)
                act.activation(l_sq[:, m % 2, :], xc[:, m, :], ACT.Square).then_inc(l_sq_s, 1)
                if m == 5:
                    hi_next(B_SSM // 2 + 2, 1)
            act.wait_ge(l_stat2, 1)
            for hf, bank in enumerate((py, ph)):
                n = steps.did(act.activation(l_rstd[:, hf * H2:(hf + 1) * H2], bank[:, 0:H2], ACT.Ln,
                                             bias=eps[:, :], scale=1.0 / D_MODEL))
            steps.need(n)
            act.activation(l_rstd, l_rstd, ACT.Exp, scale=-0.5).then_inc(l_rstd_s, 1)
            hi_next(B_SSM // 2 + 3, 0)

            def cc_high(m):
                act.wait_ge(l_sil, m + 1)
                act.activation(rb_hi[:, m, :], xc[:, m, :], ACT.Copy).then_inc(cc_hi_s, 1)

            for m in range(KT):
                act.wait_ge(l_t, m + 1)
                act.activation(xc[:, m, :], xc[:, m, :], ACT.Silu, bias=par1("ln_b", m), scale=par1("ln_g", m))\
                    .then_inc(l_sil, 1)
                if m >= 1:
                    cc_high(m - 1)
                if m == 5:
                    hi_next(B_SSM // 2 + 3, 1)
            cc_high(KT - 1)
            for m in range(KT):
                act.wait_ge(g_in_s[m % 2], 16 * (m // 2) + 16)
                act.activation(g_in[:, m % 2, :, :], g_in[:, m % 2, :, :], ACT.Tanh, scale=0.5)
                act.wait_ge(tile_done, 2 * B_PW + m + 1)
                act.activation(halves(pw_a[:, m % 2, :]), main(m), ACT.Identity, bias=par1("b_pw", m), scale=0.5)\
                    .then_inc(tile_free[m % 2], 1)
                if m >= 1:
                    act.wait_ge(p_m, 3 * m)
                    act.activation(ra_hi[:, m - 1, :], pw_m[:, (m - 1) % 2, :], ACT.Copy).then_inc(mg_hi, 1)
                if m % 2 == 0:
                    hi_next((B_PW + m // 2) // 2, (m // 2) % 2)
            act.wait_ge(p_m, 3 * KT)
            act.activation(ra_hi[:, KT - 1, :], pw_m[:, (KT - 1) % 2, :], ACT.Copy).then_inc(mg_hi, 1)
            for m in range(KT):
                if m % 2 == 0:
                    hi_next((B_WOUT + m // 2) // 2, (m // 2) % 2)
                act.wait_ge(tile_free[m % 2], B_WOUT + m // 2 + 1)
                if m >= 2:
                    act.wait_ge(o_sum_s, m - 1)
                act.activation(o_sq[:, m % 2, :], h_sb[:, m, :], ACT.Square).then_inc(o_act, 1)
                act.activation(rb_hi[:, m, :], h_sb[:, m, :], ACT.Copy, scale=par1("g_ffn", m)).then_inc(o_act, 1)
            act.wait_ge(o_stat, 1)
            for hf, bank in enumerate((pt, ps)):
                n = steps.did(act.activation(o_rstd[:, hf * H2:(hf + 1) * H2], bank[:, 0:H2], ACT.Ln,
                                             bias=eps[:, :], scale=1.0 / D_MODEL))
            steps.need(n)
            act.activation(o_rstd, o_rstd, ACT.Exp, scale=-0.5).then_inc(o_rstd_s, 1)

            def hidden(i, n):
                k = KT * i + n
                act.wait_ge(f_v_s, k + 1)
                act.activation(f_s[:, n % 2, :], f_v[:, n % 2, :], ACT.Square).then_inc(f_sq_s, 1)
                act.wait_ge(f_sq_s, k + 1)
                act.activation(ra_hi[:, n, :], f_s[:, n % 2, :], ACT.Copy).then_inc(f_hi, 1)

            def quarter(i, last):
                for j in range(4):
                    hi_next(B_FFN // 2 + 4 * i + j // 2, j % 2)
                    for m in range(2):
                        n = 2 * j + m
                        act.wait_ge(tile_done, 2 * B_FFN + 16 * i + n + 1)
                        act.activation(halves(f_r[:, n % 2, :]), main(m), ACT.Relu).then_inc(tile_free[m], 1)
                        if n >= 1:
                            hidden(i, n - 1)
                hidden(i, KT - 1)
                for j in range(3 if last else 4):
                    hi_next(B_FFN // 2 + 4 * i + 2 + j // 2, j % 2)

            with act.Fori(0, 3) as i:
                quarter(i, False)
            quarter(3, True)
            for m in range(KT):
                act.wait_ge(tile_free[m % 2], NBLOCKS - 3 + m // 2)
                if m >= 2:
                    act.wait_ge(z_stat, m - 1)
                act.activation(o_sq[:, m % 2, :], h_sb[:, m, :], ACT.Square).then_inc(z_sq, 1)
            act.wait_ge(z_stat, KT)
            for hf, bank in enumerate((py, ph)):
                n = steps.did(act.activation(o_rstd[:, hf * H2:(hf + 1) * H2], bank[:, 0:H2], ACT.Ln,
                                             bias=eps[:, :], scale=1.0 / D_MODEL))
            steps.need(n)
            act.activation(o_rstd, o_rstd, ACT.Exp, scale=-0.5).then_inc(z_rstd, 1)

        @block.vector
        def _(dve):
            steps = Steps(dve, dve_c)

            def lo(b, s):
                dve.wait_ge(w_hi_s, b + 1)
                dve.tensor_tensor(w_lo[:, s, :], w_raw[:, s, :], fr(w_hi[:, s, :]), ALU.subtract)\
                    .then_inc(w_lo_s, 1)

            def lo_next(pair, s):
                lo(2 * pair + 1, 1) if s == 0 else lo(2 * pair + 2, 0)

            dve.wait_ge(par_s, 32)
            at, n = PARAMS["b_pw"]
            dve.tensor_scalar(pars[:, at:at + n], pars[:, at:at + n], 0.5, None, ALU.mult).then_inc(par_ready, 1)
            dve.wait_ge(n_rstd, 1)
            for k in range(KT):
                if k >= 2:
                    dve.wait_ge(u_hi_s, k - 1)
                dve.scalar_tensor_tensor(xn0[:, k % 2, :], x_t[:, k, :], par1("g_mix", k), rstd0, ALU.mult,
                                         ALU.mult).then_inc(n_xn, 1)
                if k == 0:
                    dve.wait_ge(wdt_hi_s, 1)
                    dve.tensor_tensor(rb_lo[:, :, :].rearrange("p k t -> p (k t)")[:, 0:KT * P], wdt_raw,
                                      fr(rb_hi[:, :, :].rearrange("p k t -> p (k t)")[:, 0:KT * P]),
                                      ALU.subtract).then_inc(wdt_ready, 1)
                dve.wait_ge(u_hi_s, k + 1)
                dve.wait_ge(n_xn, k + 1)
                dve.tensor_tensor(ra_lo[:, k, :], xn0[:, k % 2, :], fr(ra_hi[:, k, :]), ALU.subtract)\
                    .then_inc(u_ready, 1)
            lo(0, 0)
            dve.wait_ge(dt_act, 2)
            dve.scalar_tensor_tensor(dt_e, dt_v, -1.0, dt_v, ALU.mult, ALU.min).then_inc(dt_dve, 1)
            steps.did(dve.tensor_scalar(a_neg[:, :], a_neg[:, :], -1.0, None, ALU.mult))
            n_r = steps.did(dve.tensor_scalar(dt_r, dt_v, 0.0, None, ALU.max))
            lo(1, 1)
            dve.wait_ge(dt_act, 3)
            n = steps.did(dve.tensor_scalar(dt_z, dt_e, 2.0, None, ALU.add))
            steps.need(n)
            n = steps.did(dve.reciprocal(dt_z, dt_z))
            steps.need(n)
            n_z = steps.did(dve.tensor_tensor(dt_z, dt_z, dt_e, ALU.mult))
            steps.need(n_z)
            n = steps.did(dve.tensor_tensor(dt_z2, dt_z, dt_z, ALU.mult))
            steps.need(n)
            n = steps.did(dve.tensor_scalar(dt_p, dt_z2, 1.0 / 17, None, ALU.mult))
            for odd in range(15, 1, -2):
                steps.need(n)
                n = steps.did(dve.scalar_tensor_tensor(dt_p, dt_p, 1.0 / odd, dt_z2, ALU.add, ALU.mult))
            steps.need(n)
            n = steps.did(dve.scalar_tensor_tensor(dt_t, dt_p, 1.0, dt_z, ALU.add, ALU.mult))
            steps.need(n)
            n = steps.did(dve.scalar_tensor_tensor(dt_r, dt_t, 2.0, dt_r, ALU.mult, ALU.add))
            steps.need(n)
            n = steps.did(dve.tensor_scalar(dt_p, dt_r, a_neg[:, :], None, ALU.mult))
            steps.need(n)
            dve.wait_ge(const_s, 3)
            n = steps.did(dve.tensor_tensor_scan(dt_t, scan_keep, dt_p, 0.0, ALU.mult, ALU.add))
            steps.need(n)
            n = steps.did(dve.tensor_copy(acum_bf[:, :], dt_t[0:96, :]))
            steps.need(n)
            n = steps.did(dve.tensor_tensor(dt_z[0:96, :], dt_t[0:96, :], acum_bf[:, :], ALU.subtract))
            steps.need(n)
            steps.did(dve.tensor_copy(acum_bf[32:64, :], dt_z[32:64, :]))
            n = steps.did(dve.tensor_copy(acum_bf[64:96, :], dt_z[64:96, :]))
            steps.need(n)
            n = steps.did(dve.tensor_tensor(dt_z[64:96, :], dt_z[64:96, :], acum_bf[64:96, :], ALU.subtract))
            steps.need(n)
            dve.tensor_copy(acum_bf[64:96, :], dt_z[64:96, :]).then_inc(acum_ready, 1)

            class Conv31:

                def __init__(self, p):
                    self.p, self.k, self.last = p, 2, [None, None]

                def start(self):
                    dve.wait_ge(conv01_s, self.p + 1)

                def taps(self, n):
                    for k in range(self.k, min(self.k + n, CK)):
                        to = (conv_a, conv_b)[k % 2]
                        w = par1("conf_w", self.p * CK + k)
                        src = gx[:, k:k + SEQ]
                        if self.last[k % 2] is not None:
                            steps.need(self.last[k % 2])
                        self.last[k % 2] = steps.did(
                            dve.scalar_tensor_tensor(to, src, w, to, ALU.mult, ALU.add))
                    self.k = min(self.k + n, CK)

                def finish(self):
                    self.taps(CK)
                    dve.wait_ge(cc_free, self.p + 1)
                    steps.need(max(self.last))
                    n = steps.did(dve.tensor_tensor(ccs[:, 0:SEQ], conv_a, conv_b, ALU.add))
                    dve.wait_ge(cpre_ready, self.p + 1)
                    hs = NSEQ // 2
                    prod = conv_b[:, 0:hs * TDEC * CK]
                    base = gd[:, 0:1, 0:1]
                    w = par1("conf_w", self.p * CK, CK)
                    for b in range(2):
                        wins = bass.AP(base.tensor, base.offset + b * hs * (CPRE + TDEC),
                                       [[base.ap[0][0], P], [CPRE + TDEC, hs], [1, TDEC], [1, CK]])
                        steps.need(n)
                        n = steps.did(dve.tensor_tensor(
                            prod.rearrange("p (b t k) -> p b t k", b=hs, t=TDEC), wins,
                            w.unsqueeze(1).unsqueeze(1).broadcast_to([P, hs, TDEC, CK]), ALU.mult))
                        steps.need(n)
                        n = steps.did(dve.tensor_reduce(
                            ccs[:, SEQ + b * hs * TDEC:SEQ + (b + 1) * hs * TDEC],
                            prod.rearrange("p (n k) -> p n k", k=CK), AX.X, ALU.add))
                    steps.need(n)
                    dve.tensor_scalar(ccs[:, SEQ:T], ccs[:, SEQ:T], par1("conf_b", self.p), None, ALU.add)\
                        .then_inc(cc_ready, 1)

            def by_head(ap, c, p):
                return ap[:, c, bass.ds(4 * p, HPG)].unsqueeze(2).broadcast_to([P, HPG, HD])

            def heads(ap):
                return ap.rearrange("p (h d) -> p h d", d=HD)

            def ssd_scores(c, p):
                dve.wait_ge(decay_ready, NCH * p + c + 1)
                dve.tensor_tensor(m_t, decay, scores.unsqueeze(1).broadcast_to([P, HPG, P]), ALU.mult)\
                    .then_inc(m_ready, 1)

            def ssd_state(c, p):
                cs = slice(c * CHUNK, (c + 1) * CHUNK)
                y_in_chunk = py[:, 0:256].rearrange("p (j n) -> p j n", j=2)
                dve.wait_ge(ys_done, NCH * p + c + 1)
                if c == 0:
                    dve.wait_ge(ssd_free, p + 1)
                    steps.did(dve.tensor_copy(y_sb[:, :, cs], y_in_chunk))
                    dve.tensor_copy(h_t, ph[:, 0:256]).then_inc(h_ready, 1)
                else:
                    if c == 1:
                        dve.wait_ge(e_ready, p + 1)
                    n = steps.did(dve.tensor_tensor(y_tmp, py[:, 256:512].rearrange("p (j n) -> p j n", j=2),
                                                    e_acc[:, :, cs], ALU.mult))
                    dve.wait_ge(h_ready, NCH * p + c)
                    n2 = steps.did(dve.tensor_tensor(heads(h_t), heads(h_t), by_head(exp_last, c, p), ALU.mult))
                    steps.need(n)
                    steps.did(dve.tensor_tensor(y_sb[:, :, cs], y_tmp, y_in_chunk, ALU.add))
                    steps.need(n2)
                    dve.tensor_tensor(h_t, h_t, ph[:, 0:256], ALU.add).then_inc(h_ready, 1)

            def ssd_y(p):
                dve.wait_ge(z_ready, p + 1)
                steps.need(steps.n)
                for j in range(2):
                    n = steps.did(dve.scalar_tensor_tensor(y_sb[:, j, 0:SEQ], sil[:, j, 0:SEQ],
                                                           par1("d_skip", 2 * p + j), y_sb[:, j, 0:SEQ],
                                                           ALU.mult, ALU.add))
                steps.need(n)
                dve.tensor_tensor(y_sb[:, :, 0:SEQ], y_sb[:, :, 0:SEQ], zs[:, :, 0:SEQ], ALU.mult).then_inc(y_done, 1)

            def conv4(g, pair):
                tiles = (2 * pair, 2 * pair + 1)
                dve.wait_ge(raw_ready, 4 * g + 2 * pair + 2)
                last = {}
                for k in range(SK - 1):
                    for i in tiles:
                        w = par1("ssm_w", (4 * g + i) * SK + k)
                        if k:
                            steps.need(last[i])
                        to = acc[:, i, 0:CW]
                        ins = dve.scalar_tensor_tensor(to, raw[:, i, k:k + CW], w, to, ALU.mult, ALU.add)
                        if k == SK - 2:
                            ins.then_inc(conv4_s, 1)
                        else:
                            last[i] = steps.did(ins)

            def decode_m(p):
                dve.wait_ge(d_dec_s, p + 1)
                dve.tensor_tensor(d_m[0:NDEC], d_decay[0:NDEC],
                                  d_sc[0:NDEC, :].unsqueeze(1).broadcast_to([NDEC, HPG, NDEC]), ALU.mult)\
                    .then_inc(d_m_s, 1)
                dve.wait_ge(d_off, p + 1)
                return steps.did(dve.tensor_tensor(
                    st.rearrange("p b (h d) -> p b h d", d=HD), st.rearrange("p b (h d) -> p b h d", d=HD),
                    exp_last[:, NCH:, bass.ds(4 * p, HPG)].unsqueeze(3).broadcast_to([P, NSEQ, HPG, HD]),
                    ALU.mult))

            def state_add(r, bank, done):
                v = st[:, 2 * r:2 * r + 2, :].rearrange("p b n -> p (b n)")
                dve.tensor_tensor(v, v, bank[:, :], ALU.add).then_inc(done, 1)

            def decode_y(p, n_st):
                dve.wait_ge(d_y, p + 1)
                n = steps.did(dve.tensor_tensor(d_tmp, py[:, 64:128].rearrange("p (j n) -> p j n", j=2), d_e,
                                                ALU.mult))
                steps.need(n)
                n = steps.did(dve.tensor_tensor(d_tmp, d_tmp, py[:, 0:64].rearrange("p (j n) -> p j n", j=2),
                                                ALU.add))
                steps.need(n)
                for j in range(2):
                    n = steps.did(dve.scalar_tensor_tensor(d_tmp[:, j, :], d_cur[:, j, :],
                                                           par1("d_skip", 2 * p + j), d_tmp[:, j, :], ALU.mult,
                                                           ALU.add))
                steps.need(n)
                dve.tensor_tensor(y_sb[:, :, SEQ:T], d_tmp, d_z[:, :, :], ALU.mult).then_inc(d_ycur, 1)
                steps.need(n_st)
                for r, bank in enumerate((ph, ps, pt)):
                    state_add(r, bank, d_add)

            def decode_sum(p):
                dve.wait_ge(d_sq_s, p + 1)
                dve.tensor_tensor(d_ssum, d_sq[:, 0, :], d_sq[:, 1, :], ALU.add).then_inc(d_ssum_s, 1)

            def decode_last(p):
                dve.wait_ge(d_r3, p + 1)
                state_add(3, ph, st_ready)

            def decode_norm(p):
                dve.wait_ge(d_rstd_s, p + 1)
                for j in range(2):
                    ins = dve.scalar_tensor_tensor(d_yn[:, j, :], y_sb[:, j, :], par1("norm_g", 2 * p + j),
                                                   d_rstd, ALU.mult, ALU.mult)
                ins.then_inc(d_yn_s, 1)

            def group(g, ssd):
                p = g - 1
                if ssd:
                    conv = Conv31(p)
                    for c in range(NCH):
                        if c:
                            conv.taps(4)
                        ssd_scores(c, p)
                        if c == 0:
                            conv.start()
                            conv.taps(2)
                            lo(4 * g + 1, 1)
                        conv.taps(3)
                        ssd_state(c, p)
                        if c == 1:
                            lo(4 * g + 2, 0)
                    ssd_y(p)
                else:
                    dve.wait_ge(const_s, 6)
                    lo(4 * g + 2, 0)
                lo(4 * g + 3, 1)
                conv4(g, 0)
                if ssd:
                    n_st = decode_m(p)
                conv4(g, 1)
                if ssd:
                    decode_y(p, n_st)
                    decode_sum(p)
                lo(4 * g + 4, 0)
                if ssd:
                    conv.finish()
                    decode_last(p)
                    decode_norm(p)
                dve.wait_ge(tile_free[1], 4 * g + 4)
                if ssd:
                    dve.wait_ge(cout_copied, g)
                steps.did(dve.scalar_tensor_tensor(gx[:, CPRE:], zh[:, 1, 0:SEQ], 1.0, zh[:, 0, 0:SEQ], ALU.add,
                                                   ALU.mult))
                dve.scalar_tensor_tensor(gd[:, :, CPRE:], zh[:, 1, SEQ:T].rearrange("p (b t) -> p b t", t=TDEC), 1.0,
                                         zh[:, 0, SEQ:T].rearrange("p (b t) -> p b t", t=TDEC), ALU.add, ALU.mult)\
                    .then_inc(glu_ready, 1)

            group(0, False)
            dve.wait_ge(nat_copied, 2)
            steps.did(dve.tensor_scalar(nacum_nat[:, 0:NCH, :], acum_nat[:, 0:NCH, :], -1.0, None, ALU.mult))
            steps.did(dve.tensor_scalar(nacum_nat[0:NDEC, NCH, :], acum_nat[0:NDEC, NCH, :], -1.0, None, ALU.mult))
            dve.wait_ge(nat_b, 1)
            steps.did(dve.tensor_tensor(w_nat[:, 0:NCH, :], py[:, 0:NCH * HEADS]
                                        .rearrange("p (c h) -> p c h", h=HEADS), acum_nat[:, 0:NCH, :],
                                        ALU.subtract))
            dve.tensor_tensor(w_nat[0:NDEC, NCH, :], ph[0:NDEC, 0:HEADS], acum_nat[0:NDEC, NCH, :], ALU.subtract)\
                .then_inc(nat_diff, 1)
            dve.wait_ge(nat_exp, 1)
            steps.did(dve.tensor_tensor(dtw_nat[:, 0:NCH, :], dt_nat[:, 0:NCH, :], w_nat[:, 0:NCH, :], ALU.mult))
            dve.tensor_tensor(dtw_nat[0:NDEC, NCH, :], dt_nat[0:NDEC, NCH, :], w_nat[0:NDEC, NCH, :], ALU.mult)\
                .then_inc(nat_ready, 1)
            with dve.Fori(1, GROUPS) as g:
                steps.enter(g - 1, K_GROUP)
                group(g, True)
            steps.leave(GROUPS - 1)
            p = GROUPS - 1
            conv = Conv31(p)
            for c in range(NCH):
                if c:
                    conv.taps(4)
                ssd_scores(c, p)
                if c == 0:
                    conv.start()
                    conv.taps(2)
                    lo(B_GATES + 1, 1)
                conv.taps(3)
                ssd_state(c, p)
                if c == 1:
                    lo(B_GATES + 2, 0)
            ssd_y(p)
            lo(B_GATES + 3, 1)
            n_st = decode_m(p)
            conv.taps(CK)
            decode_y(p, n_st)
            decode_sum(p)
            lo(B_GATES + 4, 0)
            conv.finish()
            decode_last(p)
            decode_norm(p)

            def y_low(i, hi_part, to):
                for j in range(2):
                    k = (2 * i + j) % KT
                    dve.wait_ge(ys_hi, 2 * i + j + 1)
                    dve.tensor_tensor(to[:, k, :], y_ld[:, i % 2, j, :], fr(hi_part[:, k, :]), ALU.subtract)\
                        .then_inc(ys_ready, 1)

            for i in range(4):
                lo_next((B_GATES + 4 + i) // 2, i % 2)
                if i == 0:
                    dve.wait_ge(st_st, 16 * GROUPS)
                    dve.wait_ge(yn_st, 16 * GROUPS)
                y_low(i, rb_hi, rb_lo)
            for i in range(4):
                lo_next((B_SSM + i) // 2, i % 2)
                y_low(4 + i, ra_hi, ra_lo)

            def b_add(i):
                for m in range(2):
                    dve.wait_ge(tile_done, 2 * (B_SSM + 4 + i) + m + 1)
                    v = halves(b_sum[:, 2 * i + m, :])
                    dve.scalar_tensor_tensor(v, main(m), 0.5, v, ALU.mult, ALU.add).then_inc(tile_free[m], 1)

            lo_next(B_SSM // 2 + 2, 0)
            dve.wait_ge(l_mean_s, 1)
            dve.wait_ge(cc_in, 32)

            def square_sum(m):
                dve.wait_ge(l_sq_s, m + 1)
                if m == 0:
                    ins = dve.tensor_copy(l_ssum, l_sq[:, 0, :])
                else:
                    dve.wait_ge(l_ssum_s, m)
                    ins = dve.tensor_tensor(l_ssum, l_ssum, l_sq[:, m % 2, :], ALU.add)
                ins.then_inc(l_ssum_s, 1)

            for m in range(KT):
                dve.tensor_tensor(xc[:, m, :], xc[:, m, :], l_mean, ALU.subtract).then_inc(l_xc, 1)
                if m >= 1:
                    square_sum(m - 1)
                if m == 3:
                    b_add(0)
                if m == 5:
                    lo_next(B_SSM // 2 + 2, 1)
            square_sum(KT - 1)
            b_add(1)
            lo_next(B_SSM // 2 + 3, 0)
            dve.wait_ge(l_rstd_s, 1)

            def cc_low(m):
                dve.wait_ge(cc_hi_s, m + 1)
                dve.tensor_tensor(rb_lo[:, m, :], xc[:, m, :], fr(rb_hi[:, m, :]), ALU.subtract)\
                    .then_inc(cc_ready2, 1)

            for m in range(KT):
                dve.wait_ge(l_xc, KT)
                dve.tensor_tensor(xc[:, m, :], xc[:, m, :], l_rstd, ALU.mult).then_inc(l_t, 1)
                if m >= 2:
                    cc_low(m - 2)
                if m == 3:
                    b_add(2)
                if m == 5:
                    lo_next(B_SSM // 2 + 3, 1)
            cc_low(KT - 2)
            cc_low(KT - 1)
            b_add(3)
            dve.wait_ge(tile_free[1], B_PW)

            def mg_low(m):
                dve.wait_ge(mg_hi, m + 1)
                dve.tensor_tensor(ra_lo[:, m, :], pw_m[:, m % 2, :], fr(ra_hi[:, m, :]), ALU.subtract)\
                    .then_inc(mg_ready, 1)

            for m in range(KT):
                if m % 2 == 0:
                    lo_next((B_PW + m // 2) // 2, (m // 2) % 2)
                dve.wait_ge(tile_free[m % 2], B_PW + m // 2 + 1)
                if m >= 2:
                    dve.wait_ge(mg_ready, m - 1)
                a, o = pw_a[:, m % 2, :], pw_m[:, m % 2, :]
                dve.scalar_tensor_tensor(a, g_in[:, m % 2, 0, :], 1.0, a, ALU.add, ALU.mult).then_inc(p_m, 1)
                dve.scalar_tensor_tensor(o, g_in[:, m % 2, 1, :], 1.0, b_sum[:, m, :], ALU.add, ALU.mult)\
                    .then_inc(p_m, 1)
                dve.wait_ge(p_m, 3 * m + 2)
                dve.tensor_tensor(o, o, a, ALU.add).then_inc(p_m, 1)
                if m >= 1:
                    mg_low(m - 1)
            mg_low(KT - 1)

            def h_low(m):
                dve.wait_ge(o_act, 2 * m + 2)
                if m == 0:
                    ins = dve.tensor_copy(o_ssum, o_sq[:, 0, :])
                else:
                    dve.wait_ge(o_sum_s, m)
                    ins = dve.tensor_tensor(o_ssum, o_ssum, o_sq[:, m % 2, :], ALU.add)
                ins.then_inc(o_sum_s, 1)
                dve.scalar_tensor_tensor(rb_lo[:, m, :], h_sb[:, m, :], par1("g_ffn", m), fr(rb_hi[:, m, :]),
                                         ALU.mult, ALU.subtract).then_inc(hn_ready, 1)

            for m in range(KT):
                if m % 2 == 0:
                    lo_next((B_WOUT + m // 2) // 2, (m // 2) % 2)
                dve.wait_ge(x_in2[m % 2], 16 * (m // 2) + 16)
                dve.wait_ge(tile_done, 2 * B_WOUT + m + 1)
                dve.tensor_tensor(halves(h_sb[:, m, :]), main(m), halves(x_in[:, m % 2, :]), ALU.add)\
                    .then_inc(tile_free[m % 2], 1)
                if m >= 1:
                    h_low(m - 1)
            h_low(KT - 1)
            dve.wait_ge(o_rstd_s, 1)

            def quarter(i, last):
                def hidden_low(n):
                    dve.wait_ge(f_hi, KT * i + n + 1)
                    dve.tensor_tensor(ra_lo[:, n, :], f_s[:, n % 2, :], fr(ra_hi[:, n, :]), ALU.subtract)\
                        .then_inc(f_ready, 1)

                for j in range(4):
                    lo_next(B_FFN // 2 + 4 * i + j // 2, j % 2)
                    for m in range(2):
                        n = 2 * j + m
                        dve.wait_ge(tile_free[m], B_FFN + 8 * i + j + 1)
                        dve.tensor_tensor(f_v[:, n % 2, :], f_r[:, n % 2, :], o_rstd, ALU.mult).then_inc(f_v_s, 1)
                        if n >= 1:
                            hidden_low(n - 1)
                hidden_low(KT - 1)
                for j in range(4):
                    if not last or j < 3:
                        lo_next(B_FFN // 2 + 4 * i + 2 + j // 2, j % 2)
                    for m in range(2):
                        n = 2 * j + m
                        dve.wait_ge(tile_done, 2 * B_FFN + 16 * i + 8 + n + 1)
                        v = halves(h_sb[:, n, :])
                        dve.tensor_tensor(v, v, main(m), ALU.add).then_inc(tile_free[m], 1)

            with dve.Fori(0, 3) as i:
                quarter(i, False)
            quarter(3, True)
            dve.wait_ge(z_rstd, 1)
            dve.wait_ge(tile_free[1], NBLOCKS)
            for m in range(KT):
                if m >= 2:
                    dve.wait_ge(out_st[m % 2], 16 * (m // 2))
                dve.scalar_tensor_tensor(o_y[:, m % 2, :], h_sb[:, m, :], par1("g_final", m), o_rstd, ALU.mult,
                                         ALU.mult).then_inc(z_y, 1)


K_GROUP = 60


def _cols(w, *ranges):
    b = np.concatenate([w[:, a:a + n] for a, n in ranges], axis=1)
    return b.reshape(KT, P, BW).transpose(1, 0, 2).reshape(P, KT * BW)


def _tiles(x, k):
    return x.T.reshape(k, P, -1).transpose(1, 0, 2).reshape(P, -1)


def kernel(**inputs):
    import concourse.bacc as bacc
    from concourse.bass_utils import run_bass_kernel_spmd

    a = {k: np.asarray(v) for k, v in inputs.items()}
    w_in, w_pw, w_so, w_o, w_up, w_dn = (a[n][0] for n in (
        "w_in", "conf_w_pw", "ssm_w_out", "w_out", "w_up", "w_down"))
    gate0, z0 = 2 * D_MODEL, 4 * D_MODEL
    xbc0 = z0 + 2 * D_MODEL
    dt0 = xbc0 + 4 * D_MODEL
    blocks = []
    for g in range(GROUPS):
        blocks += [_cols(w_in, (xbc0 + 256 * g, 256)),
                   _cols(w_in, (xbc0 + 2048 + P * g, P), (xbc0 + 3072 + P * g, P)),
                   _cols(w_in, (z0 + 256 * g, 256)),
                   _cols(w_in, (P * g, P), (D_MODEL + P * g, P))]
    blocks += [_cols(w_in, (gate0 + P * i, P), (gate0 + D_MODEL + P * i, P)) for i in range(8)]
    for q in range(2):
        blocks += [_cols(w_so[1024 * q:1024 * (q + 1)], (256 * i, 256)) for i in range(4)]
    blocks += [_cols(w_pw, (256 * i, 256)) for i in range(4)]
    blocks += [_cols(w_o, (256 * i, 256)) for i in range(4)]
    for q in range(4):
        blocks += [_cols(w_up, (1024 * q + 256 * i, 256)) for i in range(4)]
        blocks += [_cols(w_dn[1024 * q:1024 * (q + 1)], (256 * i, 256)) for i in range(4)]
    w_all = np.stack(blocks)
    w_dt = np.tile(w_in[:, dt0:dt0 + HEADS], (1, 4)).reshape(KT, P, P).transpose(1, 0, 2).reshape(P, KT * P)
    x_all = _tiles(np.concatenate([a["x_prompt"].reshape(SEQ, -1), a["x_sample"].reshape(NDEC, -1)]), KT)

    def xbc_order(v, n):
        xs = v[:2048].reshape(GROUPS, 2, P, n)
        bc = [v[s:s + 1024].reshape(GROUPS, 1, P, n) for s in (2048, 3072)]
        return np.concatenate([xs] + bc, axis=1).transpose(2, 0, 1, 3)

    def vec(v):
        return v.reshape(-1, P).T

    par = np.concatenate([
        vec(a["g_mix"][0]), a["conf_dw_w"][0].T.reshape(8, P, CK).transpose(1, 0, 2).reshape(P, -1),
        vec(a["conf_dw_b"][0]), vec(a["conf_ln_g"][0]), vec(a["conf_ln_b"][0]), vec(a["conf_b_pw"][0]),
        xbc_order(a["ssm_conv_w"][0].T, SK).reshape(P, -1),
        xbc_order(a["ssm_conv_b"][0].reshape(-1, 1), 1).reshape(P, -1),
        vec(np.repeat(a["ssm_d"][0], HD)), vec(a["ssm_norm_g"][0]), vec(a["g_ffn"][0]), vec(a["g_final"])], axis=1)
    dt_par = np.stack([np.tile(a["ssm_dt_bias"][0], 4), np.tile(a["ssm_a_log"][0], 4)], axis=1)
    conf_state = a["state_conf_conv"][0].transpose(2, 0, 1).reshape(GROUPS, P, NSEQ * CPRE)
    conv_state = xbc_order(a["state_ssm_conv"][0].transpose(2, 0, 1).reshape(4096, -1), NSEQ * SPRE)        .transpose(1, 0, 2, 3).reshape(GROUPS, P, -1)
    ssm_state = a["state_ssm"][0].reshape(NSEQ, GROUPS, 256, NST).transpose(1, 3, 0, 2).reshape(GROUPS, P, -1)

    nc = bacc.Bacc("TRN2", target_bir_lowering=False, num_devices=1)
    arrays, args = {}, []
    for name, v in [("x_all", x_all), ("w_all", w_all), ("w_dt", w_dt), ("par", par), ("dt_par", dt_par),
                    ("conf_state", conf_state), ("conv_state", conv_state), ("ssm_state", ssm_state)]:
        v = np.ascontiguousarray(v, dtype=np.float32)
        arrays[f"in_{name}"] = v
        args.append(nc.dram_tensor(f"in_{name}", v.shape, F32, kind="ExternalInput").ap())
    for name, shape in [("y", (P, KT * T)), ("conf", (GROUPS, P, CPRE * (NSEQ + 1))),
                        ("conv", (GROUPS, P, 4 * SPRE * (NSEQ + 1))), ("hp", (GROUPS, P, 256)),
                        ("hs", (GROUPS, P, NSEQ * 256))]:
        args.append(nc.dram_tensor(f"out_{name}", shape, F32, kind="ExternalOutput").ap())
    hybrid_layer(nc, *args)
    r = run_bass_kernel_spmd(nc, [arrays], core_ids=[0]).results[0]

    y = r["out_y"].reshape(P, KT, T).transpose(2, 1, 0).reshape(T, D_MODEL)
    conf = r["out_conf"].reshape(D_MODEL, NSEQ + 1, CPRE).transpose(1, 2, 0)
    conv = r["out_conv"].reshape(GROUPS, P, 4, NSEQ + 1, SPRE)
    conv = np.concatenate([conv[:, :, 0:2].transpose(0, 2, 1, 3, 4).reshape(2048, NSEQ + 1, SPRE),
                           conv[:, :, 2].reshape(1024, NSEQ + 1, SPRE),
                           conv[:, :, 3].reshape(1024, NSEQ + 1, SPRE)]).transpose(1, 2, 0)
    hp = r["out_hp"].reshape(GROUPS, NST, HPG, HD).transpose(0, 2, 3, 1).reshape(1, 1, HEADS, HD, NST)
    hs = r["out_hs"].reshape(GROUPS, NST, NSEQ, HPG, HD).transpose(2, 0, 3, 4, 1).reshape(1, NSEQ, HEADS, HD, NST)
    return (y[:SEQ].reshape(1, SEQ, D_MODEL), y[SEQ:].reshape(NSEQ, TDEC, D_MODEL),
            conf[None, 0:1], conv[None, 0:1], hp, conf[None, 1:], conv[None, 1:], hs)
```

```python
from contextlib import ExitStack

import numpy as np

import concourse.bass as bass
from concourse import mybir

F32 = mybir.dt.float32
F32R = mybir.dt.float32r
BF16 = mybir.dt.bfloat16
ALU = mybir.AluOpType
ACT = mybir.ActivationFunctionType
AX = mybir.AxisListType

P = 128
D_MODEL = 1024
KT = D_MODEL // P
SEQ, NSEQ, TDEC = 512, 8, 4
NDEC = NSEQ * TDEC
T = SEQ + NDEC
H2 = T // 2
GROUPS, HPG, HD, NST = 8, 4, 64, 128
HEADS = GROUPS * HPG
CK, SK = 31, 4
CPRE, SPRE = CK - 1, SK - 1
CHUNK = 128
NCH = SEQ // CHUNK
EPS = 1e-6
BW = 256
NBLOCKS = 88
XW = SPRE + SEQ + NSEQ * (SPRE + TDEC)
CW = XW - SPRE
BIG = -1.0e30
REP = 3
B_GROUP, B_GATES, B_SSM, B_PW, B_WOUT, B_FFN = 0, 32, 40, 48, 52, 56
PARAMS = {}
_at = 0
for _name, _n in [("g_mix", 8), ("conf_w", 8 * CK), ("conf_b", 8), ("ln_g", 8), ("ln_b", 8), ("b_pw", 8),
                  ("ssm_w", 32 * SK), ("ssm_b", 32), ("d_skip", 16), ("norm_g", 16), ("g_ffn", 8),
                  ("g_final", 8)]:
    PARAMS[_name] = (_at, _n)
    _at += _n
NPAR = _at


class Steps:

    def __init__(self, eng, sem):
        self.eng, self.sem, self.base, self.n = eng, sem, 0, 0

    def did(self, ins):
        ins.then_inc(self.sem, 1)
        self.n += 1
        return self.n

    def need(self, step):
        self.eng.wait_ge(self.sem, self.base + step)

    def enter(self, i, per):
        self.outer, self.per = self.base + self.n, per
        self.base, self.n = self.outer + i * per, 0

    def leave(self, rounds):
        assert self.n == self.per, f"{self.sem}: the body makes {self.n} steps, {self.per} given"
        self.base, self.n = self.outer + rounds * self.per, 0


def hybrid_layer(nc, x_all, w_all, w_dt, par, dt_par, conf_state, conv_state, ssm_state,
                 y_out, conf_out, conv_out, hp_out, hs_out):
    ctx = ExitStack()
    with ctx:
        def sb(name, shape, dt=F32):
            return ctx.enter_context(nc.sbuf_tensor(name, shape, dt))

        def sem(name):
            return ctx.enter_context(nc.semaphore(name))

        y_dram = nc.dram_tensor("y_scratch", (GROUPS, P, 2, T), F32, kind="Internal").ap()
        cc_dram = nc.dram_tensor("cc_scratch", (GROUPS, P, T), F32, kind="Internal").ap()
        gate_dram = nc.dram_tensor("gate_scratch", (GROUPS, P, 2, T), F32, kind="Internal").ap()

        w_raw = sb("w_raw", [P, 2, KT * BW])
        w_hi = sb("w_hi", [P, 2, KT * BW], F32R)
        w_lo = sb("w_lo", [P, 2, KT * BW], F32R)
        ra_hi = sb("ra_hi", [P, KT, T], F32R)
        ra_lo = sb("ra_lo", [P, KT, T], F32R)
        with nc.sbuf_tensor("dec", [P, 2 * KT * T], F32) as dec:
            pass
        rb_hi = sb("rb_hi", [P, KT, T], F32R)
        rb_lo = sb("rb_lo", [P, KT, T], F32R)
        ident = sb("ident", [P, P])
        ones = sb("ones", [P, P])
        ident_bf = sb("ident_bf", [P, P], BF16)
        mask_bf = sb("mask_bf", [P, P], BF16)
        mask_dec = sb("mask_dec", [NDEC, NDEC], BF16)
        seq_mask = sb("seq_mask", [REP * NDEC, NSEQ])
        sel = sb("sel", [96, HEADS, HD], BF16)
        last_sel = sb("last_sel", [NDEC, NDEC])
        acum_bf = sb("acum_bf", [96, T], BF16)
        dt_nat = sb("dt_nat", [P, NCH + 1, HEADS])
        acum_nat = sb("acum_nat", [P, NCH + 1, HEADS])
        nacum_nat = sb("nacum_nat", [P, NCH + 1, HEADS])
        w_nat = sb("w_nat", [P, NCH + 1, HEADS])
        dtw_nat = sb("dtw_nat", [P, NCH + 1, HEADS])
        exp_last = sb("exp_last", [P, NCH + NSEQ, HEADS])
        pars = sb("pars", [P, NPAR])
        dt_pars = sb("dt_pars", [P, 2])
        a_neg = sb("a_neg", [P, 1])
        eps = sb("eps", [P, 1])
        ln_eps = sb("ln_eps", [P, 1])
        cc_sum = sb("cc_sum", [P, T])
        d_cur = sb("d_cur", [P, 4, P // NDEC, NDEC])[:, :, :, :]
        d_z = sb("d_z", [P, 2, NDEC])[:, :, :]
        d_wr = sb("d_wr", [REP * NDEC, HPG * HD], F32R)
        d_br = sb("d_br", [REP * NDEC, P], F32R)
        d_bm = sb("d_bm", [REP * NDEC, NSEQ, P], F32R)
        ARENA = 16972
        arena = sb("arena", [P, ARENA])

        def views(*fields, at=0, space=arena, size=ARENA):
            out = []
            for shape in fields:
                n = int(np.prod(shape))
                v = space[:, at:at + n]
                if len(shape) == 2:
                    v = v.rearrange("p (a b) -> p a b", b=shape[1])
                elif len(shape) == 3:
                    v = v.rearrange("p (a b c) -> p a b c", b=shape[1], c=shape[2])
                out.append(v)
                at += n
            assert at <= size, at
            return out, at

        (raw, acc, sil, zs, zh, gx, gd, conv_a, conv_b, ccs, cstate, cout, sstate, sout), ssd_at = views(
            (4, XW), (4, XW), (4, XW), (2, T), (2, T), (CPRE + SEQ,),
            (NSEQ, CPRE + TDEC), (SEQ,), (SEQ,), (T,), (NSEQ, CPRE), (CPRE * (NSEQ + 1),),
            (4, NSEQ, SPRE), (4, SPRE * (NSEQ + 1)))
        raw_d, sil_d = (x[:, :, SPRE + SEQ:XW].rearrange("p a (b t) -> p a b t", b=NSEQ)
                        for x in (raw, sil))
        sil_d = sil_d[:, :, :, 0:TDEC]
        (h_t, xdt, wxdt, b_nat, scores, decay, m_t, y_tmp, e_acc, y_sb), _ = views(
            (HPG * HD,), (HPG * HD,), (HPG * HD,), (P,), (P,), (HPG, P), (HPG, P), (2, P), (2, SEQ), (2, T),
            at=ssd_at)
        d_ssum = e_acc.rearrange("p j n -> p (j n)")[:, 0:T]
        (st, d_sq, d_xdt, d_wxdt, d_bn, d_sc, d_decay, d_m, d_e, d_tmp), _ = views(
            (NSEQ, 256), (2, T), (256,), (256,), (P,), (NDEC,), (HPG, NDEC), (HPG, NDEC), (2, NDEC), (2, NDEC),
            space=dec, size=2 * KT * T, at=KT * T)
        (d_rstd,), _ = views((T,), space=dec, size=KT * T)
        d_yn = d_sq
        (x_t, sq0, ssum0, rstd0, xn0), norm_end = views((KT, T), (2, T), (T,), (T,), (2, T))
        assert norm_end + 1024 <= ssd_at
        wdt_raw = arena[:, norm_end:norm_end + 1024]
        (dt_v, dt_e, dt_z, dt_z2, dt_p, dt_r, dt_t, scan_keep), _ = views(*[(T,)] * 8, at=ssd_at)
        (gates_sb,), _ = views((2, T))
        (y_ld,), b_at = views((2, 2 * T), at=4 * XW)
        y_ld = y_ld.rearrange("p a (j t) -> p a j t", j=2)
        (b_sum, xc, l_sq), ln_at = views((KT, T), (KT, T), (2, T), at=b_at)
        (l_mean, l_ssum, l_rstd, pw_m), _ = views((T,), (T,), (T,), (2, T), at=ln_at)
        g_in, pw_a = y_ld, l_sq
        (x_in,), _ = views((2, T), at=ln_at)
        (h_sb, o_sq, o_ssum, o_rstd, f_r, f_v, f_s), _ = views(
            (KT, T), (2, T), (T,), (T,), (2, T), (2, T), (2, T))

        psum = [ctx.enter_context(nc.psum_tensor(f"main{s}", [P, 2, 512], F32)) for s in range(2)]
        pt = ctx.enter_context(nc.psum_tensor("pt", [P, 512], F32))
        ps = ctx.enter_context(nc.psum_tensor("ps", [P, 512], F32))
        py = ctx.enter_context(nc.psum_tensor("py", [P, 512], F32))
        ph = ctx.enter_context(nc.psum_tensor("ph", [P, 512], F32))

        def main(t):
            return psum[t % 2][:, :, 0:H2]

        def halves(ap):
            return ap.rearrange("p (a b) -> p a b", a=2)

        def par1(name, i, n=1):
            at, _ = PARAMS[name]
            return pars[:, bass.ds(at + i, n)]

        def fr(ap):
            return ap.bitcast(F32)

        w_in = [sem(f"w_in{s}") for s in range(2)]
        w_hi_s = sem("w_hi_s")
        w_lo_s = sem("w_lo_s")
        tile_done = sem("tile_done")
        tile_free = [sem(f"tile_free{s}") for s in range(2)]
        act_c = sem("act_c")
        dve_c = sem("dve_c")
        pool_c = sem("pool_c")
        pool_passed = sem("pool_passed")
        const_s = sem("const_s")
        par_s = sem("par_s")
        par_ready = sem("par_ready")
        x_in_s = [sem(f"x_in_s{s}") for s in range(4)]
        n_sq = sem("n_sq")
        n_sum = sem("n_sum")
        n_stat = sem("n_stat")
        n_rstd = sem("n_rstd")
        n_xn = sem("n_xn")
        u_hi_s = sem("u_hi_s")
        u_ready = sem("u_ready")
        wdt_in = sem("wdt_in")
        wdt_hi_s = sem("wdt_hi_s")
        wdt_ready = sem("wdt_ready")
        dt_psum = sem("dt_psum")
        dt_act = sem("dt_act")
        dt_dve = sem("dt_dve")
        acum_ready = sem("acum_ready")
        nat_t = sem("nat_t")
        nat_copied = sem("nat_copied")
        nat_b = sem("nat_b")
        nat_diff = sem("nat_diff")
        nat_exp = sem("nat_exp")
        nat_ready = sem("nat_ready")
        rep_s = sem("rep_s")
        sstate_in = sem("sstate_in")
        sstate_used = sem("sstate_used")
        raw_ready = sem("raw_ready")
        conv4_s = sem("conv4_s")
        sil_ready = sem("sil_ready")
        z_ready = sem("z_ready")
        dec_saved = sem("dec_saved")
        glu_ready = sem("glu_ready")
        cstate_in = sem("cstate_in")
        cpre_ready = sem("cpre_ready")
        conv01_s = sem("conv01_s")
        cc_ready = sem("cc_ready")
        cc_free = sem("cc_free")
        cc_added = sem("cc_added")
        cc_st = sem("cc_st")
        cout_copied = sem("cout_copied")
        cout_st = sem("cout_st")
        sout_copied = sem("sout_copied")
        sout_st = sem("sout_st")
        pt_done = sem("pt_done")
        ps_done = sem("ps_done")
        e_psum = sem("e_psum")
        e_ready = sem("e_ready")
        decay_ready = sem("decay_ready")
        xb_ready = sem("xb_ready")
        m_ready = sem("m_ready")
        ys_done = sem("ys_done")
        h_ready = sem("h_ready")
        y_done = sem("y_done")
        ssd_free = sem("ssd_free")
        ssd_st = sem("ssd_st")
        st_in = sem("st_in")
        d_off = sem("d_off")
        d_pt = sem("d_pt")
        d_ps = sem("d_ps")
        d_w_s = sem("d_w_s")
        d_hi_s = sem("d_hi_s")
        d_lo_s = sem("d_lo_s")
        d_bn_s = sem("d_bn_s")
        d_dec_s = sem("d_dec_s")
        d_m_s = sem("d_m_s")
        d_y = sem("d_y")
        d_add = sem("d_add")
        d_r3 = sem("d_r3")
        st_ready = sem("st_ready")
        st_st = sem("st_st")
        d_ycur = sem("d_ycur")
        d_sq_s = sem("d_sq_s")
        d_ssum_s = sem("d_ssum_s")
        d_stat = sem("d_stat")
        y_ln_s = sem("y_ln_s")
        d_rstd_s = sem("d_rstd_s")
        d_yn_s = sem("d_yn_s")
        yn_st = sem("yn_st")
        gates_st = [sem(f"gates_st{s}") for s in range(2)]
        y_in = [sem(f"y_in{s}") for s in range(2)]
        ys_hi = sem("ys_hi")
        ys_ready = sem("ys_ready")
        cc_in = sem("cc_in")
        l_stat = sem("l_stat")
        l_mean_s = sem("l_mean_s")
        l_xc = sem("l_xc")
        l_sq_s = sem("l_sq_s")
        l_ssum_s = sem("l_ssum_s")
        l_stat2 = sem("l_stat2")
        l_rstd_s = sem("l_rstd_s")
        l_t = sem("l_t")
        l_sil = sem("l_sil")
        cc_hi_s = sem("cc_hi_s")
        cc_split = sem("cc_split")
        g_in_s = [sem(f"g_in_s{s}") for s in range(2)]
        p_m = sem("p_m")
        mg_hi = sem("mg_hi")
        mg_ready = sem("mg_ready")
        x_in2 = [sem(f"x_in2{s}") for s in range(2)]
        o_act = sem("o_act")
        o_sum_s = sem("o_sum_s")
        hn_ready = sem("hn_ready")
        o_stat = sem("o_stat")
        o_rstd_s = sem("o_rstd_s")
        f_v_s = sem("f_v_s")
        f_sq_s = sem("f_sq_s")
        f_hi = sem("f_hi")
        f_ready = sem("f_ready")
        z_sq = sem("z_sq")
        z_sum = sem("z_sum")
        z_stat = sem("z_stat")
        z_rstd = sem("z_rstd")
        z_y = sem("z_y")
        out_st = sem("out_st")

        block = ctx.enter_context(nc.Block())

        @block.sync
        def _(sp):
            part = KT // 4
            for i in range(4):
                sp.dma_start(x_t[:, i * part:(i + 1) * part, :],
                             x_all[:, i * part * T:(i + 1) * part * T]
                             .rearrange("p (k t) -> p k t", t=T)).then_inc(x_in_s[i], 16)
            sp.dma_start(wdt_raw, w_dt).then_inc(wdt_in, 16)
            sp.dma_start(pars[:, :], par).then_inc(par_s, 16)
            sp.dma_start(dt_pars[:, :], dt_par).then_inc(par_s, 16)
            sp.dma_start(w_raw[:, 0, :], w_all[0]).then_inc(w_in[0], 16)
            sp.dma_start(w_raw[:, 1, :], w_all[1]).then_inc(w_in[1], 16)
            with sp.Fori(1, NBLOCKS // 2) as i:
                for s in range(2):
                    sp.wait_ge(w_lo_s, 2 * i + (s - 1))
                    sp.dma_start(w_raw[:, s, :], w_all[bass.ds(2 * i + s, 1), :, :]
                                 .rearrange("a p n -> p (a n)")).then_inc(w_in[s], 16)

            for m in range(KT):
                sp.wait_ge(z_y, m + 1)
                sp.dma_start(y_out[:, m * T:(m + 1) * T], h_sb[:, m, :]).then_inc(out_st, 16)
            sp.wait_ge(out_st, 16 * KT)

        @block.gpsimd
        def _(pool):
            st_c = Steps(pool, pool_c)
            st_c.did(pool.memset(ident[:, :], 0.0))
            st_c.did(pool.memset(mask_bf[:, :], 0.0))
            st_c.did(pool.memset(mask_dec[:, :], 0.0))
            st_c.did(pool.memset(seq_mask[0:NDEC, :], 1.0))
            pool.memset(ones[:, :], 1.0).then_inc(const_s, 1)
            pool.memset(eps[:, :], EPS).then_inc(const_s, 1)
            st_c.did(pool.memset(scan_keep, 1.0))
            st_c.need(5)
            st_c.did(pool.memset(scan_keep[:, 0:SEQ:CHUNK], 0.0))
            pool.memset(scan_keep[:, SEQ:T:TDEC], 0.0).then_inc(const_s, 1)
            n = st_c.did(pool.affine_select(out=ident[:, :], in_=ident[:, :], compare_op=ALU.not_equal, fill=1.0,
                                            base=0, pattern=[[-1, P]], channel_multiplier=1))
            st_c.did(pool.affine_select(out=mask_bf[:, :], in_=mask_bf[:, :], compare_op=ALU.is_ge, fill=BIG,
                                        base=0, pattern=[[1, P]], channel_multiplier=-1))
            st_c.need(n)
            m = st_c.did(pool.tensor_copy(ident_bf[:, :], ident[:, :]))
            dec3 = mask_dec[:, :].rearrange("s (b t) -> s b t", t=TDEC)
            m = st_c.did(pool.affine_select(out=mask_dec[:, :], in_=mask_dec[:, :], compare_op=ALU.is_ge, fill=BIG,
                                            base=0, pattern=[[1, NDEC]], channel_multiplier=-1))
            st_c.need(m)
            m = st_c.did(pool.affine_select(out=dec3, in_=dec3, compare_op=ALU.is_ge, fill=BIG, base=TDEC - 1,
                                            pattern=[[TDEC, NSEQ], [0, TDEC]], channel_multiplier=-1))
            st_c.need(m)
            st_c.did(pool.affine_select(out=dec3, in_=dec3, compare_op=ALU.is_ge, fill=BIG, base=0,
                                        pattern=[[-TDEC, NSEQ], [0, TDEC]], channel_multiplier=1))
            m = st_c.did(pool.affine_select(out=seq_mask[0:NDEC, :], in_=seq_mask[0:NDEC, :], compare_op=ALU.is_ge, fill=0.0,
                                            base=TDEC - 1, pattern=[[TDEC, NSEQ]], channel_multiplier=-1))
            st_c.need(m)
            st_c.did(pool.affine_select(out=seq_mask[0:NDEC, :], in_=seq_mask[0:NDEC, :], compare_op=ALU.is_ge, fill=0.0,
                                        base=0, pattern=[[-TDEC, NSEQ]], channel_multiplier=1))
            st_c.did(pool.tensor_copy(last_sel[:, :].rearrange("s (b t) -> s b t", t=TDEC),
                                      ident[0:NDEC, TDEC - 1:NDEC:TDEC].unsqueeze(2)
                                      .broadcast_to([NDEC, NSEQ, TDEC])))
            m = st_c.did(pool.memset(sel[:, :, :], 0.0))
            for part in range(3):
                st_c.need(m)
                m = st_c.did(pool.affine_select(out=sel[:, :, :], in_=sel[:, :, :], compare_op=ALU.not_equal,
                                                fill=1.0, base=-HEADS * part, pattern=[[-1, HEADS], [0, HD]],
                                                channel_multiplier=1))
            pool.memset(cc_sum[:, :], 0.0).then_inc(const_s, 1)
            pool.wait_ge(u_ready, KT)
            pool.memset(raw[:, :, 0:SPRE], 0.0).then_inc(const_s, 1)
            pool.memset(gx[:, 0:CPRE], 0.0).then_inc(const_s, 1)

            def held(s, value):
                pool.wait_ge(s, value)
                pool.sem_inc(pool_passed, 1)

            def load_conv_state(g):
                pool.dma_start(sstate.rearrange("p a b c -> p (a b c)"),
                               conv_state[bass.ds(g, 1), :, :].rearrange("a p n -> p (a n)"))\
                    .then_inc(sstate_in, 16)

            def load_conf_state(g):
                pool.dma_start(cstate.rearrange("p a b -> p (a b)"),
                               conf_state[bass.ds(g, 1), :, :].rearrange("a p n -> p (a n)"))\
                    .then_inc(cstate_in, 16)

            def conf_prefix(g):
                held(cstate_in, 16 * g + 16)
                pool.tensor_copy(gd[:, :, 0:CPRE], cstate).then_inc(cpre_ready, 1)
                held(cpre_ready, g + 1)

            def save_conv_state(g):
                held(raw_ready, 4 * g + 4)
                pool.tensor_copy(sout[:, :, 0:SPRE], raw[:, :, SEQ:SEQ + SPRE])
                pool.tensor_copy(sout[:, :, SPRE:].rearrange("p a (b c) -> p a b c", c=SPRE),
                                 raw_d[:, :, :, TDEC:TDEC + SPRE]).then_inc(sout_copied, 1)
                pool.wait_ge(sout_copied, g + 1)
                pool.dma_start(conv_out[bass.ds(g, 1), :, :].rearrange("a p n -> p (a n)"),
                               sout.rearrange("p a b -> p (a b)")).then_inc(sout_st, 16)

            def save_conf_state(g):
                held(glu_ready, g + 1)
                pool.tensor_copy(cout[:, 0:CPRE], gx[:, SEQ:SEQ + CPRE])
                pool.tensor_copy(cout[:, CPRE:].rearrange("p (b c) -> p b c", c=CPRE),
                                 gd[:, :, TDEC:TDEC + CPRE]).then_inc(cout_copied, 1)
                pool.wait_ge(cout_copied, g + 1)
                pool.dma_start(conf_out[bass.ds(g, 1), :, :].rearrange("a p n -> p (a n)"), cout)\
                    .then_inc(cout_st, 16)

            def add_cc(p):
                pool.wait_ge(cc_ready, p + 1)
                pool.dma_start(cc_dram[bass.ds(p, 1), :, :].rearrange("a p n -> p (a n)"), ccs).then_inc(cc_st, 16)
                pool.tensor_tensor(cc_sum[:, :], cc_sum[:, :], ccs, ALU.add).then_inc(cc_added, 1)
                pool.wait_ge(cc_added, p + 1)
                pool.wait_ge(cc_st, 16 * p + 16)
                pool.sem_inc(cc_free, 1)

            def load_states(p):
                pool.dma_start(st.rearrange("p b n -> p (b n)"),
                               ssm_state[bass.ds(p, 1), :, :].rearrange("a p n -> p (a n)")).then_inc(st_in, 16)

            def store_hp(p):
                pool.wait_ge(y_done, p + 1)
                pool.dma_start(hp_out[bass.ds(p, 1), :, :].rearrange("a p n -> p (a n)"), h_t).then_inc(ssd_st, 16)

            def store_states(p):
                pool.wait_ge(st_ready, p + 1)
                pool.dma_start(hs_out[bass.ds(p, 1), :, :].rearrange("a p n -> p (a n)"),
                               st.rearrange("p b n -> p (b n)")).then_inc(st_st, 16)

            def store_yn(p):
                pool.wait_ge(d_yn_s, p + 1)
                pool.dma_start(y_dram[bass.ds(p, 1), :, :, :].rearrange("a p j n -> p (a j) n"), d_yn)\
                    .then_inc(yn_st, 16)

            pool.sem_inc(cc_free, 1)
            pool.sem_inc(ssd_free, 1)
            load_conv_state(0)
            load_conf_state(0)
            pool.wait_ge(dt_psum, 1)
            load_states(0)
            conf_prefix(0)
            save_conv_state(0)

            def conv_out_of(p):
                add_cc(p)
                conf_prefix(p + 1)

            def states_out_of(p):
                store_states(p)
                store_yn(p)
                pool.wait_ge(st_st, 16 * (p + 1))
                pool.wait_ge(yn_st, 16 * (p + 1))
                load_states(p + 1)

            def saves(g):
                save_conf_state(g - 1)
                pool.wait_ge(sout_st, 16 * g)
                store_hp(g - 1)
                save_conv_state(g)
                pool.wait_ge(ssd_st, 16 * g)
                pool.sem_inc(ssd_free, 1)

            load_conv_state(1)
            load_conf_state(1)
            pool.wait_ge(nat_ready, 1)
            for rep in range(1, REP):
                rows = slice(rep * NDEC, (rep + 1) * NDEC)
                pool.dma_start(dtw_nat[rows, NCH, :], dtw_nat[0:NDEC, NCH, :]).then_inc(rep_s, 16)
                pool.dma_start(seq_mask[rows, :], seq_mask[0:NDEC, :]).then_inc(rep_s, 16)
            saves(1)
            with pool.Fori(2, GROUPS) as g:
                load_conv_state(g)
                conv_out_of(g - 2)
                load_conf_state(g)
                states_out_of(g - 2)
                pool.wait_ge(cout_st, 16 * (g - 1))
                saves(g)
            conv_out_of(GROUPS - 2)
            states_out_of(GROUPS - 2)
            pool.wait_ge(cout_st, 16 * (GROUPS - 1))
            save_conf_state(GROUPS - 1)

            def store_gates(i):
                for m in range(2):
                    pool.wait_ge(tile_free[m], B_GATES + i + 1)
                    pool.dma_start(gate_dram[i][:, m, :], gates_sb[:, m, :]).then_inc(gates_st[m], 16)

            def load_yn(i):
                pool.dma_start(y_ld[:, i % 2, :, :], y_dram[i]).then_inc(y_in[i % 2], 16)

            def load_cc():
                for s_out in (ssd_st, st_st, cc_st, cout_st, sout_st):
                    pool.wait_ge(s_out, 16 * GROUPS)
                for i in range(2):
                    pool.dma_start(xc[:, 4 * i:4 * i + 4, :], cc_dram[4 * i:4 * i + 4].rearrange("a p n -> p a n"))\
                        .then_inc(cc_in, 16)

            for i in range(3):
                store_gates(i)
            store_hp(GROUPS - 1)
            store_gates(3)
            store_states(GROUPS - 1)
            pool.wait_ge(sil_ready, 4 * GROUPS)
            load_yn(0)
            load_yn(1)
            store_yn(GROUPS - 1)
            add_cc(GROUPS - 1)
            pool.wait_ge(yn_st, 16 * GROUPS)
            for i in range(2, GROUPS):
                if i == 4:
                    load_cc()
                if i + 2 < GROUPS:
                    store_gates(i + 2)
                pool.wait_ge(ys_ready, 2 * (i - 1))
                load_yn(i)
            for m in range(2):
                pool.wait_ge(gates_st[m], 16 * GROUPS)

            pool.wait_ge(ys_ready, 2 * GROUPS)
            for m in range(KT):
                if m >= 2:
                    pool.wait_ge(p_m, 3 * (m - 1))
                pool.dma_start(g_in[:, m % 2, :, :], gate_dram[m]).then_inc(g_in_s[m % 2], 16)
            for m in range(KT):
                if m >= 2:
                    pool.wait_ge(tile_free[m % 2], B_WOUT + (m - 2) // 2 + 1)
                pool.dma_start(x_in[:, m % 2, :], x_all[:, m * T:(m + 1) * T]).then_inc(x_in2[m % 2], 16)
        @block.tensor
        def _(pe):
            def fill(b, rhs_hi, rhs_lo, t0, m0=0, m1=2, between=None):
                bs, be, count = b
                for m in range(m0, m1):
                    t = t0 + m
                    if m == 0:
                        pe.wait_ge(w_lo_s, be + 1)
                    if count(t) is not None:
                        pe.wait_ge(tile_free[t % 2], count(t))
                    for hf in range(2):
                        for k in range(KT):
                            if between:
                                between(hf * KT + k)
                            at = k * BW + m * P
                            for j, (w, x) in enumerate(((w_hi, rhs_hi), (w_hi, rhs_lo), (w_lo, rhs_hi))):
                                last = pe.matmul(psum[t % 2][:, hf, 0:H2], w[:, bs, at:at + P],
                                                 x[:, k, hf * H2:(hf + 1) * H2],
                                                 start=(k == 0 and j == 0), stop=(k == KT - 1 and j == 2))
                    last.then_inc(tile_done, 1)

            def fill_late(b, rhs_hi, rhs_lo, ready, base, between=None):
                bs, be, count = b
                pe.wait_ge(w_lo_s, be + 1)
                for ks in (range(KT - 2), range(KT - 2, KT)):
                    pe.wait_ge(ready, base + ks.stop)
                    if between and ks.start:
                        between()
                    for m in range(2):
                        if not ks.start:
                            pe.wait_ge(tile_free[m], count(m))
                        for hf in range(2):
                            for k in ks:
                                at = k * BW + m * P
                                for j, (w, x) in enumerate(((w_hi, rhs_hi), (w_hi, rhs_lo), (w_lo, rhs_hi))):
                                    last = pe.matmul(psum[m][:, hf, 0:H2], w[:, bs, at:at + P],
                                                     x[:, k, hf * H2:(hf + 1) * H2],
                                                     start=(k == 0 and j == 0), stop=(k == KT - 1 and j == 2),
                                                     skip_group_check=True)
                        if ks.start:
                            last.then_inc(tile_done, 1)

            def blk(slot, b):
                return slot, b, (lambda t: b) if not (isinstance(b, int) and b == 0) else (lambda t: None)

            pe.wait_ge(const_s, 1)
            pe.wait_ge(n_sum, KT)
            for hf in range(2):
                last = pe.matmul(psum[0][:, hf, 0:H2], ones[:, :], ssum0[:, hf * H2:(hf + 1) * H2],
                                 start=True, stop=True)
            last.then_inc(n_stat, 1)
            pe.wait_ge(wdt_ready, 1)
            pe.wait_ge(n_rstd, 1)
            wdt_hi, wdt_lo = (x[:, :, :].rearrange("p k t -> p (k t)") for x in (rb_hi, rb_lo))
            for k in range(KT):
                pe.wait_ge(u_ready, k + 1)
                for hf in range(2):
                    for j, (w, x) in enumerate(((wdt_hi, ra_hi), (wdt_hi, ra_lo), (wdt_lo, ra_hi))):
                        last = pe.matmul(psum[0][:, hf, 0:H2], w[:, k * P:(k + 1) * P],
                                         x[:, k, hf * H2:(hf + 1) * H2],
                                         start=(k == 0 and j == 0), stop=(k == KT - 1 and j == 2))
            last.then_inc(dt_psum, 1)

            def pick_head(p, h):
                return sel[:, bass.ds(4 * p + h, 1), 0:1].rearrange("r a b -> r (a b)").broadcast_to([96, P])

            def pick_pair(p, j):
                return sel[:, bass.ds(4 * p + 2 * j, 2), :].rearrange("r a b -> r (a b)")

            def ssd_e(p):
                pe.wait_ge(glu_ready, p + 1)
                for j, bank in enumerate((ph, py)):
                    pe.matmul(bank[:, :], pick_pair(p, j), acum_bf[:, 0:SEQ],
                              start=True, stop=True).then_inc(e_psum, 1)

            def ssd_1(c, p):
                cs = slice(c * CHUNK, (c + 1) * CHUNK)
                if c == 0:
                    pe.wait_ge(sil_ready, 4 * p + 4)
                    pe.wait_ge(dec_saved, p + 1)
                    pe.wait_ge(nat_ready, 1)
                for j in range(3):
                    pe.transpose(pt[:, j * P:(j + 1) * P], sil[:, j, cs], ident[:, :])
                pe.matmul(pt[:, 3 * P:4 * P], sil[:, 2, cs], sil[:, 3, cs], start=True, stop=True)\
                    .then_inc(pt_done, 1)
                for h in range(HPG):
                    pe.matmul(ps[:, h * P:(h + 1) * P], pick_head(p, h), acum_bf[:, cs],
                              start=(h == 0), stop=False, skip_group_check=True)
                pe.matmul(ps[:, :], ident_bf[:, :], mask_bf[:, :].unsqueeze(1).broadcast_to([P, HPG, P]),
                          start=False, stop=True, skip_group_check=True).then_inc(ps_done, 1)

            def ssd_2(c, p):
                cs = slice(c * CHUNK, (c + 1) * CHUNK)
                if c == 0:
                    pe.wait_ge(e_ready, p + 1)
                pe.wait_ge(m_ready, NCH * p + c + 1)
                pe.wait_ge(xb_ready, NCH * p + c + 1)
                if c:
                    pe.wait_ge(h_ready, NCH * p + c)
                for h in range(HPG):
                    pe.matmul(py[(h % 2) * HD:(h % 2 + 1) * HD, (h // 2) * P:(h // 2 + 1) * P],
                              xdt[:, h * HD:(h + 1) * HD], m_t[:, h, :], start=True, stop=True,
                              skip_group_check=True)
                if c:
                    for j in range(2):
                        pe.matmul(py[:, 256 + j * P:256 + (j + 1) * P], h_t[:, j * P:(j + 1) * P], sil[:, 3, cs],
                                  start=True, stop=True, skip_group_check=True)
                pe.matmul(ph[:, 0:256], b_nat, wxdt, start=True, stop=True).then_inc(ys_done, 1)

            OFF_FROM, E_AT = 6, KT - 1

            def decode_wait(g):
                pe.wait_ge(dec_saved, g + 1)
                pe.wait_ge(st_in, 16 * g + 16)
                pe.wait_ge(h_ready, NCH * g + NCH)

            def decode_off(n):
                j, b = n // NSEQ, n % NSEQ
                return pe.matmul(py[:, 64 + j * NDEC + TDEC * b:64 + j * NDEC + TDEC * (b + 1)],
                                 st[:, b, j * P:(j + 1) * P], d_cur[:, 3, 0, TDEC * b:TDEC * (b + 1)],
                                 start=True, stop=True, skip_group_check=True)

            def decode_in(g):
                for n in range(2 * KT - OFF_FROM, 2 * NSEQ):
                    last = decode_off(n)
                last.then_inc(d_off, 1)
                for j in range(3):
                    pe.transpose(pt[:, j * P:(j + 1) * P], d_cur[:, j, :, :].rearrange("p a n -> p (a n)"), ident[:, :])
                pe.matmul(pt[0:NDEC, 384:384 + NDEC], d_cur[:, 2, 0, :], d_cur[:, 3, 0, :], start=True, stop=True)\
                    .then_inc(d_pt, 1)
                for h in range(HPG):
                    pe.matmul(ps[:, h * NDEC:(h + 1) * NDEC], pick_head(g, h),
                              acum_bf[:, SEQ:T], start=(h == 0), stop=False, skip_group_check=True)
                pe.matmul(ps[:, 0:HPG * NDEC], ident_bf[0:NDEC, :],
                          mask_dec[:, :].unsqueeze(1).broadcast_to([NDEC, HPG, NDEC]), start=False, stop=True,
                          skip_group_check=True)
                for j in range(2):
                    last = pe.matmul(ps[:, 128 + j * NDEC:128 + (j + 1) * NDEC],
                                     pick_pair(g, j), acum_bf[:, SEQ:T],
                                     start=True, stop=True, skip_group_check=True)
                last.then_inc(d_ps, 1)

            def decode_add(bank, r):
                for b in range(2):
                    last = pe.matmul(bank[:, b * 256:(b + 1) * 256], d_bm[:, 2 * r + b, :], d_wr[:, :],
                                     start=True, stop=True, skip_group_check=True)
                return last

            def decode_mid(g):
                pe.wait_ge(d_m_s, g + 1)
                pe.wait_ge(d_bn_s, g + 1)
                for h in range(HPG):
                    pe.matmul(py[(h % 2) * HD:(h % 2 + 1) * HD, (h // 2) * NDEC:(h // 2 + 1) * NDEC],
                              d_xdt[0:NDEC, h * HD:(h + 1) * HD], d_m[0:NDEC, h, :], start=True, stop=True,
                              skip_group_check=True)
                for r, bank in enumerate((ph, ps, pt)):
                    last = decode_add(bank, r)
                last.then_inc(d_y, 1)

            def decode_end(g):
                pe.wait_ge(d_add, 3 * g + 1)
                decode_add(ph, 3).then_inc(d_r3, 1)
                pe.wait_ge(d_ssum_s, g + 1)
                pe.matmul(ps[:, :], ones[:, :], d_ssum[:, 0:SEQ], start=True, stop=True)
                pe.matmul(pt[:, 0:NDEC], ones[:, :], d_ssum[:, SEQ:T], start=True, stop=True).then_inc(d_stat, 1)

            def group(g, ssd):
                p = g - 1

                def spread_e(n):
                    if n == E_AT:
                        ssd_e(p)

                def spread_off(n):
                    if n == OFF_FROM:
                        decode_wait(p)
                    if n >= OFF_FROM:
                        decode_off(n - OFF_FROM)

                if ssd:
                    ssd_1(0, p)
                for j in range(4):
                    for m in range(2):
                        if not ssd and j == 0 and m == 0:
                            pe.wait_ge(dt_act, 1)
                        fill(blk(j % 2, 4 * g + j), ra_hi, ra_lo, 0, m, m + 1,
                             between={(0, 0): spread_e, (2, 0): spread_off}.get((j, m)) if ssd else None)
                        if ssd and j < 2:
                            c = 2 * j + m
                            ssd_2(c, p)
                            if c < NCH - 1:
                                ssd_1(c + 1, p)
                        elif ssd and (j, m) == (2, 0):
                            decode_in(p)
                        elif ssd and (j, m) == (2, 1):
                            decode_mid(p)
                        elif ssd and (j, m) == (3, 0):
                            decode_end(p)

            group(0, False)
            pe.wait_ge(acum_ready, 1)
            pe.wait_ge(const_s, 4)
            for q, src in enumerate((dt_r, dt_t)):
                for c in range(NCH + 1):
                    n = CHUNK if c < NCH else NDEC
                    last = pe.transpose(ps[0:n, (q * (NCH + 1) + c) * HEADS:(q * (NCH + 1) + c + 1) * HEADS],
                                        src[0:HEADS, c * CHUNK:c * CHUNK + n], ident[0:HEADS, 0:HEADS])
            last.then_inc(nat_t, 1)
            pe.wait_ge(nat_copied, 2)
            pe.matmul(py[:, 0:NCH * HEADS], ident[:, P - 1:P].broadcast_to([P, P]),
                      acum_nat[:, 0:NCH, :], start=True, stop=True)
            for b in range(NSEQ):
                last_tok = TDEC * b + TDEC - 1
                pe.matmul(py[:, (NCH + b) * HEADS:(NCH + b + 1) * HEADS],
                          ident[0:NDEC, last_tok:last_tok + 1].broadcast_to([NDEC, P]),
                          acum_nat[0:NDEC, NCH, :], start=True, stop=True)
            pe.matmul(ph[0:NDEC, 0:HEADS],
                      last_sel[:, :],
                      acum_nat[0:NDEC, NCH, :], start=True, stop=True).then_inc(nat_b, 1)
            with pe.Fori(1, GROUPS) as g:
                group(g, True)
            group(GROUPS, True)
            with pe.Fori(2, 4) as i:
                for s in range(2):
                    fill(blk(s, B_GATES + 2 * i + s), ra_hi, ra_lo, 0)
            pe.wait_ge(cc_added, GROUPS)
            pe.wait_ge(d_rstd_s, GROUPS)
            for hf, bank in enumerate((pt, ps)):
                last = pe.matmul(bank[:, 0:H2], ones[:, :], cc_sum[:, hf * H2:(hf + 1) * H2],
                                 start=True, stop=True)
            last.then_inc(l_stat, 1)
            fill_late(blk(0, B_SSM), rb_hi, rb_lo, ys_ready, 0)
            for i in range(1, 4):
                fill(blk(i % 2, B_SSM + i), rb_hi, rb_lo, 0)
            fill_late(blk(0, B_SSM + 4), ra_hi, ra_lo, ys_ready, KT)
            pe.wait_ge(l_ssum_s, KT)
            for hf, bank in enumerate((py, ph)):
                last = pe.matmul(bank[:, 0:H2], ones[:, :], l_ssum[:, hf * H2:(hf + 1) * H2],
                                 start=True, stop=True)
            last.then_inc(l_stat2, 1)
            for i in range(1, 4):
                fill(blk(i % 2, B_SSM + 4 + i), ra_hi, ra_lo, 0)
            fill_late(blk(0, B_PW), rb_hi, rb_lo, cc_split, 0)
            for i in range(1, 4):
                fill(blk(i % 2, B_PW + i), rb_hi, rb_lo, 0)
            fill_late(blk(0, B_WOUT), ra_hi, ra_lo, mg_ready, 0)
            for i in range(1, 4):
                fill(blk(i % 2, B_WOUT + i), ra_hi, ra_lo, 0)

            def ffn_stat():
                pe.wait_ge(o_sum_s, KT)
                for hf, bank in enumerate((pt, ps)):
                    last = pe.matmul(bank[:, 0:H2], ones[:, :], o_ssum[:, hf * H2:(hf + 1) * H2],
                                     start=True, stop=True)
                last.then_inc(o_stat, 1)

            def quarter(i, first):
                b = B_FFN + 8 * i
                if first:
                    fill_late(blk(0, b), rb_hi, rb_lo, hn_ready, 0, ffn_stat)
                else:
                    fill(blk(0, b), rb_hi, rb_lo, 0)
                for j in range(1, 4):
                    fill(blk(j % 2, b + j), rb_hi, rb_lo, 0)
                fill_late(blk(0, b + 4), ra_hi, ra_lo, f_ready, KT * i)
                for j in range(1, 4):
                    fill(blk(j % 2, b + 4 + j), ra_hi, ra_lo, 0)

            quarter(0, True)
            with pe.Fori(1, 4) as i:
                quarter(i, False)
            for n, sq in enumerate((o_ssum, o_sq[:, (KT - 1) % 2, :])):
                pe.wait_ge((z_sum, z_sq)[n], (KT - 1, KT)[n])
                for hf, bank in enumerate((py, ph)):
                    last = pe.matmul(bank[:, 0:H2], ones[:, :], sq[:, hf * H2:(hf + 1) * H2],
                                     start=(n == 0), stop=(n == 1))
            last.then_inc(z_stat, 1)

        @block.scalar
        def _(act):
            steps = Steps(act, act_c)

            def hi(b, s, turn):
                act.wait_ge(w_in[s], 16 * turn + 16)
                if not isinstance(b, int) or b >= 2:
                    act.wait_ge(tile_done, 2 * b - 2)
                act.activation(w_hi[:, s, :], w_raw[:, s, :], ACT.Copy).then_inc(w_hi_s, 1)

            def hi_next(pair, s):
                if s == 0:
                    hi(2 * pair + 1, 1, pair)
                else:
                    hi(2 * pair + 2, 0, pair + 1)

            for k in range(KT):
                act.wait_ge(x_in_s[4 * k // KT], 16)
                if k >= 2:
                    act.wait_ge(n_sum, k - 1)
                act.activation(sq0[:, k % 2, :], x_t[:, k, :], ACT.Square).then_inc(n_sq, 1)
            act.wait_ge(wdt_in, 16)
            act.activation(rb_hi[:, :, :].rearrange("p k t -> p (k t)")[:, 0:KT * P], wdt_raw, ACT.Copy)\
                .then_inc(wdt_hi_s, 1)
            act.wait_ge(const_s, 2)
            act.activation(ln_eps[:, :], eps[:, :], ACT.Ln)
            act.wait_ge(n_stat, 1)
            n = steps.did(act.activation(halves(rstd0), main(0), ACT.Ln, bias=eps[:, :], scale=1.0 / D_MODEL))
            steps.need(n)
            act.activation(rstd0, rstd0, ACT.Exp, scale=-0.5).then_inc(n_rstd, 1)
            hi(0, 0, 0)
            for k in range(KT):
                act.wait_ge(n_xn, k + 1)
                act.activation(ra_hi[:, k, :], xn0[:, k % 2, :], ACT.Copy).then_inc(u_hi_s, 1)
            act.wait_ge(par_s, 32)
            act.wait_ge(dt_psum, 1)
            act.activation(halves(dt_v), main(0), ACT.Identity, bias=dt_pars[:, 0:1]).then_inc(dt_act, 1)
            act.activation(a_neg[:, :], dt_pars[:, 1:2], ACT.Exp).then_inc(dt_act, 1)
            hi(1, 1, 0)
            act.wait_ge(dt_dve, 1)
            act.activation(dt_e, dt_e, ACT.Exp).then_inc(dt_act, 1)

            def evac_raw(g, j, m, first):
                i = 2 * j + m
                if i == 0:
                    act.wait_ge(par_ready, 1)
                    act.wait_ge(sstate_in, 16 * g + 16)
                    if not first:
                        act.wait_ge(sout_copied, g)
                    act.activation(raw_d[:, :, :, 0:SPRE], sstate, ACT.Copy).then_inc(sstate_used, 1)
                act.wait_ge(tile_done, 8 * g + i + 1)
                q = H2 - NDEC
                act.activation(raw[:, i, SPRE:SPRE + H2], psum[m][:, 0, 0:H2], ACT.Copy)
                act.activation(raw[:, i, SPRE + H2:SPRE + SEQ], psum[m][:, 1, 0:q], ACT.Copy)
                act.activation(raw_d[:, i, :, SPRE:], psum[m][:, 1, q:H2].rearrange("p (b t) -> p b t", t=TDEC),
                               ACT.Copy).then_inc(tile_free[m], 1)
                act.wait_ge(tile_free[m], 4 * g + j + 1)
                act.activation(acc[:, i, 0:CW], raw[:, i, SPRE:], ACT.Identity,
                               bias=par1("ssm_b", 4 * g + i), scale=par1("ssm_w", (4 * g + i) * SK + SK - 1))\
                    .then_inc(raw_ready, 1)

            def ssd_exps(c, p):
                act.wait_ge(pt_done, NCH * p + c + 1)
                act.activation(scores, pt[:, 3 * P:4 * P], ACT.Copy)
                act.wait_ge(ps_done, NCH * p + c + 1)
                for h in range(HPG):
                    last = act.activation(decay[:, h, :], ps[:, h * P:(h + 1) * P], ACT.Exp,
                                          bias=nacum_nat[:, c, bass.ds(4 * p + h, 1)])
                last.then_inc(decay_ready, 1)
                act.activation(b_nat, pt[:, 2 * P:3 * P], ACT.Copy)
                for to, factor in ((xdt, dt_nat), (wxdt, dtw_nat)):
                    for h in range(HPG):
                        last = act.activation(to[:, h * HD:(h + 1) * HD], pt[:, h * HD:(h + 1) * HD], ACT.Copy,
                                              scale=factor[:, c, bass.ds(4 * p + h, 1)])
                last.then_inc(xb_ready, 1)
                if c == 0:
                    ssd_e_exp(p)

            def ssd_e_exp(p):
                for j, bank in enumerate((ph, py)):
                    act.wait_ge(e_psum, 2 * p + j + 1)
                    last = act.activation(e_acc[:, j, :], bank[:, :], ACT.Exp)
                last.then_inc(e_ready, 1)

            def conv01(g):
                act.wait_ge(glu_ready, g + 1)
                act.activation(conv_a, gx[:, 0:SEQ], ACT.Identity, bias=par1("conf_b", g),
                               scale=par1("conf_w", g * CK))
                act.activation(conv_b, gx[:, 1:1 + SEQ], ACT.Copy, scale=par1("conf_w", g * CK + 1))\
                    .then_inc(conv01_s, 1)

            def decode_in(p):
                act.wait_ge(d_pt, p + 1)
                act.activation(d_bn[0:REP * NDEC, :], pt[0:REP * NDEC, 2 * P:3 * P], ACT.Copy).then_inc(d_w_s, 1)
                for to, factor, n in ((d_wxdt, dtw_nat, REP * NDEC), (d_xdt, dt_nat, NDEC)):
                    for h in range(HPG):
                        act.activation(to[0:n, h * HD:(h + 1) * HD], pt[0:n, h * HD:(h + 1) * HD], ACT.Copy,
                                       scale=factor[0:n, NCH, bass.ds(4 * p + h, 1)]).then_inc(d_w_s, 1)
                    if n > NDEC:
                        act.wait_ge(d_w_s, 9 * p + 5)
                        act.activation(d_wr[:, :], d_wxdt[0:REP * NDEC, :], ACT.Copy)
                        act.activation(d_br[:, :], d_bn[0:REP * NDEC, :], ACT.Copy).then_inc(d_hi_s, 1)
                act.activation(d_sc[0:NDEC, :], pt[0:NDEC, 384:384 + NDEC], ACT.Copy)
                act.wait_ge(d_ps, p + 1)
                for h in range(HPG):
                    act.activation(d_decay[0:NDEC, h, :], ps[0:NDEC, h * NDEC:(h + 1) * NDEC], ACT.Exp,
                                   bias=nacum_nat[0:NDEC, NCH, bass.ds(4 * p + h, 1)])
                act.activation(d_e.rearrange("p a b -> p (a b)"), ps[:, 128:128 + 2 * NDEC], ACT.Exp)\
                    .then_inc(d_dec_s, 1)

            def decode_b(p):
                act.wait_ge(d_lo_s, p + 1)
                for b in range(NSEQ):
                    last = act.activation(d_bm[:, b, :], fr(d_br[:, :]), ACT.Copy, scale=seq_mask[:, b:b + 1])
                last.then_inc(d_bn_s, 1)

            def y_square(p):
                act.wait_ge(d_ycur, p + 1)
                act.activation(d_sq, y_sb, ACT.Square).then_inc(d_sq_s, 1)

            def y_rstd(p):
                act.wait_ge(d_stat, p + 1)
                act.activation(d_rstd[:, 0:SEQ], ps[:, :], ACT.Ln, bias=eps[:, :], scale=1.0 / 256)\
                    .then_inc(y_ln_s, 1)
                act.activation(d_rstd[:, SEQ:T], pt[:, 0:NDEC], ACT.Ln, bias=eps[:, :], scale=1.0 / 256)\
                    .then_inc(y_ln_s, 1)
                act.wait_ge(y_ln_s, 2 * p + 2)
                act.activation(d_rstd, d_rstd, ACT.Exp, scale=-0.5).then_inc(d_rstd_s, 1)

            def group(g, ssd):
                p = g - 1
                for j in range(2):
                    for m in range(2):
                        if ssd:
                            ssd_exps(2 * j + m, p)
                        if ssd and (j, m) == (0, 0):
                            conv01(p)
                            hi(4 * g + 1, 1, 2 * g)
                        evac_raw(g, j, m, not ssd)
                    hi(4 * g + 2 + j, j % 2, 2 * g + 1)
                if ssd:
                    act.wait_ge(y_done, g)
                act.wait_ge(tile_done, 8 * g + 5)
                act.activation(halves(zs[:, 0, :]), main(0), ACT.Copy).then_inc(tile_free[0], 1)
                if ssd:
                    decode_in(p)
                    decode_b(p)
                act.wait_ge(tile_free[0], 4 * g + 3)
                act.activation(zs[:, 0, :], zs[:, 0, :], ACT.Silu)
                for i in range(4):
                    act.wait_ge(conv4_s, 4 * g + i + 1)
                    act.activation(sil[:, i, 0:CW], acc[:, i, 0:CW], ACT.Silu).then_inc(sil_ready, 1)
                    if i == 1:
                        act.wait_ge(tile_done, 8 * g + 6)
                        act.activation(halves(zs[:, 1, :]), main(1), ACT.Silu).then_inc(tile_free[1], 1)
                if ssd:
                    y_square(p)
                hi(4 * g + 4, 0, 2 * g + 2)
                if ssd:
                    act.wait_ge(glu_ready, g)
                act.wait_ge(tile_done, 8 * g + 7)
                act.activation(halves(zh[:, 0, :]), main(0), ACT.Copy, scale=0.5).then_inc(tile_free[0], 1)
                if ssd:
                    y_rstd(p)
                act.wait_ge(sil_ready, 4 * g + 4)
                for rep in range(P // NDEC):
                    last = act.activation(d_cur[:, :, rep, :].rearrange("p a (b t) -> p a b t", b=NSEQ), sil_d,
                                          ACT.Copy)
                last.then_inc(dec_saved, 1)
                act.activation(d_z, zs[:, :, SEQ:T], ACT.Copy).then_inc(z_ready, 1)
                act.wait_ge(tile_done, 8 * g + 8)
                act.activation(halves(zh[:, 1, :]), main(1), ACT.Tanh, scale=0.5).then_inc(tile_free[1], 1)

            group(0, False)
            act.wait_ge(nat_t, 1)
            for q, dst in enumerate((dt_nat, acum_nat)):
                at = q * (NCH + 1) * HEADS
                steps.did(act.activation(dst[:, 0:NCH, :].rearrange("p c h -> p (c h)"),
                                         ps[:, at:at + NCH * HEADS], ACT.Copy))
                act.activation(dst[0:NDEC, NCH, :], ps[0:NDEC, at + NCH * HEADS:at + (NCH + 1) * HEADS],
                               ACT.Copy).then_inc(nat_copied, 1)
            act.wait_ge(nat_diff, 1)
            act.activation(exp_last[:, :, :].rearrange("p c h -> p (c h)"), py[:, 0:(NCH + NSEQ) * HEADS], ACT.Exp)
            steps.did(act.activation(w_nat[:, 0:NCH, :], w_nat[:, 0:NCH, :], ACT.Exp))
            act.activation(w_nat[0:NDEC, NCH, :], w_nat[0:NDEC, NCH, :], ACT.Exp).then_inc(nat_exp, 1)
            act.wait_ge(nat_ready, 1)
            act.wait_ge(rep_s, 32 * (REP - 1))
            with act.Fori(1, GROUPS) as g:
                group(g, True)

            def gate(i, m):
                act.wait_ge(tile_done, 2 * (B_GATES + i) + m + 1)
                if not isinstance(i, int) or i:
                    act.wait_ge(gates_st[m], 16 * i)
                act.activation(halves(gates_sb[:, m, :]), main(m), ACT.Copy).then_inc(tile_free[m], 1)

            p = GROUPS - 1
            for c in range(NCH):
                ssd_exps(c, p)
                if c == 0:
                    conv01(p)
                    hi(B_GATES + 1, 1, B_GATES // 2)
                    act.wait_ge(sout_copied, GROUPS)
                gate(c // 2, c % 2)
                if c % 2:
                    hi(B_GATES + 2 + c // 2, c // 2, B_GATES // 2 + 1)
            gate(2, 0)
            decode_in(p)
            decode_b(p)
            gate(2, 1)
            y_square(p)
            hi(B_GATES + 4, 0, B_GATES // 2 + 2)
            gate(3, 0)
            y_rstd(p)
            gate(3, 1)

            def y_high(i, to):
                act.wait_ge(y_in[i % 2], 16 * (i // 2) + 16)
                for j in range(2):
                    act.activation(to[:, (2 * i + j) % KT, :], y_ld[:, i % 2, j, :], ACT.Copy).then_inc(ys_hi, 1)

            act.wait_ge(d_yn_s, GROUPS)
            for i in range(4):
                hi_next((B_GATES + 4 + i) // 2, i % 2)
                for m in range(2):
                    gate(4 + i, m)
                    if m == 0:
                        y_high(i, rb_hi)
            act.wait_ge(l_stat, 1)
            for hf, bank in enumerate((pt, ps)):
                last = act.activation(l_mean[:, hf * H2:(hf + 1) * H2], bank[:, 0:H2], ACT.Copy,
                                      scale=1.0 / D_MODEL)
            last.then_inc(l_mean_s, 1)
            for i in range(4):
                hi_next((B_SSM + i) // 2, i % 2)
                if i == 0:
                    act.wait_ge(tile_done, 2 * B_SSM)
                y_high(4 + i, ra_hi)
                for m in range(2):
                    act.wait_ge(tile_done, 2 * (B_SSM + i) + m + 1)
                    act.activation(halves(b_sum[:, 2 * i + m, :]), main(m), ACT.Copy, scale=0.5)\
                        .then_inc(tile_free[m], 1)
                    n = 2 * i + m
                    act.wait_ge(l_xc, n + 1)
                    if n >= 2:
                        act.wait_ge(l_ssum_s, n - 1)
                    act.activation(l_sq[:, m, :], xc[:, n, :], ACT.Square).then_inc(l_sq_s, 1)
            hi_next(B_SSM // 2 + 2, 0)
            act.wait_ge(l_stat2, 1)
            for hf, bank in enumerate((py, ph)):
                n = steps.did(act.activation(l_rstd[:, hf * H2:(hf + 1) * H2], bank[:, 0:H2], ACT.Ln,
                                             bias=eps[:, :], scale=1.0 / D_MODEL))
            steps.need(n)
            act.activation(l_rstd, l_rstd, ACT.Exp, scale=-0.5).then_inc(l_rstd_s, 1)
            hi_next(B_SSM // 2 + 2, 1)

            def cc_high(m):
                act.wait_ge(l_sil, m + 1)
                act.activation(rb_hi[:, m, :], xc[:, m, :], ACT.Copy).then_inc(cc_hi_s, 1)

            for m in range(KT):
                act.wait_ge(l_t, m + 1)
                act.activation(xc[:, m, :], xc[:, m, :], ACT.Silu, bias=par1("ln_b", m), scale=par1("ln_g", m))\
                    .then_inc(l_sil, 1)
                if m >= 1:
                    cc_high(m - 1)
                if m == 2:
                    hi_next(B_SSM // 2 + 3, 0)
                if m == 6:
                    hi_next(B_SSM // 2 + 3, 1)
            cc_high(KT - 1)
            for m in range(KT):
                if m % 2 == 0:
                    hi_next((B_PW + m // 2) // 2, (m // 2) % 2)
                act.wait_ge(g_in_s[m % 2], 16 * (m // 2) + 16)
                act.activation(g_in[:, m % 2, :, :], g_in[:, m % 2, :, :], ACT.Tanh, scale=0.5)
                act.wait_ge(tile_done, 2 * B_PW + m + 1)
                act.activation(halves(pw_a[:, m % 2, :]), main(m), ACT.Identity, bias=par1("b_pw", m), scale=0.5)\
                    .then_inc(tile_free[m % 2], 1)
                if m >= 1:
                    act.wait_ge(p_m, 3 * m)
                    act.activation(ra_hi[:, m - 1, :], pw_m[:, (m - 1) % 2, :], ACT.Copy).then_inc(mg_hi, 1)
            act.wait_ge(p_m, 3 * KT)
            act.activation(ra_hi[:, KT - 1, :], pw_m[:, (KT - 1) % 2, :], ACT.Copy).then_inc(mg_hi, 1)
            for m in range(KT):
                if m % 2 == 0:
                    hi_next((B_WOUT + m // 2) // 2, (m // 2) % 2)
                act.wait_ge(tile_free[m % 2], B_WOUT + m // 2 + 1)
                if m >= 2:
                    act.wait_ge(o_sum_s, m - 1)
                act.activation(o_sq[:, m % 2, :], h_sb[:, m, :], ACT.Square).then_inc(o_act, 1)
                act.activation(rb_hi[:, m, :], h_sb[:, m, :], ACT.Copy, scale=par1("g_ffn", m)).then_inc(o_act, 1)
            def hidden(i, n):
                k = KT * i + n
                act.wait_ge(f_v_s, k + 1)
                act.activation(f_s[:, n % 2, :], f_v[:, n % 2, :], ACT.Square).then_inc(f_sq_s, 1)
                act.wait_ge(f_sq_s, k + 1)
                act.activation(ra_hi[:, n, :], f_s[:, n % 2, :], ACT.Copy).then_inc(f_hi, 1)

            def ffn_rstd():
                act.wait_ge(o_stat, 1)
                for hf, bank in enumerate((pt, ps)):
                    n = steps.did(act.activation(o_rstd[:, hf * H2:(hf + 1) * H2], bank[:, 0:H2], ACT.Ln,
                                                 bias=eps[:, :], scale=1.0 / D_MODEL))
                steps.need(n)
                act.activation(o_rstd, o_rstd, ACT.Exp, scale=-0.5).then_inc(o_rstd_s, 1)

            def quarter(i, first=False, last=False):
                for j in range(4):
                    hi_next(B_FFN // 2 + 4 * i + j // 2, j % 2)
                    if first and j == 0:
                        ffn_rstd()
                    for m in range(2):
                        n = 2 * j + m
                        act.wait_ge(tile_done, 2 * B_FFN + 16 * i + n + 1)
                        act.activation(halves(f_r[:, n % 2, :]), main(m), ACT.Relu).then_inc(tile_free[m], 1)
                        if n >= 1:
                            hidden(i, n - 1)
                hidden(i, KT - 1)
                for j in range(4):
                    if not last or j < 3:
                        hi_next(B_FFN // 2 + 4 * i + 2 + j // 2, j % 2)
                    if last:
                        final_square(2 * j)
                        final_square(2 * j + 1)

            def final_square(m):
                act.wait_ge(tile_free[m % 2], NBLOCKS - 3 + m // 2)
                if m >= 2:
                    act.wait_ge(z_sum, m - 1)
                act.activation(o_sq[:, m % 2, :], h_sb[:, m, :], ACT.Square).then_inc(z_sq, 1)

            quarter(0, first=True)
            with act.Fori(1, 3) as i:
                quarter(i)
            quarter(3, last=True)
            act.wait_ge(z_stat, 1)
            for hf, bank in enumerate((py, ph)):
                n = steps.did(act.activation(o_rstd[:, hf * H2:(hf + 1) * H2], bank[:, 0:H2], ACT.Ln,
                                             bias=eps[:, :], scale=1.0 / D_MODEL))
            steps.need(n)
            act.activation(o_rstd, o_rstd, ACT.Exp, scale=-0.5).then_inc(z_rstd, 1)

        @block.vector
        def _(dve):
            steps = Steps(dve, dve_c)

            def lo(b, s):
                dve.wait_ge(w_hi_s, b + 1)
                dve.tensor_tensor(w_lo[:, s, :], w_raw[:, s, :], fr(w_hi[:, s, :]), ALU.subtract)\
                    .then_inc(w_lo_s, 1)

            def lo_next(pair, s):
                lo(2 * pair + 1, 1) if s == 0 else lo(2 * pair + 2, 0)

            for k in range(KT):
                dve.wait_ge(n_sq, k + 1)
                if k == 0:
                    dve.tensor_copy(ssum0, sq0[:, 0, :]).then_inc(n_sum, 1)
                else:
                    dve.wait_ge(n_sum, k)
                    dve.tensor_tensor(ssum0, ssum0, sq0[:, k % 2, :], ALU.add).then_inc(n_sum, 1)
            dve.wait_ge(wdt_hi_s, 1)
            dve.tensor_tensor(rb_lo[:, :, :].rearrange("p k t -> p (k t)")[:, 0:KT * P], wdt_raw,
                              fr(rb_hi[:, :, :].rearrange("p k t -> p (k t)")[:, 0:KT * P]),
                              ALU.subtract).then_inc(wdt_ready, 1)
            dve.wait_ge(par_s, 32)
            at, n = PARAMS["b_pw"]
            dve.tensor_scalar(pars[:, at:at + n], pars[:, at:at + n], 0.5, None, ALU.mult).then_inc(par_ready, 1)

            def make_u(k):
                if k >= 2:
                    dve.wait_ge(u_hi_s, k - 1)
                    dve.wait_ge(u_ready, k - 1)
                dve.scalar_tensor_tensor(xn0[:, k % 2, :], x_t[:, k, :], par1("g_mix", k), rstd0, ALU.mult,
                                         ALU.mult).then_inc(n_xn, 1)

            dve.wait_ge(n_rstd, 1)
            make_u(0)
            for k in range(KT):
                if k < KT - 1:
                    make_u(k + 1)
                dve.wait_ge(u_hi_s, k + 1)
                dve.wait_ge(n_xn, k + 1)
                dve.tensor_tensor(ra_lo[:, k, :], xn0[:, k % 2, :], fr(ra_hi[:, k, :]), ALU.subtract)\
                    .then_inc(u_ready, 1)
            lo(0, 0)
            dve.wait_ge(dt_act, 2)
            dve.scalar_tensor_tensor(dt_e, dt_v, -1.0, dt_v, ALU.mult, ALU.min).then_inc(dt_dve, 1)
            steps.did(dve.tensor_scalar(a_neg[:, :], a_neg[:, :], -1.0, None, ALU.mult))
            n_r = steps.did(dve.tensor_scalar(dt_r, dt_v, 0.0, None, ALU.max))
            lo(1, 1)
            dve.wait_ge(dt_act, 3)
            n = steps.did(dve.tensor_scalar(dt_z, dt_e, 2.0, None, ALU.add))
            steps.need(n)
            n = steps.did(dve.reciprocal(dt_z, dt_z))
            steps.need(n)
            n_z = steps.did(dve.tensor_tensor(dt_z, dt_z, dt_e, ALU.mult))
            steps.need(n_z)
            n = steps.did(dve.tensor_tensor(dt_z2, dt_z, dt_z, ALU.mult))
            steps.need(n)
            n = steps.did(dve.tensor_scalar(dt_p, dt_z2, 1.0 / 17, None, ALU.mult))
            for odd in range(15, 1, -2):
                steps.need(n)
                n = steps.did(dve.scalar_tensor_tensor(dt_p, dt_p, 1.0 / odd, dt_z2, ALU.add, ALU.mult))
            steps.need(n)
            n = steps.did(dve.scalar_tensor_tensor(dt_t, dt_p, 1.0, dt_z, ALU.add, ALU.mult))
            steps.need(n)
            n = steps.did(dve.scalar_tensor_tensor(dt_r, dt_t, 2.0, dt_r, ALU.mult, ALU.add))
            steps.need(n)
            n = steps.did(dve.tensor_scalar(dt_p, dt_r, a_neg[:, :], None, ALU.mult))
            steps.need(n)
            dve.wait_ge(const_s, 3)
            n = steps.did(dve.tensor_tensor_scan(dt_t, scan_keep, dt_p, 0.0, ALU.mult, ALU.add))
            steps.need(n)
            n = steps.did(dve.tensor_copy(acum_bf[:, :], dt_t[0:96, :]))
            steps.need(n)
            n = steps.did(dve.tensor_tensor(dt_z[0:96, :], dt_t[0:96, :], acum_bf[:, :], ALU.subtract))
            steps.need(n)
            steps.did(dve.tensor_copy(acum_bf[32:64, :], dt_z[32:64, :]))
            n = steps.did(dve.tensor_copy(acum_bf[64:96, :], dt_z[64:96, :]))
            steps.need(n)
            n = steps.did(dve.tensor_tensor(dt_z[64:96, :], dt_z[64:96, :], acum_bf[64:96, :], ALU.subtract))
            steps.need(n)
            dve.tensor_copy(acum_bf[64:96, :], dt_z[64:96, :]).then_inc(acum_ready, 1)

            TAPS_BEFORE, TAPS_AFTER = (0, 2, 4, 4), (1, 4, 3, 4)

            class Conv31:

                def __init__(self, p):
                    self.p, self.k, self.last = p, 2, [None, None]

                def start(self):
                    dve.wait_ge(conv01_s, self.p + 1)

                def taps(self, n):
                    for k in range(self.k, min(self.k + n, CK)):
                        to = (conv_a, conv_b)[k % 2]
                        w = par1("conf_w", self.p * CK + k)
                        src = gx[:, k:k + SEQ]
                        if self.last[k % 2] is not None:
                            steps.need(self.last[k % 2])
                        self.last[k % 2] = steps.did(
                            dve.scalar_tensor_tensor(to, src, w, to, ALU.mult, ALU.add))
                    self.k = min(self.k + n, CK)

                def finish(self):
                    self.taps(CK)
                    dve.wait_ge(cc_free, self.p + 1)
                    steps.need(max(self.last))
                    n = steps.did(dve.tensor_tensor(ccs[:, 0:SEQ], conv_a, conv_b, ALU.add))
                    dve.wait_ge(cpre_ready, self.p + 1)
                    hs = NSEQ // 2
                    prod = conv_b[:, 0:hs * TDEC * CK]
                    base = gd[:, 0:1, 0:1]
                    w = par1("conf_w", self.p * CK, CK)
                    for b in range(2):
                        wins = bass.AP(base.tensor, base.offset + b * hs * (CPRE + TDEC),
                                       [[base.ap[0][0], P], [CPRE + TDEC, hs], [1, TDEC], [1, CK]])
                        steps.need(n)
                        n = steps.did(dve.tensor_tensor(
                            prod.rearrange("p (b t k) -> p b t k", b=hs, t=TDEC), wins,
                            w.unsqueeze(1).unsqueeze(1).broadcast_to([P, hs, TDEC, CK]), ALU.mult))
                        steps.need(n)
                        n = steps.did(dve.tensor_reduce(
                            ccs[:, SEQ + b * hs * TDEC:SEQ + (b + 1) * hs * TDEC],
                            prod.rearrange("p (n k) -> p n k", k=CK), AX.X, ALU.add))
                    steps.need(n)
                    dve.tensor_scalar(ccs[:, SEQ:T], ccs[:, SEQ:T], par1("conf_b", self.p), None, ALU.add)\
                        .then_inc(cc_ready, 1)

            def by_head(ap, c, p):
                return ap[:, c, bass.ds(4 * p, HPG)].unsqueeze(2).broadcast_to([P, HPG, HD])

            def heads(ap):
                return ap.rearrange("p (h d) -> p h d", d=HD)

            def ssd_scores(c, p):
                dve.wait_ge(decay_ready, NCH * p + c + 1)
                dve.tensor_tensor(m_t, decay, scores.unsqueeze(1).broadcast_to([P, HPG, P]), ALU.mult)\
                    .then_inc(m_ready, 1)

            def ssd_state(c, p):
                cs = slice(c * CHUNK, (c + 1) * CHUNK)
                y_in_chunk = py[:, 0:256].rearrange("p (j n) -> p j n", j=2)
                dve.wait_ge(ys_done, NCH * p + c + 1)
                if c == 0:
                    dve.wait_ge(ssd_free, p + 1)
                    steps.did(dve.tensor_copy(y_sb[:, :, cs], y_in_chunk))
                    dve.tensor_copy(h_t, ph[:, 0:256]).then_inc(h_ready, 1)
                else:
                    if c == 1:
                        dve.wait_ge(e_ready, p + 1)
                    n = steps.did(dve.tensor_tensor(y_tmp, py[:, 256:512].rearrange("p (j n) -> p j n", j=2),
                                                    e_acc[:, :, cs], ALU.mult))
                    dve.wait_ge(h_ready, NCH * p + c)
                    n2 = steps.did(dve.tensor_tensor(heads(h_t), heads(h_t), by_head(exp_last, c, p), ALU.mult))
                    steps.need(n)
                    steps.did(dve.tensor_tensor(y_sb[:, :, cs], y_tmp, y_in_chunk, ALU.add))
                    steps.need(n2)
                    dve.tensor_tensor(h_t, h_t, ph[:, 0:256], ALU.add).then_inc(h_ready, 1)

            def ssd_y(p):
                dve.wait_ge(z_ready, p + 1)
                steps.need(steps.n)
                for j in range(2):
                    n = steps.did(dve.scalar_tensor_tensor(y_sb[:, j, 0:SEQ], sil[:, j, 0:SEQ],
                                                           par1("d_skip", 2 * p + j), y_sb[:, j, 0:SEQ],
                                                           ALU.mult, ALU.add))
                steps.need(n)
                dve.tensor_tensor(y_sb[:, :, 0:SEQ], y_sb[:, :, 0:SEQ], zs[:, :, 0:SEQ], ALU.mult).then_inc(y_done, 1)

            def conv4(g, pair):
                tiles = (2 * pair, 2 * pair + 1)
                dve.wait_ge(raw_ready, 4 * g + 2 * pair + 2)
                last = {}
                for k in range(SK - 1):
                    for i in tiles:
                        w = par1("ssm_w", (4 * g + i) * SK + k)
                        if k:
                            steps.need(last[i])
                        to = acc[:, i, 0:CW]
                        ins = dve.scalar_tensor_tensor(to, raw[:, i, k:k + CW], w, to, ALU.mult, ALU.add)
                        if k == SK - 2:
                            ins.then_inc(conv4_s, 1)
                        else:
                            last[i] = steps.did(ins)

            def decode_m(p, conv):
                dve.wait_ge(d_hi_s, p + 1)
                dve.tensor_tensor(d_wr[NDEC:2 * NDEC, :], d_wxdt[NDEC:2 * NDEC, :], fr(d_wr[NDEC:2 * NDEC, :]),
                                  ALU.subtract)
                dve.tensor_tensor(d_br[2 * NDEC:, :], d_bn[2 * NDEC:3 * NDEC, :], fr(d_br[2 * NDEC:, :]),
                                  ALU.subtract).then_inc(d_lo_s, 1)
                conv.taps(3)
                dve.wait_ge(d_dec_s, p + 1)
                dve.tensor_tensor(d_m[0:NDEC], d_decay[0:NDEC],
                                  d_sc[0:NDEC, :].unsqueeze(1).broadcast_to([NDEC, HPG, NDEC]), ALU.mult)\
                    .then_inc(d_m_s, 1)
                dve.wait_ge(d_off, p + 1)
                return steps.did(dve.tensor_tensor(
                    st.rearrange("p b (h d) -> p b h d", d=HD), st.rearrange("p b (h d) -> p b h d", d=HD),
                    exp_last[:, NCH:, bass.ds(4 * p, HPG)].unsqueeze(3).broadcast_to([P, NSEQ, HPG, HD]),
                    ALU.mult))

            def state_add(r, bank, done):
                v = st[:, 2 * r:2 * r + 2, :].rearrange("p b n -> p (b n)")
                dve.tensor_tensor(v, v, bank[:, :], ALU.add).then_inc(done, 1)

            def decode_y(p, n_st):
                dve.wait_ge(d_y, p + 1)
                n = steps.did(dve.tensor_tensor(d_tmp, py[:, 64:128].rearrange("p (j n) -> p j n", j=2), d_e,
                                                ALU.mult))
                steps.need(n)
                n = steps.did(dve.tensor_tensor(d_tmp, d_tmp, py[:, 0:64].rearrange("p (j n) -> p j n", j=2),
                                                ALU.add))
                steps.need(n)
                for j in range(2):
                    n = steps.did(dve.scalar_tensor_tensor(d_tmp[:, j, :], d_cur[:, j, 0, :],
                                                           par1("d_skip", 2 * p + j), d_tmp[:, j, :], ALU.mult,
                                                           ALU.add))
                steps.need(n)
                dve.tensor_tensor(y_sb[:, :, SEQ:T], d_tmp, d_z[:, :, :], ALU.mult).then_inc(d_ycur, 1)
                steps.need(n_st)
                for r, bank in enumerate((ph, ps, pt)):
                    state_add(r, bank, d_add)

            def decode_sum(p):
                dve.wait_ge(d_sq_s, p + 1)
                dve.tensor_tensor(d_ssum, d_sq[:, 0, :], d_sq[:, 1, :], ALU.add).then_inc(d_ssum_s, 1)

            def decode_last(p):
                dve.wait_ge(d_r3, p + 1)
                state_add(3, ph, st_ready)

            def decode_norm(p):
                dve.wait_ge(d_rstd_s, p + 1)
                for j in range(2):
                    ins = dve.scalar_tensor_tensor(d_yn[:, j, :], y_sb[:, j, :], par1("norm_g", 2 * p + j),
                                                   d_rstd, ALU.mult, ALU.mult)
                ins.then_inc(d_yn_s, 1)

            def group(g, ssd):
                p = g - 1
                if ssd:
                    conv = Conv31(p)
                    for c in range(NCH):
                        conv.taps(TAPS_BEFORE[c])
                        ssd_scores(c, p)
                        if c == 0:
                            conv.start()
                            conv.taps(2)
                            lo(4 * g + 1, 1)
                        if c == 2:
                            lo(4 * g + 2, 0)
                        conv.taps(TAPS_AFTER[c])
                        ssd_state(c, p)
                    ssd_y(p)
                else:
                    dve.wait_ge(const_s, 6)
                    lo(4 * g + 2, 0)
                lo(4 * g + 3, 1)
                conv4(g, 0)
                if ssd:
                    n_st = decode_m(p, conv)
                conv4(g, 1)
                if ssd:
                    decode_y(p, n_st)
                    decode_sum(p)
                lo(4 * g + 4, 0)
                if ssd:
                    conv.finish()
                    decode_last(p)
                    decode_norm(p)
                dve.wait_ge(tile_free[1], 4 * g + 4)
                if ssd:
                    dve.wait_ge(cout_copied, g)
                steps.did(dve.scalar_tensor_tensor(gx[:, CPRE:], zh[:, 1, 0:SEQ], 1.0, zh[:, 0, 0:SEQ], ALU.add,
                                                   ALU.mult))
                dve.scalar_tensor_tensor(gd[:, :, CPRE:], zh[:, 1, SEQ:T].rearrange("p (b t) -> p b t", t=TDEC), 1.0,
                                         zh[:, 0, SEQ:T].rearrange("p (b t) -> p b t", t=TDEC), ALU.add, ALU.mult)\
                    .then_inc(glu_ready, 1)

            group(0, False)
            dve.wait_ge(nat_copied, 2)
            steps.did(dve.tensor_scalar(nacum_nat[:, 0:NCH, :], acum_nat[:, 0:NCH, :], -1.0, None, ALU.mult))
            steps.did(dve.tensor_scalar(nacum_nat[0:NDEC, NCH, :], acum_nat[0:NDEC, NCH, :], -1.0, None, ALU.mult))
            dve.wait_ge(nat_b, 1)
            steps.did(dve.tensor_tensor(w_nat[:, 0:NCH, :], py[:, 0:NCH * HEADS]
                                        .rearrange("p (c h) -> p c h", h=HEADS), acum_nat[:, 0:NCH, :],
                                        ALU.subtract))
            dve.tensor_tensor(w_nat[0:NDEC, NCH, :], ph[0:NDEC, 0:HEADS], acum_nat[0:NDEC, NCH, :], ALU.subtract)\
                .then_inc(nat_diff, 1)
            dve.wait_ge(nat_exp, 1)
            steps.did(dve.tensor_tensor(dtw_nat[:, 0:NCH, :], dt_nat[:, 0:NCH, :], w_nat[:, 0:NCH, :], ALU.mult))
            dve.tensor_tensor(dtw_nat[0:NDEC, NCH, :], dt_nat[0:NDEC, NCH, :], w_nat[0:NDEC, NCH, :], ALU.mult)\
                .then_inc(nat_ready, 1)
            with dve.Fori(1, GROUPS) as g:
                steps.enter(g - 1, K_GROUP)
                group(g, True)
            steps.leave(GROUPS - 1)
            p = GROUPS - 1
            conv = Conv31(p)
            for c in range(NCH):
                conv.taps(TAPS_BEFORE[c])
                ssd_scores(c, p)
                if c == 0:
                    conv.start()
                    conv.taps(2)
                    lo(B_GATES + 1, 1)
                conv.taps(TAPS_AFTER[c])
                ssd_state(c, p)
                if c == 1:
                    lo(B_GATES + 2, 0)
            ssd_y(p)
            lo(B_GATES + 3, 1)
            n_st = decode_m(p, conv)
            conv.taps(CK)
            decode_y(p, n_st)
            decode_sum(p)
            lo(B_GATES + 4, 0)
            conv.finish()
            decode_last(p)
            decode_norm(p)

            def y_low(i, hi_part, to):
                for j in range(2):
                    k = (2 * i + j) % KT
                    dve.wait_ge(ys_hi, 2 * i + j + 1)
                    dve.tensor_tensor(to[:, k, :], y_ld[:, i % 2, j, :], fr(hi_part[:, k, :]), ALU.subtract)\
                        .then_inc(ys_ready, 1)

            for i in range(4):
                lo_next((B_GATES + 4 + i) // 2, i % 2)
                if i == 0:
                    dve.wait_ge(st_st, 16 * GROUPS)
                    dve.wait_ge(yn_st, 16 * GROUPS)
                y_low(i, rb_hi, rb_lo)
            def square_sum(m):
                dve.wait_ge(l_sq_s, m + 1)
                if m == 0:
                    ins = dve.tensor_copy(l_ssum, l_sq[:, 0, :])
                else:
                    dve.wait_ge(l_ssum_s, m)
                    ins = dve.tensor_tensor(l_ssum, l_ssum, l_sq[:, m % 2, :], ALU.add)
                ins.then_inc(l_ssum_s, 1)

            for i in range(4):
                lo_next((B_SSM + i) // 2, i % 2)
                if i == 0:
                    dve.wait_ge(l_mean_s, 1)
                    dve.wait_ge(cc_in, 32)
                y_low(4 + i, ra_hi, ra_lo)
                for m in (2 * i, 2 * i + 1):
                    dve.tensor_tensor(xc[:, m, :], xc[:, m, :], l_mean, ALU.subtract).then_inc(l_xc, 1)
                    if m >= 1:
                        square_sum(m - 1)
            square_sum(KT - 1)

            def b_add(i):
                for m in range(2):
                    dve.wait_ge(tile_done, 2 * (B_SSM + 4 + i) + m + 1)
                    v = halves(b_sum[:, 2 * i + m, :])
                    dve.scalar_tensor_tensor(v, main(m), 0.5, v, ALU.mult, ALU.add).then_inc(tile_free[m], 1)

            lo_next(B_SSM // 2 + 2, 0)
            b_add(0)
            lo_next(B_SSM // 2 + 2, 1)
            dve.wait_ge(l_rstd_s, 1)

            def cc_low(m):
                dve.wait_ge(cc_hi_s, m + 1)
                dve.tensor_tensor(rb_lo[:, m, :], xc[:, m, :], fr(rb_hi[:, m, :]), ALU.subtract)\
                    .then_inc(cc_split, 1)

            for m in range(KT):
                dve.wait_ge(l_xc, KT)
                dve.tensor_tensor(xc[:, m, :], xc[:, m, :], l_rstd, ALU.mult).then_inc(l_t, 1)
                if m >= 2:
                    cc_low(m - 2)
                if m == 2:
                    b_add(1)
                    lo_next(B_SSM // 2 + 3, 0)
                if m == 6:
                    b_add(2)
                    lo_next(B_SSM // 2 + 3, 1)
            cc_low(KT - 2)
            cc_low(KT - 1)
            b_add(3)

            def mg_low(m):
                dve.wait_ge(mg_hi, m + 1)
                dve.tensor_tensor(ra_lo[:, m, :], pw_m[:, m % 2, :], fr(ra_hi[:, m, :]), ALU.subtract)\
                    .then_inc(mg_ready, 1)

            for m in range(KT):
                if m % 2 == 0:
                    lo_next((B_PW + m // 2) // 2, (m // 2) % 2)
                dve.wait_ge(tile_free[m % 2], B_PW + m // 2 + 1)
                if m >= 2:
                    dve.wait_ge(mg_ready, m - 1)
                a, o = pw_a[:, m % 2, :], pw_m[:, m % 2, :]
                dve.scalar_tensor_tensor(a, g_in[:, m % 2, 0, :], 1.0, a, ALU.add, ALU.mult).then_inc(p_m, 1)
                dve.scalar_tensor_tensor(o, g_in[:, m % 2, 1, :], 1.0, b_sum[:, m, :], ALU.add, ALU.mult)\
                    .then_inc(p_m, 1)
                dve.wait_ge(p_m, 3 * m + 2)
                dve.tensor_tensor(o, o, a, ALU.add).then_inc(p_m, 1)
                if m >= 1:
                    mg_low(m - 1)
            mg_low(KT - 1)

            def h_low(m):
                dve.wait_ge(o_act, 2 * m + 2)
                if m == 0:
                    ins = dve.tensor_copy(o_ssum, o_sq[:, 0, :])
                else:
                    dve.wait_ge(o_sum_s, m)
                    ins = dve.tensor_tensor(o_ssum, o_ssum, o_sq[:, m % 2, :], ALU.add)
                ins.then_inc(o_sum_s, 1)
                dve.scalar_tensor_tensor(rb_lo[:, m, :], h_sb[:, m, :], par1("g_ffn", m), fr(rb_hi[:, m, :]),
                                         ALU.mult, ALU.subtract).then_inc(hn_ready, 1)

            for m in range(KT):
                if m % 2 == 0:
                    lo_next((B_WOUT + m // 2) // 2, (m // 2) % 2)
                dve.wait_ge(x_in2[m % 2], 16 * (m // 2) + 16)
                dve.wait_ge(tile_done, 2 * B_WOUT + m + 1)
                dve.tensor_tensor(halves(h_sb[:, m, :]), main(m), halves(x_in[:, m % 2, :]), ALU.add)\
                    .then_inc(tile_free[m % 2], 1)
                if m >= 1:
                    h_low(m - 1)
            h_low(KT - 1)

            def quarter(i, first=False, last=False):
                def hidden_low(n):
                    dve.wait_ge(f_hi, KT * i + n + 1)
                    dve.tensor_tensor(ra_lo[:, n, :], f_s[:, n % 2, :], fr(ra_hi[:, n, :]), ALU.subtract)\
                        .then_inc(f_ready, 1)

                for j in range(4):
                    lo_next(B_FFN // 2 + 4 * i + j // 2, j % 2)
                    if first and j == 0:
                        dve.wait_ge(o_rstd_s, 1)
                    for m in range(2):
                        n = 2 * j + m
                        dve.wait_ge(tile_free[m], B_FFN + 8 * i + j + 1)
                        dve.tensor_tensor(f_v[:, n % 2, :], f_r[:, n % 2, :], o_rstd, ALU.mult).then_inc(f_v_s, 1)
                        if n >= 1:
                            hidden_low(n - 1)
                hidden_low(KT - 1)
                for j in range(4):
                    if not last or j < 3:
                        lo_next(B_FFN // 2 + 4 * i + 2 + j // 2, j % 2)
                    for m in range(2):
                        n = 2 * j + m
                        dve.wait_ge(tile_done, 2 * B_FFN + 16 * i + 8 + n + 1)
                        v = halves(h_sb[:, n, :])
                        dve.tensor_tensor(v, v, main(m), ALU.add).then_inc(tile_free[m], 1)
                        if last and 1 <= n < KT:
                            final_sum(n - 1)

            def final_sum(n):
                dve.wait_ge(z_sq, n + 1)
                if n == 0:
                    dve.tensor_copy(o_ssum, o_sq[:, 0, :]).then_inc(z_sum, 1)
                else:
                    dve.wait_ge(z_sum, n)
                    dve.tensor_tensor(o_ssum, o_ssum, o_sq[:, n % 2, :], ALU.add).then_inc(z_sum, 1)

            quarter(0, first=True)
            with dve.Fori(1, 3) as i:
                quarter(i)
            quarter(3, last=True)
            dve.wait_ge(z_rstd, 1)
            for m in range(KT):
                dve.scalar_tensor_tensor(h_sb[:, m, :], h_sb[:, m, :], par1("g_final", m), o_rstd, ALU.mult,
                                         ALU.mult).then_inc(z_y, 1)


K_GROUP = 60


def _cols(w, *ranges):
    b = np.concatenate([w[:, a:a + n] for a, n in ranges], axis=1)
    return b.reshape(KT, P, BW).transpose(1, 0, 2).reshape(P, KT * BW)


def _tiles(x, k):
    return x.T.reshape(k, P, -1).transpose(1, 0, 2).reshape(P, -1)


def kernel(**inputs):
    import concourse.bacc as bacc
    from concourse.bass_utils import run_bass_kernel_spmd

    a = {k: np.asarray(v) for k, v in inputs.items()}
    w_in, w_pw, w_so, w_o, w_up, w_dn = (a[n][0] for n in (
        "w_in", "conf_w_pw", "ssm_w_out", "w_out", "w_up", "w_down"))
    gate0, z0 = 2 * D_MODEL, 4 * D_MODEL
    xbc0 = z0 + 2 * D_MODEL
    dt0 = xbc0 + 4 * D_MODEL
    blocks = []
    for g in range(GROUPS):
        blocks += [_cols(w_in, (xbc0 + 256 * g, 256)),
                   _cols(w_in, (xbc0 + 2048 + P * g, P), (xbc0 + 3072 + P * g, P)),
                   _cols(w_in, (z0 + 256 * g, 256)),
                   _cols(w_in, (P * g, P), (D_MODEL + P * g, P))]
    blocks += [_cols(w_in, (gate0 + P * i, P), (gate0 + D_MODEL + P * i, P)) for i in range(8)]
    for q in range(2):
        blocks += [_cols(w_so[1024 * q:1024 * (q + 1)], (256 * i, 256)) for i in range(4)]
    blocks += [_cols(w_pw, (256 * i, 256)) for i in range(4)]
    blocks += [_cols(w_o, (256 * i, 256)) for i in range(4)]
    for q in range(4):
        blocks += [_cols(w_up, (1024 * q + 256 * i, 256)) for i in range(4)]
        blocks += [_cols(w_dn[1024 * q:1024 * (q + 1)], (256 * i, 256)) for i in range(4)]
    w_all = np.stack(blocks)
    w_dt = np.tile(w_in[:, dt0:dt0 + HEADS], (1, 4)).reshape(KT, P, P).transpose(1, 0, 2).reshape(P, KT * P)
    x_all = _tiles(np.concatenate([a["x_prompt"].reshape(SEQ, -1), a["x_sample"].reshape(NDEC, -1)]), KT)

    def xbc_order(v, n):
        xs = v[:2048].reshape(GROUPS, 2, P, n)
        bc = [v[s:s + 1024].reshape(GROUPS, 1, P, n) for s in (2048, 3072)]
        return np.concatenate([xs] + bc, axis=1).transpose(2, 0, 1, 3)

    def vec(v):
        return v.reshape(-1, P).T

    par = np.concatenate([
        vec(a["g_mix"][0]), a["conf_dw_w"][0].T.reshape(8, P, CK).transpose(1, 0, 2).reshape(P, -1),
        vec(a["conf_dw_b"][0]), vec(a["conf_ln_g"][0]), vec(a["conf_ln_b"][0]), vec(a["conf_b_pw"][0]),
        xbc_order(a["ssm_conv_w"][0].T, SK).reshape(P, -1),
        xbc_order(a["ssm_conv_b"][0].reshape(-1, 1), 1).reshape(P, -1),
        vec(np.repeat(a["ssm_d"][0], HD)), vec(a["ssm_norm_g"][0]), vec(a["g_ffn"][0]), vec(a["g_final"])], axis=1)
    dt_par = np.stack([np.tile(a["ssm_dt_bias"][0], 4), np.tile(a["ssm_a_log"][0], 4)], axis=1)
    conf_state = a["state_conf_conv"][0].transpose(2, 0, 1).reshape(GROUPS, P, NSEQ * CPRE)
    conv_state = xbc_order(a["state_ssm_conv"][0].transpose(2, 0, 1).reshape(4096, -1), NSEQ * SPRE)\
        .transpose(1, 0, 2, 3).reshape(GROUPS, P, -1)
    ssm_state = a["state_ssm"][0].reshape(NSEQ, GROUPS, 256, NST).transpose(1, 3, 0, 2).reshape(GROUPS, P, -1)

    nc = bacc.Bacc("TRN2", target_bir_lowering=False, num_devices=1)
    arrays, args = {}, []
    for name, v in [("x_all", x_all), ("w_all", w_all), ("w_dt", w_dt), ("par", par), ("dt_par", dt_par),
                    ("conf_state", conf_state), ("conv_state", conv_state), ("ssm_state", ssm_state)]:
        v = np.ascontiguousarray(v, dtype=np.float32)
        arrays[f"in_{name}"] = v
        args.append(nc.dram_tensor(f"in_{name}", v.shape, F32, kind="ExternalInput").ap())
    for name, shape in [("y", (P, KT * T)), ("conf", (GROUPS, P, CPRE * (NSEQ + 1))),
                        ("conv", (GROUPS, P, 4 * SPRE * (NSEQ + 1))), ("hp", (GROUPS, P, 256)),
                        ("hs", (GROUPS, P, NSEQ * 256))]:
        args.append(nc.dram_tensor(f"out_{name}", shape, F32, kind="ExternalOutput").ap())
    hybrid_layer(nc, *args)
    r = run_bass_kernel_spmd(nc, [arrays], core_ids=[0]).results[0]

    y = r["out_y"].reshape(P, KT, T).transpose(2, 1, 0).reshape(T, D_MODEL)
    conf = r["out_conf"].reshape(D_MODEL, NSEQ + 1, CPRE).transpose(1, 2, 0)
    conv = r["out_conv"].reshape(GROUPS, P, 4, NSEQ + 1, SPRE)
    conv = np.concatenate([conv[:, :, 0:2].transpose(0, 2, 1, 3, 4).reshape(2048, NSEQ + 1, SPRE),
                           conv[:, :, 2].reshape(1024, NSEQ + 1, SPRE),
                           conv[:, :, 3].reshape(1024, NSEQ + 1, SPRE)]).transpose(1, 2, 0)
    hp = r["out_hp"].reshape(GROUPS, NST, HPG, HD).transpose(0, 2, 3, 1).reshape(1, 1, HEADS, HD, NST)
    hs = r["out_hs"].reshape(GROUPS, NST, NSEQ, HPG, HD).transpose(2, 0, 3, 4, 1).reshape(1, NSEQ, HEADS, HD, NST)
    return (y[:SEQ].reshape(1, SEQ, D_MODEL), y[SEQ:].reshape(NSEQ, TDEC, D_MODEL),
            conf[None, 0:1], conv[None, 0:1], hp, conf[None, 1:], conv[None, 1:], hs)
```
